# Optimizing a Trainium2 kernel written in Bass

```python
import jax, jax.numpy as jnp
from jax import lax
import numpy as np
import math

D_MODEL = 1024
BATCH = 1
SEQ = 2048
DEPTH = 2

GRID_W = 64
CTX_LEN = 256
D_MIX = 1024
FOUR_GROUPS = 4
FOUR_DIM = 64
D_FOUR = FOUR_GROUPS * FOUR_DIM
NA_HEADS = 6
NA_HEAD_DIM = 64
D_NA = NA_HEADS * NA_HEAD_DIM
NA_KH = 8
NA_KW = 16
GLA_HEADS = 4
GLA_DK = 48
GLA_DV = 96
D_GLA_K = GLA_HEADS * GLA_DK
D_GLA_V = GLA_HEADS * GLA_DV
GLA_RANK = 16
GLA_TAU = 16.0
GLA_CHUNK = 64
ROPE_BASE = 10000.0
EPS = 1e-6

IN_SIZES = (D_FOUR, D_FOUR, D_NA, D_NA, D_NA, D_NA, D_GLA_K, D_GLA_K, D_GLA_V, D_GLA_V, GLA_RANK, GLA_RANK)
D_IN = sum(IN_SIZES)
IN_SPLITS = tuple(int(s) for s in np.cumsum(IN_SIZES)[:-1])


def rmsnorm(x, w):
    xf = x.astype(jnp.float32)
    y = xf * lax.rsqrt(jnp.mean(xf * xf, axis=-1, keepdims=True) + EPS)
    return (y * w.astype(jnp.float32)).astype(x.dtype)

def split_heads(t, h):
    return t.reshape(t.shape[:-1] + (h, t.shape[-1] // h))

def rope_2d(t):
    L = t.shape[1]
    pos = jnp.arange(L)
    row = (pos // GRID_W).astype(jnp.float32)
    col = (pos % GRID_W).astype(jnp.float32)
    half = t.shape[-1] // 2
    n_freq = half // 2
    inv = ROPE_BASE ** (-jnp.arange(n_freq, dtype=jnp.float32) / n_freq)

    def rot(u, p):
        ang = p[:, None] * inv[None, :]
        cos = jnp.cos(ang)[None, :, None, :]
        sin = jnp.sin(ang)[None, :, None, :]
        u1, u2 = u[..., :n_freq], u[..., n_freq:]
        return jnp.concatenate([u1 * cos - u2 * sin, u1 * sin + u2 * cos], axis=-1)

    tf = t.astype(jnp.float32)
    out = jnp.concatenate([rot(tf[..., :half], row), rot(tf[..., half:], col)], axis=-1)
    return out.astype(t.dtype)

def fourier_mix(u, w_four):
    B, L, _ = u.shape
    ug = u.astype(jnp.float32).reshape(B, L, FOUR_GROUPS, FOUR_DIM)
    f = jnp.fft.fft2(ug, axes=(1, 3), norm="ortho").real
    return f.reshape(B, L, D_FOUR).astype(u.dtype) @ w_four

def neighbourhood_attention(q, k, v, kc, vc, rpb):
    B, L, H, d = q.shape
    rows = L // GRID_W
    kh = min(NA_KH, rows)
    r = np.arange(rows)
    row_start = np.clip(r - kh // 2, 0, rows - kh)
    row_idx = row_start[:, None] + np.arange(kh)[None, :]
    cq = np.arange(GRID_W)
    col_start = np.clip(cq - NA_KW // 2, 0, GRID_W - NA_KW)
    col_mask = (cq[None, :] >= col_start[:, None]) & (cq[None, :] < col_start[:, None] + NA_KW)
    row_off = row_idx - r[:, None] + NA_KH - 1
    col_off = np.clip(cq[None, :] - cq[:, None] + NA_KW - 1, 0, 2 * NA_KW - 2)
    bias = rpb[:, row_off[:, None, :, None], col_off[None, :, None, :]].astype(jnp.float32)
    bias = jnp.where(col_mask[None, None, :, None, :], bias, -jnp.inf)

    scale = d ** -0.5
    qg = q.reshape(B, rows, GRID_W, H, d) * scale
    kg = k.reshape(B, rows, GRID_W, H, d)[:, row_idx]
    vg = v.reshape(B, rows, GRID_W, H, d)[:, row_idx]
    s_loc = jnp.einsum('brqhd,brikhd->bhrqik', qg, kg).astype(jnp.float32) + bias[None]
    s_loc = s_loc.reshape(B, H, rows, GRID_W, kh * GRID_W)
    s_ctx = jnp.einsum('brqhd,bchd->bhrqc', qg, kc).astype(jnp.float32)
    p = jax.nn.softmax(jnp.concatenate([s_loc, s_ctx], axis=-1), axis=-1)
    p_loc = p[..., :kh * GRID_W].reshape(B, H, rows, GRID_W, kh, GRID_W).astype(v.dtype)
    p_ctx = p[..., kh * GRID_W:].astype(v.dtype)
    o = jnp.einsum('bhrqik,brikhd->brqhd', p_loc, vg) + jnp.einsum('bhrqc,bchd->brqhd', p_ctx, vc)
    return o.reshape(B, L, H * d)

def context_attention(qc, kc, vc):
    B, Lc, H, d = qc.shape
    s = jnp.einsum('bqhd,bkhd->bhqk', qc, kc).astype(jnp.float32) * (d ** -0.5)
    p = jax.nn.softmax(s, axis=-1).astype(vc.dtype)
    return jnp.einsum('bhqk,bkhd->bqhd', p, vc).reshape(B, Lc, H * d)

def gla_scan(q, k, v, log_a, s0):
    B, L, H, dk = q.shape
    dv = v.shape[-1]
    n = L // GLA_CHUNK

    def chunks(t):
        return t.astype(jnp.float32).reshape(B, n, GLA_CHUNK, H, t.shape[-1]).transpose(1, 0, 3, 2, 4)

    tri = jnp.tril(jnp.ones((GLA_CHUNK, GLA_CHUNK), dtype=bool))

    def step(state, inp):
        qi, ki, vi, gi = inp
        b = jnp.cumsum(gi, axis=2)
        b_end = b[:, :, -1:, :]
        q_dec = qi * jnp.exp(b)
        k_dec = ki * jnp.exp(-b)
        a = jnp.where(tri, jnp.einsum('bhtk,bhsk->bhts', q_dec, k_dec), 0.0)
        o = jnp.einsum('bhts,bhsv->bhtv', a, vi) + jnp.einsum('bhtk,bhkv->bhtv', q_dec, state)
        k_to_end = ki * jnp.exp(b_end - b)
        state = jnp.exp(b_end[:, :, 0, :])[..., None] * state + jnp.einsum('bhsk,bhsv->bhkv', k_to_end, vi)
        return state, o

    state, o = lax.scan(step, s0.astype(jnp.float32), (chunks(q), chunks(k), chunks(v), chunks(log_a)))
    o = o.transpose(1, 0, 3, 2, 4).reshape(B, L, H, dv)
    return o, state

def gla_log_decay(z, w_a, b_a):
    g = (z @ w_a + b_a).astype(jnp.float32)
    return split_heads(jax.nn.log_sigmoid(g) / GLA_TAU, GLA_HEADS)

def gla_out_norm(o, w, dtype):
    o = o * lax.rsqrt(jnp.mean(o * o, axis=-1, keepdims=True) + EPS) * w.astype(jnp.float32)
    return o.reshape(o.shape[0], o.shape[1], D_GLA_V).astype(dtype)

def first_inputs(seed: int = 0) -> dict:
    key = jax.random.key(seed)
    ks = jax.random.split(key, 20)
    f32 = jnp.float32
    nrm = lambda k, shape, s: jax.random.normal(k, shape, f32) * s
    return {
        "x": nrm(ks[0], (BATCH, SEQ, D_MODEL), 1.0),
        "c": nrm(ks[1], (BATCH, D_MODEL), 1.0),
        "ctx": nrm(ks[2], (BATCH, CTX_LEN, D_MODEL), 1.0),
        "c_ctx": nrm(ks[3], (D_MODEL,), 1.0),
        "w_ada": nrm(ks[4], (DEPTH, D_MODEL, 3 * D_MODEL), 0.5 * D_MODEL ** -0.5),
        "b_ada": nrm(ks[5], (DEPTH, 3 * D_MODEL), 0.02),
        "norm_w": 1.0 + nrm(ks[6], (DEPTH, D_MODEL), 0.02),
        "w_in": nrm(ks[7], (DEPTH, D_MODEL, D_IN), D_MODEL ** -0.5),
        "w_four": nrm(ks[8], (DEPTH, D_FOUR, D_FOUR), D_FOUR ** -0.5),
        "rpb": nrm(ks[9], (DEPTH, NA_HEADS, 2 * NA_KH - 1, 2 * NA_KW - 1), 0.1),
        "w_alpha_fwd": nrm(ks[10], (DEPTH, GLA_RANK, D_GLA_K), GLA_RANK ** -0.5),
        "b_alpha_fwd": nrm(ks[11], (DEPTH, D_GLA_K), 0.1),
        "w_alpha_bwd": nrm(ks[12], (DEPTH, GLA_RANK, D_GLA_K), GLA_RANK ** -0.5),
        "b_alpha_bwd": nrm(ks[13], (DEPTH, D_GLA_K), 0.1),
        "gla_norm_w": 1.0 + nrm(ks[14], (DEPTH, GLA_DV), 0.02),
        "w_out": nrm(ks[15], (DEPTH, D_MIX, D_MODEL), D_MIX ** -0.5),
        "norm_f": 1.0 + nrm(ks[16], (D_MODEL,), 0.02),
    }

def first_block(x, c, ctx, c_ctx, w_ada, b_ada, norm_w, w_in, w_four, rpb,
              w_alpha_fwd, b_alpha_fwd, w_alpha_bwd, b_alpha_bwd, gla_norm_w, w_out, norm_f):
    silu_c = jax.nn.silu(c)
    silu_cc = jax.nn.silu(c_ctx)
    for l in range(DEPTH):
        last = l == DEPTH - 1
        shift_x, scale_x, gate_x = jnp.split(silu_c @ w_ada[l] + b_ada[l], 3, axis=-1)
        shift_c, scale_c, gate_c = jnp.split(silu_cc @ w_ada[l] + b_ada[l], 3, axis=-1)
        hx = rmsnorm(x, norm_w[l]) * (1.0 + scale_x[:, None, :]) + shift_x[:, None, :]
        hc = rmsnorm(ctx, norm_w[l]) * (1.0 + scale_c) + shift_c

        (fx, fgx, nqx, nkx, nvx, ngx, gqx, gkx, gvx, ggx, zfx, zbx) = jnp.split(hx @ w_in[l], IN_SPLITS, axis=-1)
        (fc, fgc, nqc, nkc, nvc, ngc, gqc, gkc, gvc, ggc, zfc, zbc) = jnp.split(hc @ w_in[l], IN_SPLITS, axis=-1)

        nkc_h, nvc_h = split_heads(nkc, NA_HEADS), split_heads(nvc, NA_HEADS)
        na_x = neighbourhood_attention(split_heads(nqx, NA_HEADS), split_heads(nkx, NA_HEADS),
                                       split_heads(nvx, NA_HEADS), nkc_h, nvc_h, rpb[l])

        qx_g = rope_2d(split_heads(gqx, GLA_HEADS)) * (GLA_DK ** -0.5)
        kx_g = rope_2d(split_heads(gkx, GLA_HEADS))
        vx_g = split_heads(gvx, GLA_HEADS)
        qc_g = split_heads(gqc, GLA_HEADS) * (GLA_DK ** -0.5)
        kc_g = split_heads(gkc, GLA_HEADS)
        vc_g = split_heads(gvc, GLA_HEADS)
        la_xf = gla_log_decay(zfx, w_alpha_fwd[l], b_alpha_fwd[l])
        la_cf = gla_log_decay(zfc, w_alpha_fwd[l], b_alpha_fwd[l])
        la_xb = gla_log_decay(zbx, w_alpha_bwd[l], b_alpha_bwd[l])
        la_cb = gla_log_decay(zbc, w_alpha_bwd[l], b_alpha_bwd[l])
        s0 = jnp.zeros((x.shape[0], GLA_HEADS, GLA_DK, GLA_DV), jnp.float32)
        flip = lambda t: jnp.flip(t, axis=1)
        oc_f, sc_f = gla_scan(qc_g, kc_g, vc_g, la_cf, s0)
        ox_f, _ = gla_scan(qx_g, kx_g, vx_g, la_xf, sc_f)
        oc_b, sc_b = gla_scan(flip(qc_g), flip(kc_g), flip(vc_g), flip(la_cb), s0)
        ox_b, _ = gla_scan(flip(qx_g), flip(kx_g), flip(vx_g), flip(la_xb), sc_b)
        gla_x = gla_out_norm(ox_f + flip(ox_b), gla_norm_w[l], x.dtype)

        four_x = fourier_mix(fx, w_four[l])

        mix_x = jnp.concatenate([four_x * jax.nn.silu(fgx), na_x * jax.nn.silu(ngx),
                                 gla_x * jax.nn.silu(ggx)], axis=-1)
        x_new = x + gate_x[:, None, :] * (mix_x @ w_out[l])

        if not last:
            na_c = context_attention(split_heads(nqc, NA_HEADS), nkc_h, nvc_h)
            gla_c = gla_out_norm(oc_f + flip(oc_b), gla_norm_w[l], ctx.dtype)
            four_c = fourier_mix(fc, w_four[l])
            mix_c = jnp.concatenate([four_c * jax.nn.silu(fgc), na_c * jax.nn.silu(ngc),
                                     gla_c * jax.nn.silu(ggc)], axis=-1)
            ctx = ctx + gate_c * (mix_c @ w_out[l])
        x = x_new
    return rmsnorm(x, norm_f)


_first_inputs = first_inputs


def first_inputs(seed=0):
    import zlib

    import numpy as np

    out = dict(_first_inputs(seed))
    spreads = {}
    factors = {}
    for name, (base, spread) in spreads.items():
        noise = np.random.default_rng([zlib.crc32(name.encode()), seed]).standard_normal(out[name].shape)
        drawn = base * np.exp(spread * noise) if base else spread * noise
        out[name] = __import__('jax').numpy.asarray(drawn.astype(out[name].dtype))
    for name, factor in factors.items():
        out[name] = (out[name] * factor).astype(out[name].dtype)
    return out


_narrow_inputs = first_inputs


def first_inputs(seed=0):
    out = dict(_narrow_inputs(seed))
    wider = {'ctx': 3.57,
     'b_ada': 3.42,
     'norm_w': 8.56,
     'rpb': 12.0,
     'w_alpha_fwd': 3.53,
     'b_alpha_fwd': 11.95,
     'b_alpha_bwd': 11.41,
     'gla_norm_w': 12.0,
     'norm_f': 3.22}
    for name, times in wider.items():
        mean = out[name].mean()
        out[name] = (mean + times * (out[name] - mean)).astype(out[name].dtype)
    return out


DEPTH_2 = 1

N_HEADS = 8
HEAD_DIM = 64
ATTN_WIDTH = N_HEADS * HEAD_DIM
DILATIONS = ((128, 1), (512, 4), (2048, 16))
BLK = 128
ROPE_THETA = 10000.0
GMLP_GROUPS = 4
GMLP_WIDTH = D_MODEL // 2
GMLP_GROUP_DIM = GMLP_WIDTH // GMLP_GROUPS
CHUNK = 128
IN_COLS = 4 * ATTN_WIDTH + 3 * GMLP_WIDTH
MIX_WIDTH = ATTN_WIDTH + GMLP_WIDTH
PLE_DIM = 256
NEG = -1e30


def _rmsnorm(x, g):
    xf = x.astype(jnp.float32)
    y = xf * lax.rsqrt(jnp.mean(xf * xf, axis=-1, keepdims=True) + EPS)
    return (y * g.astype(jnp.float32)).astype(x.dtype)

def _layernorm(x, g, b):
    xf = x.astype(jnp.float32)
    mu = jnp.mean(xf, axis=-1, keepdims=True)
    xc = xf - mu
    var = jnp.mean(xc * xc, axis=-1, keepdims=True)
    y = xc * lax.rsqrt(var + EPS)
    return (y * g.astype(jnp.float32) + b.astype(jnp.float32)).astype(x.dtype)

def _rope(t, positions):
    half = HEAD_DIM // 2
    inv_freq = jnp.exp(-math.log(ROPE_THETA) * jnp.arange(half, dtype=jnp.float32) / half)
    ang = positions.astype(jnp.float32)[..., None] * inv_freq
    c = jnp.cos(ang)[:, :, None, :]
    s = jnp.sin(ang)[:, :, None, :]
    tf = t.astype(jnp.float32)
    t1, t2 = tf[..., :half], tf[..., half:]
    return jnp.concatenate([t1 * c - t2 * s, t2 * c + t1 * s], axis=-1).astype(t.dtype)

def _dilated_branch(q, k, v, window, dilation):
    B, S, H, D = q.shape
    r = dilation
    L = S // r
    n_back = window // r
    Lp = ((L + BLK - 1) // BLK) * BLK
    nb = Lp // BLK

    def split(t):
        t = t.reshape(B, L, r, H, D).transpose(0, 2, 1, 3, 4).reshape(B * r, L, H, D)
        return jnp.pad(t, ((0, 0), (0, Lp - L), (0, 0), (0, 0)))

    qs = split(q).reshape(B * r, nb, BLK, H, D)
    kb = split(k).reshape(B * r, nb, BLK, H, D)
    vb = split(v).reshape(B * r, nb, BLK, H, D)
    k_prev = jnp.pad(kb, ((0, 0), (1, 0), (0, 0), (0, 0), (0, 0)))[:, :-1]
    v_prev = jnp.pad(vb, ((0, 0), (1, 0), (0, 0), (0, 0), (0, 0)))[:, :-1]
    kk = jnp.concatenate([k_prev, kb], axis=2)
    vv = jnp.concatenate([v_prev, vb], axis=2)

    scores = jnp.einsum('nbqhd,nbkhd->nbhqk', qs, kk).astype(jnp.float32) * (HEAD_DIM ** -0.5)
    dist = (jnp.arange(BLK)[:, None] + BLK) - jnp.arange(2 * BLK)[None, :]
    band = (dist >= 0) & (dist <= n_back)
    key_idx = jnp.arange(nb)[:, None] * BLK - BLK + jnp.arange(2 * BLK)[None, :]
    valid = band[None, :, :] & (key_idx >= 0)[:, None, :]
    scores = jnp.where(valid[None, :, None], scores, NEG)
    m = jnp.max(scores, axis=-1, keepdims=True)
    e = jnp.exp(scores - m)
    den = jnp.sum(e, axis=-1, keepdims=True)
    out = jnp.einsum('nbhqk,nbkhd->nbqhd', (e / den).astype(v.dtype), vv)
    lse = (m + jnp.log(den))[..., 0]
    lse = lse.transpose(0, 1, 3, 2).reshape(B * r, Lp, H)[:, :L]
    out = out.reshape(B * r, Lp, H, D)[:, :L]
    out = out.reshape(B, r, L, H, D).transpose(0, 2, 1, 3, 4).reshape(B, S, H, D)
    lse = lse.reshape(B, r, L, H).transpose(0, 2, 1, 3).reshape(B, S, H)
    return out, lse

def _dilated_attention(q, k, v):
    outs, lses = [], []
    for window, dilation in DILATIONS:
        o, l = _dilated_branch(q, k, v, window, dilation)
        outs.append(o)
        lses.append(l)
    w = jax.nn.softmax(jnp.stack(lses, axis=0), axis=0)
    o = jnp.sum(w[..., None] * jnp.stack(outs, axis=0).astype(jnp.float32), axis=0)
    return o.astype(q.dtype)

def _gmlp_spatial(u, v, w_s, b_s, ln_g, ln_b):
    B, S, _ = u.shape
    u = jax.nn.gelu(u)
    v = _layernorm(jax.nn.gelu(v), ln_g, ln_b)
    vr = v.reshape(B, S // CHUNK, CHUNK, GMLP_GROUPS, GMLP_GROUP_DIM)
    ws = w_s * jnp.tril(jnp.ones((CHUNK, CHUNK), dtype=w_s.dtype))[None]
    sv = jnp.einsum('gts,bcsgd->bctgd', ws, vr) + b_s.T[None, None, :, :, None]
    return u * sv.reshape(B, S, GMLP_WIDTH)

def second_inputs(seed: int = 0) -> dict:
    key = jax.random.key(seed)
    ks = jax.random.split(key, 16)
    f32 = jnp.float32
    nrm = lambda k, shape, scale: jax.random.normal(k, shape, f32) * scale
    x = jax.random.normal(ks[0], (BATCH, SEQ, D_MODEL), f32)
    p = jax.random.normal(ks[1], (DEPTH_2, BATCH, SEQ, PLE_DIM), f32)
    positions = jnp.broadcast_to(jnp.arange(SEQ, dtype=jnp.int32)[None, :], (BATCH, SEQ))
    return {
        "x": x,
        "p": p,
        "positions": positions,
        "g_in": 1.0 + nrm(ks[2], (DEPTH_2, D_MODEL), 0.01),
        "w_in": nrm(ks[3], (DEPTH_2, D_MODEL, IN_COLS), D_MODEL ** -0.5),
        "q_norm": 1.0 + nrm(ks[4], (DEPTH_2, HEAD_DIM), 0.01),
        "k_norm": 1.0 + nrm(ks[5], (DEPTH_2, HEAD_DIM), 0.01),
        "w_spatial": nrm(ks[6], (DEPTH_2, GMLP_GROUPS, CHUNK, CHUNK), 0.5 * CHUNK ** -0.5),
        "b_spatial": 1.0 + nrm(ks[7], (DEPTH_2, GMLP_GROUPS, CHUNK), 0.1),
        "ln_v_g": 1.0 + nrm(ks[8], (DEPTH_2, GMLP_WIDTH), 0.01),
        "ln_v_b": nrm(ks[9], (DEPTH_2, GMLP_WIDTH), 0.01),
        "w_out": nrm(ks[10], (DEPTH_2, MIX_WIDTH, D_MODEL), MIX_WIDTH ** -0.5),
        "g_ple": 1.0 + nrm(ks[11], (DEPTH_2, D_MODEL), 0.01),
        "w_ple_gate": nrm(ks[12], (DEPTH_2, D_MODEL, D_MODEL), D_MODEL ** -0.5),
        "b_ple_gate": nrm(ks[13], (DEPTH_2, D_MODEL), 0.01),
        "w_ple_proj": nrm(ks[14], (DEPTH_2, PLE_DIM, D_MODEL), PLE_DIM ** -0.5),
    }

def second_block(x, p, positions, g_in, w_in, q_norm, k_norm, w_spatial, b_spatial,
              ln_v_g, ln_v_b, w_out, g_ple, w_ple_gate, b_ple_gate, w_ple_proj):
    B, S, _ = x.shape
    h = x
    for i in range(DEPTH_2):
        a = _rmsnorm(h, g_in[i])
        z = jnp.einsum('bsd,de->bse', a, w_in[i])
        q, k, v, gate_b, u_a, v_a, gate_a = jnp.split(
            z, np.cumsum([ATTN_WIDTH] * 4 + [GMLP_WIDTH] * 2).tolist(), axis=-1)
        q = _rope(_rmsnorm(q.reshape(B, S, N_HEADS, HEAD_DIM), q_norm[i]), positions)
        k = _rope(_rmsnorm(k.reshape(B, S, N_HEADS, HEAD_DIM), k_norm[i]), positions)
        v = v.reshape(B, S, N_HEADS, HEAD_DIM)
        o_b = _dilated_attention(q, k, v).reshape(B, S, ATTN_WIDTH) * jax.nn.silu(gate_b)
        o_a = _gmlp_spatial(u_a, v_a, w_spatial[i], b_spatial[i], ln_v_g[i], ln_v_b[i]) * jax.nn.silu(gate_a)
        mixed = jnp.concatenate([o_b, o_a], axis=-1)
        h = h + jnp.einsum('bse,ed->bsd', mixed, w_out[i])
        gate = jax.nn.sigmoid(jnp.einsum('bsd,de->bse', _rmsnorm(h, g_ple[i]), w_ple_gate[i]) + b_ple_gate[i])
        h = h + gate * jnp.einsum('bsp,pd->bsd', p[i], w_ple_proj[i])
    return h


_first_inputs_2 = second_inputs


def second_inputs(seed=0):
    import zlib

    import numpy as np

    out = dict(_first_inputs_2(seed))
    spreads = {}
    factors = {}
    for name, (base, spread) in spreads.items():
        noise = np.random.default_rng([zlib.crc32(name.encode()), seed]).standard_normal(out[name].shape)
        drawn = base * np.exp(spread * noise) if base else spread * noise
        out[name] = __import__('jax').numpy.asarray(drawn.astype(out[name].dtype))
    for name, factor in factors.items():
        out[name] = (out[name] * factor).astype(out[name].dtype)
    return out


_narrow_inputs_2 = second_inputs


def second_inputs(seed=0):

    out = dict(_narrow_inputs_2(seed))
    wider = {'g_in': 12.0,
     'q_norm': 12.0,
     'k_norm': 12.0,
     'ln_v_g': 12.0,
     'ln_v_b': 12.0,
     'g_ple': 12.0,
     'b_ple_gate': 12.0}
    for name, times in wider.items():
        mean = out[name].mean()
        out[name] = (mean + times * (out[name] - mean)).astype(out[name].dtype)
    return out


def setup_inputs(seed=0):
    out = dict(first_inputs(seed))
    for name, value in second_inputs(seed + 1).items():
        if name != "x":
            out[name + "_2"] = value
    return out


def reference(
    x, c, ctx, c_ctx, w_ada, b_ada, norm_w, w_in, w_four, rpb, w_alpha_fwd, b_alpha_fwd,
    w_alpha_bwd, b_alpha_bwd, gla_norm_w, w_out, norm_f, p_2, positions_2, g_in_2, w_in_2,
    q_norm_2, k_norm_2, w_spatial_2, b_spatial_2, ln_v_g_2, ln_v_b_2, w_out_2, g_ple_2,
    w_ple_gate_2, b_ple_gate_2, w_ple_proj_2,
):
    x = first_block(
        x, c, ctx, c_ctx, w_ada, b_ada, norm_w, w_in, w_four, rpb, w_alpha_fwd, b_alpha_fwd,
        w_alpha_bwd, b_alpha_bwd, gla_norm_w, w_out, norm_f,
    )
    return second_block(
        x, p_2, positions_2, g_in_2, w_in_2, q_norm_2, k_norm_2, w_spatial_2, b_spatial_2,
        ln_v_g_2, ln_v_b_2, w_out_2, g_ple_2, w_ple_gate_2, b_ple_gate_2, w_ple_proj_2,
    )


_drawn_inputs = setup_inputs


def setup_inputs(seed=0):
    import zlib

    import numpy as np

    out = dict(_drawn_inputs(seed))
    spreads = {}
    factors = {'ctx': 3.016,
     'q_norm_2': 8.0,
     'k_norm_2': 8.0,
     'ln_v_g_2': 5.587,
     'ln_v_b_2': 6.109,
     'b_spatial_2': 2.918,
     'g_ple_2': 2.861,
     'b_ple_gate_2': 2.991}
    for name, (base, spread) in spreads.items():
        noise = np.random.default_rng([zlib.crc32(name.encode()), seed]).standard_normal(out[name].shape)
        drawn = base * np.exp(spread * noise) if base else spread * noise
        out[name] = __import__('jax').numpy.asarray(drawn.astype(out[name].dtype))
    for name, factor in factors.items():
        out[name] = (out[name] * factor).astype(out[name].dtype)
    return out
```

```python
import math
import numpy as np
import concourse.bass as bass
from concourse import mybir
from contextlib import contextmanager

F32 = mybir.dt.float32
F32R = mybir.dt.float32r
I32 = mybir.dt.int32
ALU = mybir.AluOpType
ACT = mybir.ActivationFunctionType
AX = mybir.AxisListType

D = 1024
KC = D // 128
LX, LC = 2048, 256
LT = LX + LC
NT = LT // 128
NX = LX // 128
DEPTH = 2
EPS = 1e-6
D_FOUR, D_NA, D_GK, D_GV = 256, 384, 192, 384
NA_H, NA_D = 6, 64
GRID = 64
ROWS = LX // GRID
KH, KW = 8, 16
GH, GDK, GDV, RANK, CH = 4, 48, 96, 16, 64
NCH = LT // CH
CM = 12
TM = 1024 + D_NA + D_GV
HB, HD = 8, 64
WB = 3584
N1, N2 = 128, 16
ORW = 512 + 2 * HB
NEGBIG = -1e30
LOWEST = -3e38


class Phase:

    def __init__(self, nc, name):
        self.nc, self.name = nc, name

    def sb(self, name, shape, dt=F32):
        return self.nc.alloc_sbuf_tensor(f"{self.name}_{name}", list(shape), dt)

    def ps(self, name, shape=(128, 512)):
        return self.nc.alloc_psum_tensor(f"{self.name}_{name}", list(shape), F32)

    def sem(self, name):
        return self.nc.alloc_semaphore(f"{self.name}_{name}")


class Split:

    def __init__(self, alloc, name, shape):
        self.hi, self.lo = alloc(f"{name}_hi", shape, F32R), alloc(f"{name}_lo", shape, F32R)

    def __getitem__(self, key):
        return self.hi[key], self.lo[key]


def matmul3(nc, out, lhsT, rhs, start, stop):
    (ah, al), (bh, bl) = lhsT, rhs
    nc.tensor.matmul(out, ah, bh, start=start, stop=False)
    nc.tensor.matmul(out, ah, bl, start=False, stop=False)
    return nc.tensor.matmul(out, al, bh, start=False, stop=stop)


@contextmanager
def phase(nc, name):
    with nc.cleanup_on_exit():
        yield Phase(nc, name)


def bcast_rows(row_ap, n, parts=128):
    return row_ap.rearrange("(a n) -> a n", a=1).to_broadcast([parts, n])


def ada_phase(nc, l, io, keep):
    with phase(nc, "ada") as P:
        cs = P.sb("cs", [128, KC, 2])
        wk = [P.sb(f"w{k}", [128, 3 * D]) for k in range(KC)]
        brow = P.sb("brow", [2, 3 * D])
        arow = P.sb("arow", [2, 3 * D])
        nw = P.sb("nw", [128, KC])
        acc = [P.ps(f"acc{n}") for n in range(6)]
        tp = P.ps("tp")
        w_in = [P.sem(f"w_in{k}") for k in range(KC)]
        c_in, b_in, c_ok, rows_ok, cols_ok, mm_ok, gate_out = [P.sem(s) for s in (
            "c_in", "b_in", "c_ok", "rows_ok", "cols_ok", "mm_ok", "gate_out")]
        wv = io["w_ada"].rearrange("l (k p) n -> l k p n", p=128)
        with nc.Block() as block:
            @block.sync
            def _(sp):
                sp.dma_start(cs[:, :, :], io["cT"]).then_inc(c_in, 16)
                for k in range(KC):
                    sp.dma_start(wk[k][:, :], wv[bass.ds(l, 1), k, :, :].rearrange("a p n -> p (a n)")).then_inc(w_in[k], 16)
                for r in range(2):
                    sp.dma_start(brow[r:r + 1, :], io["b_ada"][bass.ds(l, 1), :]).then_inc(b_in, 16)
                sp.dma_start(nw[:, :], io["norm_wT"][bass.ds(l, 1), :, :].rearrange("a p k -> p (a k)")).then_inc(b_in, 16)
                sp.wait_ge(rows_ok, 1)
                sp.dma_start(io["gates"], arow[:, 2 * D:3 * D]).then_inc(gate_out, 16)
                sp.wait_ge(gate_out, 16)

            @block.scalar
            def _(act):
                act.wait_ge(c_in, 16)
                act.activation(cs[:, :, :], cs[:, :, :], ACT.Silu).then_inc(c_ok, 1)

            @block.tensor
            def _(pe):
                pe.wait_ge(c_ok, 1)
                for k in range(KC):
                    pe.wait_ge(w_in[k], 16)
                    for n in range(6):
                        last = nc.tensor.matmul(acc[n][0:2, :], cs[:, k, :], wk[k][:, n * 512:(n + 1) * 512],
                                                start=(k == 0), stop=(k == KC - 1))
                last.then_inc(mm_ok, 1)
                pe.wait_ge(rows_ok, 1)
                for j in range(2 * KC):
                    last = nc.tensor.transpose(tp[:, 2 * j:2 * j + 2], arow[:, j * 128:(j + 1) * 128],
                                               keep["ident"][0:2, 0:2])
                last.then_inc(cols_ok, 1)

            @block.vector
            def _(dve):
                dve.wait_ge(mm_ok, 1)
                dve.wait_ge(b_in, 48)
                for n in range(6):
                    nc.vector.tensor_tensor(arow[:, n * 512:(n + 1) * 512], acc[n][0:2, :],
                                            brow[:, n * 512:(n + 1) * 512], ALU.add)
                dve.drain()
                nc.vector.tensor_scalar(arow[:, D:2 * D], arow[:, D:2 * D], 1.0, None, ALU.add).then_inc(rows_ok, 1)
                dve.wait_ge(cols_ok, 1)
                nc.vector.tensor_copy(keep["shift"][:, :, :], tp[:, 0:16].rearrange("p (k s) -> p k s", s=2))
                for s in range(2):
                    nc.vector.tensor_tensor(keep["scale"][:, :, s], tp[:, 16 + s:32:2], nw[:, :], ALU.mult)


def norm_transpose(P, nc, src, hT, ident, eps, groups, scale_of, shift_of, pre=None, copied=None):
    G = len(groups)
    xb = [P.sb(f"xb{j}", [128, 4, D]) for j in range(2)]
    sq = P.sb("sq", [128, D])
    ss = P.sb("ss", [128, 2, 8])
    if pre:
        wrow = P.sb("wrow", [128, D])
    tm = [P.sb(f"tm{b}", [128, 512]) for b in range(4)]
    tp = [P.ps(f"ntp{b}") for b in range(4)]
    x_in = [P.sem(f"x_in{j}") for j in range(2)]
    hi_ok = [P.sem("hi_dve"), P.sem("hi_act")]
    lo_ok = P.sem("lo_ok")
    x_free, ss_ok, xn_ok, tp_ok, ev_dve, ev_act, pre_ok, pre_out, w_in = [P.sem(s) for s in (
        "x_free", "ss_ok", "xn_ok", "tp_ok", "ev_dve", "ev_act", "pre_ok", "pre_out", "wrow_in")]
    stats = 2 if pre else 1
    rows = src.rearrange("(t p) d -> p t d", p=128)
    with nc.Block() as block:
        @block.sync
        def _(sp):
            if copied:
                sp.wait_ge(copied, 32)
            if pre:
                sp.dma_start(wrow[:, :], bcast_rows(pre[0], D)).then_inc(w_in, 16)
            for g, n in enumerate(groups):
                if g >= 2:
                    sp.wait_ge(x_free, g - 1)
                    if pre:
                        sp.wait_ge(pre_out, 16 * (g - 1))
                sp.dma_start(xb[g % 2][:, 0:n, :], rows[:, 4 * g:4 * g + n, :]).then_inc(x_in[g % 2], 16)

        @block.gpsimd
        def _(pool):
            for g in range(G + 1):
                if pre and g < G:
                    n = groups[g]
                    pool.wait_ge(pre_ok, g + 1)
                    pool.dma_start(rows[:, 4 * g:4 * g + n, :], xb[g % 2][:, 0:n, :]).then_inc(pre_out, 16)
                    pool.wait_ge(pre_out, 16 * (g + 1))
                if g >= 1:
                    n = groups[g - 1]
                    for k in range(KC):
                        c = slice(512 * (g - 1), 512 * (g - 1) + 128 * n)
                        pool.wait_ge(hi_ok[k % 2], (KC * (g - 1) + k) // 2 + 1)
                        nc.gpsimd.tensor_tensor(hT.lo[:, k, c], tm[k % 4][:, 0:128 * n], hT.hi[:, k, c].bitcast(F32),
                                                ALU.subtract).then_inc(lo_ok, 1)

        def act_evac(act, g):
            n = groups[g]
            for k in range(1, KC, 2):
                act.wait_ge(tp_ok, KC * g + k + 1)
                if KC * g + k >= 4:
                    act.wait_ge(lo_ok, KC * g + k - 3)
                act.activation(tm[k % 4][:, 0:128 * n], tp[k % 4][:, 0:128 * n], ACT.Identity,
                               scale=scale_of(k, g), bias=shift_of(k, g))
                act.drain().then_inc(ev_act, 1)
                act.activation(hT.hi[:, k, 512 * g:512 * g + 128 * n], tm[k % 4][:, 0:128 * n], ACT.Copy).then_inc(hi_ok[1], 1)

        @block.scalar
        def _(act):
            for g, n in enumerate(groups):
                for s in range(stats):
                    if s == 0:
                        act.wait_ge(x_in[g % 2], 16 * (g // 2 + 1))
                    else:
                        act.wait_ge(pre_ok, g + 1)
                    for t in range(n):
                        act.activation(sq[:, :], xb[g % 2][:, t, :], ACT.Square, accum_out=ss[:, g % 2, t:t + 1])
                        act.drain()
                    act.activation(ss[:, g % 2, 4:4 + n], ss[:, g % 2, 0:n], ACT.Sqrt,
                                   scale=1.0 / D, bias=eps[:, 0:1]).then_inc(ss_ok, 1)
                if g >= 1:
                    act_evac(act, g - 1)
            act_evac(act, G - 1)

        @block.vector
        def _(dve):
            def norm(g, s):
                n = groups[g]
                dve.wait_ge(ss_ok, stats * g + s + 1)
                nc.vector.reciprocal(ss[:, g % 2, 4:4 + n], ss[:, g % 2, 4:4 + n])
                dve.drain()
                for t in range(n):
                    if s < stats - 1:
                        if g == 0 and t == 0:
                            dve.wait_ge(w_in, 16)
                        last = nc.vector.scalar_tensor_tensor(xb[g % 2][:, t, :], xb[g % 2][:, t, :],
                                                              ss[:, g % 2, 4 + t:5 + t], wrow[:, :], ALU.mult, ALU.mult)
                    else:
                        if pre and t == 0:
                            dve.wait_ge(pre_out, 16 * (g + 1))
                        last = nc.vector.tensor_scalar(xb[g % 2][:, t, :], xb[g % 2][:, t, :],
                                                       ss[:, g % 2, 4 + t:5 + t], None, ALU.mult)
                last.then_inc(xn_ok if s == stats - 1 else pre_ok, 1)

            def evac(g):
                n = groups[g]
                for k in range(0, KC, 2):
                    dve.wait_ge(tp_ok, KC * g + k + 1)
                    if KC * g + k >= 4:
                        dve.wait_ge(lo_ok, KC * g + k - 3)
                    nc.vector.tensor_scalar(tm[k % 4][:, 0:128 * n], tp[k % 4][:, 0:128 * n],
                                            scale_of(k, g), shift_of(k, g), ALU.mult, ALU.add)
                    dve.drain().then_inc(ev_dve, 1)
                    nc.vector.tensor_copy(hT.hi[:, k, 512 * g:512 * g + 128 * n], tm[k % 4][:, 0:128 * n]).then_inc(hi_ok[0], 1)

            for g in range(G):
                for s in range(stats):
                    norm(g, s)
                if g >= 1:
                    evac(g - 1)
            evac(G - 1)

        @block.tensor
        def _(pe):
            for g, n in enumerate(groups):
                pe.wait_ge(xn_ok, g + 1)
                for k in range(KC):
                    e = (KC * g + k) // 2
                    if e >= 2:
                        pe.wait_ge(ev_act if k % 2 else ev_dve, e - 1)
                    for t in range(n):
                        last = nc.tensor.transpose(tp[k % 4][:, t * 128:(t + 1) * 128],
                                                   xb[g % 2][:, t, k * 128:(k + 1) * 128], ident[:, :])
                    last.then_inc(tp_ok, 1)
                nc.tensor.drain().then_inc(x_free, 1)


def project_cm(P, nc, hT, w, dst, n_chunks):
    TT = [(i * 512, min(512, LT - i * 512)) for i in range((LT + 511) // 512)]
    raw = [P.sb(f"raw{j}", [128, KC, 128]) for j in range(2)]
    wb = [Split(P.sb, f"wb{j}", [128, KC, 128]) for j in range(2)]
    zo = [P.sb(f"zo{j}", [128, LT]) for j in range(2)]
    acc = [P.ps(f"acc{b}") for b in range(len(TT))]
    w_in = [P.sem(f"w_in{j}") for j in range(2)]
    z_out = [P.sem(f"z_out{j}") for j in range(2)]
    mm_ok, ev_dve, ev_act, w_ok = [P.sem(s) for s in ("mm_ok", "ev_dve", "ev_act", "w_ok")]
    nD, nA = (len(TT) + 1) // 2, len(TT) // 2
    pairs = (n_chunks - 1) // 2

    def both(eng, body):
        with eng.Fori(0, pairs) as i:
            for j in range(2):
                body(i, j)
        for j in range(n_chunks - 2 * pairs):
            body(pairs, j)

    with nc.Block() as block:
        @block.sync
        def _(sp):
            for j in range(2):
                sp.sem_inc(z_out[j], 1)

            def load(c, j):
                src = w(c)
                sp.wait_ge(w_ok, c)
                sp.dma_start(raw[j][:, :, :], src).then_inc(w_in[j], 16)

            def body(i, j):
                c = 2 * i + j
                if not isinstance(c, int) or c + 1 < n_chunks:
                    load(c + 1, 1 - j)
                out = dst(c)
                sp.wait_ge(ev_dve, nD * (c + 1) + nD)
                sp.wait_ge(ev_act, nA * (c + 1) + nA)
                sp.dma_start(out, zo[j][:, :]).then_inc(z_out[j], 16)

            sp.dma_start(raw[0][:, :, :], w(0)).then_inc(w_in[0], 16)
            both(sp, body)
            for j in range(2):
                sp.wait_ge(z_out[j], 16 * ((n_chunks + 1 - j) // 2) + 1)

        @block.tensor
        def _(pe):
            pe.drain().then_inc(mm_ok, 2 * len(TT))
            def body(i, j):
                c = 2 * i + j
                pe.wait_ge(w_ok, c + 2)
                for n, (t0, tn) in enumerate(TT):
                    own, e = (ev_act, nA * c + n // 2) if n % 2 else (ev_dve, nD * c + n // 2)
                    pe.wait_ge(own, e + 1)
                    for k in range(KC):
                        last = matmul3(nc, acc[n][:, 0:tn], wb[j][:, k, :], hT[:, k, t0:t0 + tn], k == 0, k == KC - 1)
                    last.then_inc(mm_ok, 1)
            both(pe, body)

        @block.vector
        def _(dve):
            dve.drain().then_inc(ev_dve, nD)
            dve.drain().then_inc(w_ok, 1)

            def split(c, i, j):
                dve.wait_ge(w_in[j], 16 * i + 16)
                dve.wait_ge(mm_ok, len(TT) * (c + 1))
                nc.vector.tensor_copy(wb[j].hi[:, :, :], raw[j][:, :, :])
                dve.drain()
                nc.vector.tensor_tensor(wb[j].lo[:, :, :], raw[j][:, :, :], wb[j].hi[:, :, :].bitcast(F32), ALU.subtract).then_inc(w_ok, 1)

            split(0, 0, 0)

            def body(i, j):
                c = 2 * i + j
                if not isinstance(c, int) or c + 1 < n_chunks:
                    split(c + 1, i + j, 1 - j)
                dve.wait_ge(z_out[j], 16 * i + 1)
                for n, (t0, tn) in enumerate(TT):
                    if n % 2 == 0:
                        dve.wait_ge(mm_ok, len(TT) * (c + 2) + n + 1)
                        nc.vector.tensor_copy(zo[j][:, t0:t0 + tn], acc[n][:, 0:tn]).then_inc(ev_dve, 1)
            both(dve, body)

        @block.scalar
        def _(act):
            act.drain().then_inc(ev_act, nA)
            def body(i, j):
                c = 2 * i + j
                act.wait_ge(z_out[j], 16 * i + 1)
                for n, (t0, tn) in enumerate(TT):
                    if n % 2:
                        act.wait_ge(mm_ok, len(TT) * (c + 2) + n + 1)
                        act.activation(zo[j][:, t0:t0 + tn], acc[n][:, 0:tn], ACT.Copy).then_inc(ev_act, 1)
            both(act, body)


def project_tm(P, nc, hT, w, dst, width, funcs, tiles):
    n_chunks = len(funcs)
    raw = P.sb("traw", [128, KC, width])
    wb = Split(P.sb, "tw", [128, KC, width])
    zo = [P.sb(f"tz{j}", [128, width]) for j in range(3)]
    acc = [P.ps(f"tacc{b}") for b in range(3)]
    w_in, k_used = P.sem("tw_in"), P.sem("k_used")
    hi_ok, lo_dve, lo_pool = P.sem("hi_ok"), P.sem("lo_dve"), P.sem("lo_pool")
    z_out = [P.sem(f"tz_out{j}") for j in range(3)]
    mm_ok, ev = [P.sem(s) for s in ("tmm_ok", "tev")]
    with nc.Block() as block:
        @block.sync
        def _(sp):
            def load(c):
                if c >= 1:
                    sp.wait_ge(lo_dve, KC // 2 * c)
                    sp.wait_ge(lo_pool, KC // 2 * c)
                sp.dma_start(raw[:, :, :], w(c)).then_inc(w_in, 16)
            load(0)
            for c in range(n_chunks):
                if c + 1 < n_chunks:
                    load(c + 1)
                for t in range(tiles):
                    n = c * tiles + t
                    sp.wait_ge(ev, n + 1)
                    sp.dma_start(dst(c, t), zo[n % 3][:, :]).then_inc(z_out[n % 3], 16)
            total = n_chunks * tiles
            for j in range(3):
                sp.wait_ge(z_out[j], 16 * ((total + 2 - j) // 3))

        @block.tensor
        def _(pe):
            for c in range(n_chunks):
                for t in range(tiles):
                    n = c * tiles + t
                    if n >= 3:
                        pe.wait_ge(ev, n - 2)
                    for k in range(KC):
                        if t == 0:
                            pe.wait_ge(lo_pool if k % 2 else lo_dve, KC // 2 * c + k // 2 + 1)
                        last = matmul3(nc, acc[n % 3][:, 0:width], hT[:, k, t * 128:(t + 1) * 128], wb[:, k, :], k == 0, k == KC - 1)
                        if t == tiles - 1:
                            last.then_inc(k_used, 1)
                    pe.drain().then_inc(mm_ok, 1) if t == tiles - 1 else last.then_inc(mm_ok, 1)

        @block.vector
        def _(dve):
            for c in range(n_chunks):
                dve.wait_ge(w_in, 16 * (c + 1))
                for k in range(KC):
                    if c >= 1:
                        dve.wait_ge(k_used, KC * (c - 1) + k + 1)
                    nc.vector.tensor_copy(wb.hi[:, k, :], raw[:, k, :])
                    dve.drain().then_inc(hi_ok, 1)
                    if k % 2 == 0:
                        nc.vector.tensor_tensor(wb.lo[:, k, :], raw[:, k, :], wb.hi[:, k, :].bitcast(F32), ALU.subtract).then_inc(lo_dve, 1)

        @block.gpsimd
        def _(pool):
            for c in range(n_chunks):
                for k in range(1, KC, 2):
                    pool.wait_ge(hi_ok, KC * c + k + 1)
                    nc.gpsimd.tensor_tensor(wb.lo[:, k, :], raw[:, k, :], wb.hi[:, k, :].bitcast(F32), ALU.subtract).then_inc(lo_pool, 1)

        @block.scalar
        def _(act):
            for c in range(n_chunks):
                for t in range(tiles):
                    n = c * tiles + t
                    act.wait_ge(mm_ok, n + 1)
                    if n >= 3:
                        act.wait_ge(z_out[n % 3], 16 * (n // 3))
                    act.activation(zo[n % 3][:, :], acc[n % 3][:, 0:width], funcs[c]).then_inc(ev, 1)

class Neighbourhood:

    def __init__(self, P):
        self.q = P.sb("q", [128, 3, LT])
        self.kk = P.sb("k", [128, 3, LT])
        self.t2 = P.sb("t2", [128, NA_H, 15, GRID])
        self.ti = P.sb("ti", [128, NA_H, 9, GRID])
        self.cmask = P.sb("cmask", [128, GRID])
        self.pad = P.sb("pad", [90, 128])
        self.q_in, self.k_in, self.pad_ok, self.pad_in, self.pad_out, self.t_in, self.z_ok = [P.sem(s) for s in (
            "q_in", "k_in", "pad_ok", "pad_in", "pad_out", "t_in", "tz_ok")]

    def load(self, eng, l, io):
        eng.dma_start(self.cmask[:, :], io["col_mask"]).then_inc(self.pad_in, 16)
        eng.wait_ge(self.pad_ok, 1)
        eng.dma_start(self.pad[:, 48:79], io["rpb"][bass.ds(l, 1), :, :, :].rearrange("a h r c -> (a h r) c")).then_inc(self.pad_in, 16)
        eng.wait_ge(self.pad_in, 32)
        eng.dma_start(io["rpb_pad"], self.pad[:, None, :].to_broadcast([90, 64, 128])).then_inc(self.pad_out, 16)
        eng.wait_ge(self.pad_out, 16)
        for s in range(2):
            for h in range(NA_H):
                base = io["rpb_pad"][h * 15:h * 15 + 15 - s, 0, 0:GRID]
                diag = bass.AP(base.tensor, base.offset + 63, [[127, 64], [64 * 128, 15 - s], [1, GRID]])
                eng.dma_start(self.t2[64 * s:64 * s + 64, h, s:15, :], diag).then_inc(self.t_in, 16)
        eng.dma_start(self.q[:, :, :], io["zcm"][2:5, :, :].rearrange("c p t -> p c t")).then_inc(self.q_in, 16)
        eng.dma_start(self.kk[:, :, :], io["zcm"][5:8, :, :].rearrange("c p t -> p c t")).then_inc(self.k_in, 16)

    def clear(self, nc, pool):
        nc.gpsimd.memset(self.pad[:, :], 0.0).then_inc(self.pad_ok, 1)
        pool.wait_ge(self.pad_ok, 1)
        nc.gpsimd.memset(self.t2[64:128, :, 0, :], 0.0).then_inc(self.z_ok, 1)

    def scale(self, nc, pool):
        pool.wait_ge(self.z_ok, 1)
        pool.wait_ge(self.q_in, 16)
        for c in range(3):
            nc.gpsimd.tensor_scalar(self.q[:, c, :], self.q[:, c, :], NA_D ** -0.5, None, ALU.mult)

    def bias(self, nc, dve):
        t2, ti = self.t2, self.ti
        dve.wait_ge(self.t_in, 16 * 12)
        dve.wait_ge(self.z_ok, 1)
        dve.wait_ge(self.pad_in, 32)
        nc.vector.tensor_tensor(t2[:, :, :, :].rearrange("p h r c -> p (h r) c"), t2[:, :, :, :].rearrange("p h r c -> p (h r) c"),
                                self.cmask[:, None, :].to_broadcast([128, NA_H * 15, GRID]), ALU.add)
        dve.drain()
        nc.vector.tensor_copy(ti[:, :, :, :], t2[:, :, 3:12, :])
        dve.drain()
        nc.vector.memset(ti[0:64, :, 8, :], NEGBIG)
        nc.vector.memset(ti[64:128, :, 0, :], NEGBIG)


def fourier_phase(nc, l, io, keep, na):
    with phase(nc, "four") as P:
        dch = P.sb("dch", [128, 2, 2, 256])
        wf = P.sb("wf", [128, 2, 256])
        w2 = P.sb("w2", [128, 2, 512])
        fx = P.sb("fx", [128, 2, LT])
        d1 = P.sb("d1", [128, N2, 3, 128])
        d2 = P.sb("d2", [128, 2, 128])
        dc = P.sb("dc", [128, 2, 2, 256])
        ab = P.sb("ab", [128, N2 + 2, 512])
        yo = [P.sb(f"yo{j}", [128, 512]) for j in range(4)]
        fo = [P.sb(f"fo{j}", [128, 256]) for j in range(3)]
        acc = [P.ps(f"acc{b}") for b in range(6)]
        fx_in, w_in, d1_in, d2_in, w2_mm, w2_ok, ab_mm, ab_dve, ab_act, y_mm, y_ev, o_mm, o_ev = [P.sem(s) for s in (
            "fx_in", "w_in", "d1_in", "d2_in", "w2_mm", "w2_ok", "ab_mm", "ab_dve", "ab_act", "y_mm", "y_ev",
            "o_mm", "o_ev")]
        y_out = [P.sem(f"y_out{j}") for j in range(4)]
        yi_in = [P.sem(f"yi_in{j}") for j in range(4)]
        o_out = [P.sem(f"o_out{j}") for j in range(3)]
        NAB = N2 + 2
        yrows = io["four_y"].rearrange("(p t) c -> p t c", t=N2)
        NO = 16 + 2
        with nc.Block() as block:
            @block.sync
            def _(sp):
                sp.dma_start(dch[:, :, :, :], io["dft_ch"]).then_inc(w_in, 16)
                sp.dma_start(wf[:, :, :], io["w_four"][bass.ds(l, 1), :, :, :].rearrange("a p k n -> p (a k) n")).then_inc(w_in, 16)
                sp.dma_start(fx[:, :, :], io["zcm"][0:2, :, :].rearrange("c p t -> p c t")).then_inc(fx_in, 16)
                sp.dma_start(d1[:, :, :, :], io["dft_1"]).then_inc(d1_in, 16)
                sp.dma_start(d2[:, :, :], io["dft_2"]).then_inc(d2_in, 16)
                sp.dma_start(dc[:, :, :, :], io["dft_ctx"]).then_inc(d2_in, 16)
                na.load(sp, l, io)
                for t in range(N2):
                    sp.wait_ge(y_ev, t + 1)
                    sp.dma_start(yrows[:, t, :], yo[t % 4][:, :]).then_inc(y_out[t % 4], 16)
                for j in range(4):
                    sp.wait_ge(y_out[j], 16 * (N2 // 4))
                sp.wait_ge(y_mm, N2)
                for j in range(4):
                    sp.dma_start(ab[:, 4 * j:4 * j + 4, :],
                                 io["four_y"][j * 512:(j + 1) * 512, :].rearrange("(a p) c -> p a c", p=128)).then_inc(yi_in[j], 16)

            @block.gpsimd
            def _(pool):
                na.clear(nc, pool)
                na.scale(nc, pool)
                for n in range(NO):
                    pool.wait_ge(o_ev, n + 1)
                    if n < 16:
                        dst = io["mix"][0:LX, 0:256].rearrange("(a b c) d -> b a c d", a=16, b=16)[n, :, :, :]
                        pool.dma_start(dst, fo[n % 3][:, :]).then_inc(o_out[n % 3], 16)
                    else:
                        pool.dma_start(io["mix"][LX + (n - 16) * 128:LX + (n - 15) * 128, 0:256],
                                       fo[n % 3][:, :]).then_inc(o_out[n % 3], 16)
                for j in range(3):
                    pool.wait_ge(o_out[j], 16 * (NO // 3))

            @block.tensor
            def _(pe):
                pe.wait_ge(w_in, 32)
                for m in range(2):
                    for cs in range(2):
                        for k in range(2):
                            last = nc.tensor.matmul(acc[m][:, cs * 256:(cs + 1) * 256], dch[:, cs, k, m * 128:(m + 1) * 128],
                                                    wf[:, k, :], start=(k == 0), stop=(k == 1))
                last.then_inc(w2_mm, 1)
                pe.wait_ge(w2_ok, 1)
                pe.wait_ge(fx_in, 16)
                for t in range(NAB):
                    if t >= 2:
                        pe.wait_ge(ab_act if t % 2 else ab_dve, t // 2)
                    for k in range(2):
                        lhs = fx[:, k, t:LX:N2] if t < N2 else fx[:, k, LX + (t - N2) * 128:LX + (t - N2 + 1) * 128]
                        last = nc.tensor.matmul(acc[2 + t % 2][:, :], lhs, w2[:, k, :], start=(k == 0), stop=(k == 1))
                    last.then_inc(ab_mm, 1)
                pe.wait_ge(d1_in, 16)
                pe.wait_ge(ab_dve, NAB // 2)
                pe.wait_ge(ab_act, NAB // 2)
                for t in range(N2):
                    if t >= 2:
                        pe.wait_ge(y_ev, t - 1)
                    b = acc[4 + t % 2]
                    nc.tensor.matmul(b[:, 0:256], d1[:, t, 0, :], ab[:, t, 0:256], start=True, stop=False)
                    nc.tensor.matmul(b[:, 0:256], d1[:, t, 2, :], ab[:, t, 256:512], start=False, stop=True)
                    nc.tensor.matmul(b[:, 256:512], d1[:, t, 1, :], ab[:, t, 0:256], start=True, stop=False)
                    nc.tensor.matmul(b[:, 256:512], d1[:, t, 0, :], ab[:, t, 256:512], start=False, stop=True).then_inc(y_mm, 1)
                pe.wait_ge(d2_in, 32)
                for n in range(NO):
                    if n >= 2:
                        pe.wait_ge(o_ev, n - 1)
                    b = acc[n % 2]
                    if n < 16:
                        pe.wait_ge(yi_in[n // 4], 16)
                        nc.tensor.matmul(b[:, 0:256], d2[:, 0, :], ab[:, n, 0:256], start=True, stop=False)
                        last = nc.tensor.matmul(b[:, 0:256], d2[:, 1, :], ab[:, n, 256:512], start=False, stop=True)
                    else:
                        for k in range(2):
                            for cs in range(2):
                                last = nc.tensor.matmul(b[:, 0:256], dc[:, cs, k, (n - 16) * 128:(n - 15) * 128],
                                                        ab[:, N2 + k, cs * 256:(cs + 1) * 256],
                                                        start=(k + cs == 0), stop=(k + cs == 2))
                    last.then_inc(o_mm, 1)

            @block.vector
            def _(dve):
                dve.wait_ge(w2_mm, 1)
                nc.vector.tensor_copy(w2[:, 0, :], acc[0][:, :])
                nc.vector.tensor_copy(w2[:, 1, :], acc[1][:, :]).then_inc(w2_ok, 1)
                for t in range(0, NAB, 2):
                    dve.wait_ge(ab_mm, t + 1)
                    nc.vector.tensor_copy(ab[:, t, :], acc[2][:, :]).then_inc(ab_dve, 1)
                na.bias(nc, dve)
                for n in range(NO):
                    dve.wait_ge(o_mm, n + 1)
                    if n >= 3:
                        dve.wait_ge(o_out[n % 3], 16 * (n // 3))
                    nc.vector.tensor_copy(fo[n % 3][:, :], acc[n % 2][:, 0:256]).then_inc(o_ev, 1)

            @block.scalar
            def _(act):
                for t in range(1, NAB, 2):
                    act.wait_ge(ab_mm, t + 1)
                    act.activation(ab[:, t, :], acc[3][:, :], ACT.Copy).then_inc(ab_act, 1)
                for t in range(N2):
                    act.wait_ge(y_mm, t + 1)
                    if t >= 4:
                        act.wait_ge(y_out[t % 4], 16 * (t // 4))
                    act.activation(yo[t % 4][:, :], acc[4 + t % 2][:, :], ACT.Copy).then_inc(y_ev, 1)


def neighbourhood_phase(nc, l, io, keep, na):
    with phase(nc, "na") as P:
        q, kk, t2, ti = na.q, na.kk, na.t2, na.ti
        v = P.sb("v", [128, NT, 3, 192])
        s_sb = [P.sb(f"s{j}", [128, 832]) for j in range(2)]
        pt = [P.sb(f"pt{j}", [128, 7, 128]) for j in range(2)]
        st = P.sb("st", [128, 2, NA_H, 4])
        rd = P.sb("rd", [128, 2, NA_H])
        o = [P.sb(f"o{j}", [128, D_NA]) for j in range(2)]
        sp_ps = [P.ps(f"sp{j}", (128, 1024)) for j in range(2)]
        tpa, tpb = P.ps("tpa"), P.ps("tpb")
        ops = [P.ps(f"ops{j}") for j in range(2)]
        (v_in, s_mm, s_used, m_ok, e_ok, ta_mm, tb_mm, ta_ev,
         tb_ev, pv_mm, o_ev, z_ok) = [P.sem(s) for s in (
            "v_in", "s_mm", "s_used", "m_ok", "e_ok",
            "ta_mm", "tb_mm", "ta_ev", "tb_ev", "pv_mm", "o_ev", "z_ok")]
        o_out = [P.sem(f"o_out{j}") for j in range(2)]

        tiles = []
        for i in range(ROWS // 2):
            w0 = min(max(2 * i - 4, 0), ROWS - KH)
            inner = 2 <= i < ROWS // 2 - 2
            tiles.append((128 * i, w0, 9 if inner else 8, w0 - 2 * i + 7, inner))
        for i in range(LC // 128):
            tiles.append((LX + 128 * i, 0, 0, 0, False))
        units = [(i, h) for i in range(len(tiles)) for h in range(NA_H)]
        NU = len(units)

        def key_tiles(i):
            _, w0, nr, _, _ = tiles[i]
            wl = nr * GRID
            out = [(0, j, 128, j * 128, w0 // 2 + j) for j in range(wl // 128)]
            out += [(1, j, 128, wl + j * 128, NX + j) for j in range(2)]
            if wl % 128:
                out.append((1, 2, 64, wl - 64, w0 // 2 + wl // 128))
            return out

        with nc.Block() as block:
            @block.sync
            def _(sp):
                for h in range(NA_H):
                    sp.dma_start(v[:, :, h // 2, 128 * (h % 2):128 * (h % 2) + 64],
                                 io["ztm"][:, 1024 + 64 * h:1088 + 64 * h].rearrange("(t p) c -> p t c", p=128)).then_inc(v_in, 16)
                for i, t in enumerate(tiles):
                    sp.wait_ge(o_ev, i + 1)
                    sp.dma_start(io["mix"][t[0]:t[0] + 128, 256:640], o[i % 2][:, :]).then_inc(o_out[i % 2], 16)
                for j in range(2):
                    sp.wait_ge(o_out[j], 16 * (len(tiles) // 2))

            @block.gpsimd
            def _(pool):
                nc.gpsimd.memset(v[:, :, :, 64:128], 0.0).then_inc(z_ok, 1)

            @block.tensor
            def _(pe):
                def scores(n):
                    i, h = units[n]
                    tok, w0, nr, _, _ = tiles[i]
                    if n >= 2:
                        pe.wait_ge(s_used, n - 1)
                    lo, c = 64 * (h % 2), h // 2
                    ps = sp_ps[n % 2]
                    qt = q[lo:lo + 64, c, tok:tok + 128]
                    wl = nr * GRID
                    for a in range(0, wl, 512):
                        b = min(a + 512, wl)
                        nc.tensor.matmul(ps[:, a:b], qt, kk[lo:lo + 64, c, w0 * GRID + a:w0 * GRID + b], start=True, stop=True)
                    nc.tensor.matmul(ps[:, wl:wl + 256], qt, kk[lo:lo + 64, c, LX:LT], start=True, stop=True).then_inc(s_mm, 1)

                def transposes(n):
                    i, h = units[n]
                    pe.wait_ge(e_ok, n + 1)
                    ks = key_tiles(i)
                    if n >= 1:
                        pe.wait_ge(ta_ev, n)
                    local = [x for x in ks if x[0] == 0]
                    for _, j, nk, c0, _ in local:
                        last = nc.tensor.transpose(tpa[0:nk, j * 128:(j + 1) * 128], s_sb[n % 2][:, c0:c0 + nk], keep["ident"][:, :])
                    (last if local else pe.drain()).then_inc(ta_mm, 1)
                    if n >= 1:
                        pe.wait_ge(tb_ev, n)
                    for bk, j, nk, c0, _ in ks:
                        if bk == 1:
                            last = nc.tensor.transpose(tpb[0:nk, j * 128:(j + 1) * 128], s_sb[n % 2][:, c0:c0 + nk], keep["ident"][:, :])
                    last.then_inc(tb_mm, 1)

                def values(n):
                    i, h = units[n]
                    pe.wait_ge(ta_ev, n + 1)
                    pe.wait_ge(tb_ev, n + 1)
                    if h == 0 and i >= 2:
                        pe.wait_ge(o_ev, i - 1)
                    ks = key_tiles(i)
                    for m, (bk, j, nk, _, vt) in enumerate(ks):
                        last = nc.tensor.matmul(ops[i % 2][:, (h // 2) * 128:(h // 2 + 1) * 128], pt[n % 2][0:nk, 4 * bk + j, :],
                                                v[0:nk, vt, h // 2, 64 * (h % 2):64 * (h % 2) + 128],
                                                start=(m == 0 and h % 2 == 0), stop=(m == len(ks) - 1 and h % 2 == 1))
                    last.then_inc(pv_mm, 1)

                pe.wait_ge(na.k_in, 16)
                scores(0)
                for n in range(NU + 1):
                    if n + 1 < NU:
                        scores(n + 1)
                    if n < NU:
                        transposes(n)
                    if n == 1:
                        pe.wait_ge(v_in, 16 * NA_H)
                        pe.wait_ge(z_ok, 1)
                    if n >= 1:
                        values(n - 1)

            @block.vector
            def _(dve):
                def softmax_max(n):
                    i, h = units[n]
                    _, _, nr, b0, inner = tiles[i]
                    wl = nr * GRID
                    dve.wait_ge(s_mm, n + 1)
                    if n >= 2:
                        dve.wait_ge(tb_mm, n - 1)
                    ps, ss, m = sp_ps[n % 2], s_sb[n % 2], st[:, i % 2, h, :]
                    if nr:
                        bias = (ti[:, h, :, :] if inner else t2[:, h, b0:b0 + nr, :]).rearrange("p r c -> p (r c)")
                        nc.vector.tensor_tensor_reduce(out=ss[:, 0:wl], in0=ps[:, 0:wl], in1=bias, scale=1.0, scalar=LOWEST,
                                                       op0=ALU.add, op1=ALU.max, accum_out=m[:, 0:1])
                        dve.drain()
                    nc.vector.tensor_scalar(ss[:, wl:wl + 256], ps[:, wl:wl + 256], 1.0, m[:, 0:1] if nr else LOWEST,
                                            ALU.mult, ALU.max, accum_out=m[:, 1:2]).then_inc(s_used, 1)
                    dve.drain()
                    nc.vector.tensor_scalar(m[:, 2:3], m[:, 1:2], -1.0, None, ALU.mult).then_inc(m_ok, 1)

                def probs_out(n):
                    i, h = units[n]
                    dve.wait_ge(ta_mm, n + 1)
                    if n >= 2:
                        dve.wait_ge(pv_mm, n - 1)
                    if tiles[i][2]:
                        nc.vector.tensor_copy(pt[n % 2][:, 0:4, :], tpa[:, :].rearrange("p (a b) -> p a b", b=128)).then_inc(ta_ev, 1)
                    else:
                        dve.drain().then_inc(ta_ev, 1)

                def out(i):
                    dve.wait_ge(pv_mm, NA_H * (i + 1))
                    dve.wait_ge(e_ok, NA_H * (i + 1))
                    if i >= 2:
                        dve.wait_ge(o_out[i % 2], 16 * (i // 2))
                    nc.vector.reciprocal(rd[:, i % 2, :], st[:, i % 2, :, 3])
                    dve.drain()
                    nc.vector.tensor_tensor(o[i % 2][:, :].rearrange("p (h d) -> p h d", d=64),
                                            ops[i % 2][:, 0:D_NA].rearrange("p (h d) -> p h d", d=64),
                                            rd[:, i % 2, :, None].to_broadcast([128, NA_H, 64]), ALU.mult).then_inc(o_ev, 1)

                softmax_max(0)
                for n in range(NU + 1):
                    if n + 1 < NU:
                        softmax_max(n + 1)
                    if n < NU:
                        probs_out(n)
                    if n >= 2 and (n - 1) % NA_H == NA_H - 1:
                        out((n - 1) // NA_H)

            @block.scalar
            def _(act):
                def exps(n):
                    i, h = units[n]
                    w = tiles[i][2] * GRID + 256
                    act.wait_ge(m_ok, n + 1)
                    if h == 0 and i >= 2:
                        act.wait_ge(o_ev, i - 1)
                    m = st[:, i % 2, h, :]
                    act.activation(s_sb[n % 2][:, 0:w], s_sb[n % 2][:, 0:w], ACT.Exp, bias=m[:, 2:3],
                                   accum_out=m[:, 3:4]).then_inc(e_ok, 1)
                exps(0)
                for n in range(NU):
                    if n + 1 < NU:
                        exps(n + 1)
                    act.wait_ge(tb_mm, n + 1)
                    if n >= 2:
                        act.wait_ge(pv_mm, n - 1)
                    ks = key_tiles(units[n][0])
                    last = act.activation(pt[n % 2][:, 4:6, :], tpb[:, 0:256].rearrange("p (a b) -> p a b", b=128), ACT.Copy)
                    if ks[-1][2] == 64:
                        last = act.activation(pt[n % 2][0:64, 6, :], tpb[0:64, 256:384], ACT.Copy)
                    last.then_inc(tb_ev, 1)

def gla_phase(nc, l, io, keep):
    NCC = LC // CH
    fwd = list(range(LX // CH, NCH)) + list(range(LX // CH))
    order = [fwd, list(range(NCH - 1, LX // CH - 1, -1)) + list(range(LX // CH - 1, -1, -1))]
    TT = [(i * 512, min(512, LT - i * 512)) for i in range((LT + 511) // 512)]
    with phase(nc, "gla") as P:
        perm = P.sb("perm", [128, 128])
        mask = P.sb("mask", [128, 2, 128], I32)
        start = P.sb("start", [128, LT])
        wa = P.sb("wa", [64, 256])
        ba = P.sb("ba", [128, 4])
        z = P.sb("z", [64, LT])
        q = P.sb("q", [128, LT])
        k = P.sb("k", [128, LT])
        v = P.sb("v", [128, NT, 2 * GDV])
        b = [P.sb(f"b{d}", [128, LT]) for d in range(2)]
        t1 = [P.sb(f"t{d}", [128, LT]) for d in range(2)]
        cs, sn = t1[0][:, 0:LX], t1[1][:, 0:LX]
        qd = [P.sb(f"qd{d}", [128, LT]) for d in range(2)]
        kd = [P.sb(f"kd{d}", [128, LT]) for d in range(2)]
        kt = [P.sb(f"kt{d}", [128, NT, 128]) for d in range(2)]
        eb = P.sb("eb", [128, 2, NCH])
        S = P.sb("S", [128, 2, NCH, GDV])
        at = [P.sb(f"at{j}", [128, 4, 128]) for j in range(2)]
        o = [P.sb(f"o{j}", [128, 2 * GDV]) for j in range(2)]
        bank = [P.ps(f"bank{n}") for n in range(8)]
        big = bank[0:5]
        ups = [[bank[2 * p + j] for j in range(2)] for p in range(2)]
        aps = [[bank[2 * j + h] for h in range(2)] for j in range(2)]
        ops = [[bank[4 + 2 * j + h] for h in range(2)] for j in range(2)]
        UB = 5
        batches = [range(s0, min(s0 + UB, NCH - 1)) for s0 in range(0, NCH - 1, UB)]
        NB = len(batches)
        names = ("cst_in", "load_in", "v_in", "rot_mm", "rot_ev", "qk_ok", "g_mm", "abs_ok", "min_ok", "ln_ok", "b_ok",
                 "exp_q", "exp_k", "end_ok", "exp_e", "qd_ok", "kd_ok", "kte_ok", "kt_mm", "kt_dve", "kt_act", "u_mm", "s_ok",
                 "a_mm", "a_ok", "o_mm", "o_ok")
        m = {n: P.sem(n) for n in names}
        o_out = [P.sem(f"o_out{j}") for j in range(2)]
        KG = (NT + 3) // 4
        KD, KA = (KG + 1) // 2, KG // 2

        def group(g):
            return range(4 * g, min(4 * g + 4, NT))

        def store(sp, g):
            hh, n = g // NT, g % NT
            sp.wait_ge(m["o_ok"], g + 1)
            sp.dma_start(io["mix"][n * 128:(n + 1) * 128, 640 + hh * 192:640 + (hh + 1) * 192],
                         o[g % 2][:, :]).then_inc(o_out[g % 2], 16)

        with nc.Block() as block:
            @block.sync
            def _(sp):
                for dst, src in ((perm[:, :], io["rope_perm"]), (mask[:, :, :], io["gla_mask"]),
                                 (start[:, :], io["chunk_start"]),
                                 (wa[:, :], io["w_alpha"][bass.ds(l, 1), :, :].rearrange("a p n -> p (a n)")),
                                 (ba[:, :], io["b_alpha"][bass.ds(l, 1), :, :].rearrange("a p n -> p (a n)")),
                                 (z[0:RANK, :], io["zcm"][8, GDK:64, :]), (z[32:32 + RANK, :], io["zcm"][8, 64 + GDK:128, :])):
                    sp.dma_start(dst, src).then_inc(m["cst_in"], 16)
                for hh in range(2):
                    if hh:
                        sp.wait_ge(m["kt_mm"], 2 * KG)
                        sp.wait_ge(m["kd_ok"], 2)
                        sp.wait_ge(m["qd_ok"], 2)
                    sp.dma_start(q[:, :], io["zcm"][8 + hh, :, :]).then_inc(m["load_in"], 16)
                    sp.dma_start(k[:, :], io["zcm"][10 + hh, :, :]).then_inc(m["load_in"], 16)
                    sp.dma_start(cs, io["rope_cs"][:, 0, :]).then_inc(m["load_in"], 16)
                    sp.dma_start(sn, io["rope_cs"][:, 1, :]).then_inc(m["load_in"], 16)
                    if hh:
                        for n in range(NT):
                            store(sp, n)
                    c0 = 1024 + D_NA + hh * 2 * GDV
                    sp.dma_start(v[:, :, :], io["ztm"][:, c0:c0 + 2 * GDV].rearrange("(t p) c -> p t c", p=128)).then_inc(m["v_in"], 16)
                for n in range(NT, 2 * NT):
                    store(sp, n)
                for j in range(2):
                    sp.wait_ge(o_out[j], 16 * NT)

            @block.tensor
            def _(pe):
                def products(g):
                    n = g % NT
                    if g >= 2:
                        pe.wait_ge(m["a_ok"], g - 1)
                    for h in range(2):
                        for d in range(2):
                            last = nc.tensor.matmul(aps[g % 2][h][:, d * 128:(d + 1) * 128],
                                                    kd[d][64 * h:64 * h + 64, n * 128:(n + 1) * 128],
                                                    qd[d][64 * h:64 * h + 64, n * 128:(n + 1) * 128], start=True, stop=True)
                    last.then_inc(m["a_mm"], 1)

                pe.wait_ge(m["cst_in"], 16 * 7)
                for hh in range(2):
                    pe.wait_ge(m["load_in"], 64 * (hh + 1))
                    if hh:
                        pe.wait_ge(m["a_ok"], NT)
                        pe.wait_ge(m["o_ok"], NT)
                    for w, src in enumerate((q, k)):
                        if w:
                            pe.wait_ge(m["rot_ev"], 2 * hh + 1)
                        for n in range(4):
                            last = nc.tensor.matmul(big[n][:, :], perm[:, :], src[:, n * 512:(n + 1) * 512], start=True, stop=True)
                        last.then_inc(m["rot_mm"], 1)
                    pe.wait_ge(m["rot_ev"], 2 * hh + 2)
                    for d in range(2):
                        if d:
                            pe.wait_ge(m["abs_ok"], 2 * hh + 1)
                            pe.wait_ge(m["min_ok"], 2 * hh + 1)
                        for n, (a, w) in enumerate(TT):
                            last = nc.tensor.matmul(big[n][:, 0:w], wa[32 * d:32 * d + RANK, hh * 128:(hh + 1) * 128],
                                                    z[32 * d:32 * d + RANK, a:a + w], start=True, stop=True)
                        last.then_inc(m["g_mm"], 1)
                    pe.wait_ge(m["abs_ok"], 2 * hh + 2)
                    pe.wait_ge(m["min_ok"], 2 * hh + 2)
                    for d in range(2):
                        r = 2 * hh + d
                        pe.wait_ge(m["kte_ok"], r + 1)
                        if d:
                            pe.wait_ge(m["kt_dve"], KD * r)
                            pe.wait_ge(m["kt_act"], KA * r)
                        for g in range(KG):
                            for t in group(g):
                                last = nc.tensor.transpose(big[g][:, (t - 4 * g) * 128:(t - 4 * g + 1) * 128],
                                                           t1[d][:, t * 128:(t + 1) * 128], keep["ident"][:, :])
                            last.then_inc(m["kt_mm"], 1)
                    pe.wait_ge(m["kt_dve"], KD * 2 * (hh + 1))
                    pe.wait_ge(m["kt_act"], KA * 2 * (hh + 1))
                    pe.wait_ge(m["v_in"], 16 * (hh + 1))
                    for i, steps in enumerate(batches):
                        if i >= 2:
                            pe.wait_ge(m["s_ok"], hh * NB + i - 1)
                        for d in range(2):
                            for s in steps:
                                c = order[d][s]
                                p0 = 64 * (c % 2)
                                for h in range(2):
                                    last = nc.tensor.matmul(ups[c % 2][i % 2][64 * h:64 * h + 64, (s - steps[0]) * GDV:(s - steps[0] + 1) * GDV],
                                                            kt[d][p0:p0 + 64, c // 2, 64 * h:64 * h + 64],
                                                            v[p0:p0 + 64, c // 2, h * GDV:(h + 1) * GDV], start=True, stop=True)
                        last.then_inc(m["u_mm"], 1)
                    pe.wait_ge(m["s_ok"], (hh + 1) * NB)
                    pe.wait_ge(m["qd_ok"], 2 * (hh + 1))
                    pe.wait_ge(m["kd_ok"], 2 * (hh + 1))
                    products(hh * NT)
                    for n in range(NT):
                        g = hh * NT + n
                        if n + 1 < NT:
                            products(g + 1)
                        pe.wait_ge(m["a_ok"], g + 1)
                        if g >= 2:
                            pe.wait_ge(m["o_ok"], g - 1)
                        for h in range(2):
                            oc = ops[g % 2][h][:, 0:GDV]
                            for d in range(2):
                                nc.tensor.matmul(oc, at[g % 2][:, 2 * h + d, :], v[:, n, h * GDV:(h + 1) * GDV],
                                                 start=(d == 0), stop=False, skip_group_check=True)
                            for cc in range(2):
                                for d in range(2):
                                    c = 2 * n + cc
                                    last = nc.tensor.matmul(ops[g % 2][h][64 * cc:64 * cc + 64, 0:GDV],
                                                            qd[d][64 * h:64 * h + 64, c * 64:(c + 1) * 64],
                                                            S[64 * h:64 * h + 64, d, c, :], start=False, stop=(d == 1),
                                                            skip_group_check=True)
                        last.then_inc(m["o_mm"], 1)

            @block.vector
            def _(dve):
                nc.vector.memset(at[0][:, :, :], 0.0)
                nc.vector.memset(at[1][:, :, :], 0.0)
                for d in range(2):
                    nc.vector.memset(S[:, d, order[d][0], :], 0.0)
                dve.wait_ge(m["cst_in"], 16 * 7)
                for hh in range(2):
                    dve.wait_ge(m["load_in"], 64 * (hh + 1))
                    for w, x in enumerate((q, k)):
                        dve.wait_ge(m["rot_mm"], 2 * hh + w + 1)
                        nc.vector.tensor_tensor(x[:, 0:LX], x[:, 0:LX], cs, ALU.mult)
                        for n in range(4):
                            nc.vector.tensor_tensor(b[w][:, n * 512:(n + 1) * 512], big[n][:, :], sn[:, n * 512:(n + 1) * 512], ALU.mult)
                        dve.drain().then_inc(m["rot_ev"], 1)
                        nc.vector.tensor_tensor(x[:, 0:LX], x[:, 0:LX], b[w][:, 0:LX], ALU.add)
                        dve.drain()
                    nc.vector.tensor_scalar(q[:, :], q[:, :], GDK ** -0.5, None, ALU.mult).then_inc(m["qk_ok"], 1)
                    for d in range(2):
                        r = 2 * hh + d
                        dve.wait_ge(m["abs_ok"], r + 1)
                        for n, (a, w) in enumerate(TT):
                            nc.vector.tensor_scalar(b[d][:, a:a + w], big[n][:, 0:w], ba[:, 2 * d + hh:2 * d + hh + 1], 0.0, ALU.add, ALU.min)
                        dve.drain().then_inc(m["min_ok"], 1)
                    for d in range(2):
                        r = 2 * hh + d
                        dve.wait_ge(m["ln_ok"], r + 1)
                        nc.vector.tensor_tensor(t1[d][:, :], b[d][:, :], t1[d][:, :], ALU.subtract)
                        dve.drain()
                        if d == 0:
                            nc.vector.tensor_tensor_scan(b[d][:, :], start[:, :], t1[d][:, :], 0.0, ALU.mult, ALU.add)
                        else:
                            nc.vector.tensor_tensor_scan(b[d][:, ::-1], start[:, :], t1[d][:, ::-1], 0.0, ALU.mult, ALU.add)
                        dve.drain().then_inc(m["b_ok"], 1)
                        bc = b[d][:, :].rearrange("p (c t) -> p c t", t=CH)
                        end = bc[:, :, CH - 1] if d == 0 else bc[:, :, 0]
                        nc.vector.tensor_tensor(t1[d][:, :].rearrange("p (c t) -> p c t", t=CH),
                                                end[:, :, None].to_broadcast([128, NCH, CH]), bc, ALU.subtract).then_inc(m["end_ok"], 1)
                    for d in range(2):
                        r = 2 * hh + d
                        for g in range(0, KG, 2):
                            dve.wait_ge(m["kt_mm"], KG * r + g + 1)
                            n = len(group(g))
                            nc.vector.tensor_copy(kt[d][:, 4 * g:4 * g + n, :],
                                                  big[g][:, 0:128 * n].rearrange("p (a b) -> p a b", b=128)).then_inc(m["kt_dve"], 1)
                    for i, steps in enumerate(batches):
                        dve.wait_ge(m["u_mm"], hh * NB + i + 1)
                        for s in steps:
                            for d in range(2):
                                c, nx = order[d][s], order[d][s + 1]
                                nc.vector.scalar_tensor_tensor(S[:, d, nx, :], S[:, d, c, :], eb[:, d, c:c + 1],
                                                               ups[c % 2][i % 2][:, (s - steps[0]) * GDV:(s - steps[0] + 1) * GDV],
                                                               ALU.mult, ALU.add)
                            last = dve.drain()
                        last.then_inc(m["s_ok"], 1)
                    for n in range(NT):
                        g = hh * NT + n
                        dve.wait_ge(m["a_mm"], g + 1)
                        if g >= 2:
                            dve.wait_ge(m["o_mm"], g - 1)
                        for h in range(2):
                            last = nc.vector.copy_predicated(at[g % 2][:, 2 * h:2 * h + 2, :].rearrange("p a b -> p (a b)"),
                                                             mask[:, :, :].rearrange("p b c -> p (b c)"), aps[g % 2][h][:, 0:256])
                        last.then_inc(m["a_ok"], 1)

            @block.gpsimd
            def _(pool):
                for hh in range(2):
                    for d in range(2):
                        r = 2 * hh + d
                        pool.wait_ge(m["exp_q"], r + 1)
                        nc.gpsimd.tensor_tensor(qd[d][:, :], q[:, :], qd[d][:, :], ALU.mult).then_inc(m["qd_ok"], 1)
                        pool.wait_ge(m["exp_e"], r + 1)
                        nc.gpsimd.tensor_tensor(t1[d][:, :], k[:, :], t1[d][:, :], ALU.mult).then_inc(m["kte_ok"], 1)
                        pool.wait_ge(m["exp_k"], r + 1)
                        nc.gpsimd.tensor_tensor(kd[d][:, :], k[:, :], kd[d][:, :], ALU.mult).then_inc(m["kd_ok"], 1)

            @block.scalar
            def _(act):
                for hh in range(2):
                    for d in range(2):
                        r = 2 * hh + d
                        act.wait_ge(m["g_mm"], r + 1)
                        if d == 0:
                            act.wait_ge(m["qk_ok"], hh + 1)
                        for n, (a, w) in enumerate(TT):
                            act.activation(t1[d][:, a:a + w], big[n][:, 0:w], ACT.Abs, bias=ba[:, 2 * d + hh:2 * d + hh + 1])
                        act.drain().then_inc(m["abs_ok"], 1)
                        act.activation(t1[d][:, :], t1[d][:, :], ACT.Exp, scale=-1.0)
                        act.drain()
                        act.activation(t1[d][:, :], t1[d][:, :], ACT.Ln, bias=1.0).then_inc(m["ln_ok"], 1)
                    if hh:
                        act.wait_ge(m["o_mm"], NT)
                    for d in range(2):
                        r = 2 * hh + d
                        act.wait_ge(m["b_ok"], r + 1)
                        bc = b[d][:, :].rearrange("p (c t) -> p c t", t=CH)
                        act.activation(eb[:, d, :], bc[:, :, CH - 1] if d == 0 else bc[:, :, 0], ACT.Exp, scale=1.0 / 16)
                        act.activation(qd[d][:, :], b[d][:, :], ACT.Exp, scale=1.0 / 16).then_inc(m["exp_q"], 1)
                        act.wait_ge(m["end_ok"], r + 1)
                        act.activation(t1[d][:, :], t1[d][:, :], ACT.Exp, scale=1.0 / 16).then_inc(m["exp_e"], 1)
                        act.activation(kd[d][:, :], b[d][:, :], ACT.Exp, scale=-1.0 / 16).then_inc(m["exp_k"], 1)
                    for d in range(2):
                        r = 2 * hh + d
                        for g in range(1, KG, 2):
                            act.wait_ge(m["kt_mm"], KG * r + g + 1)
                            n = len(group(g))
                            act.activation(kt[d][:, 4 * g:4 * g + n, :],
                                           big[g][:, 0:128 * n].rearrange("p (a b) -> p a b", b=128), ACT.Copy).then_inc(m["kt_act"], 1)
                    for n in range(NT):
                        g = hh * NT + n
                        act.wait_ge(m["o_mm"], g + 1)
                        if g >= 2:
                            act.wait_ge(o_out[g % 2], 16 * (g // 2))
                        for h in range(2):
                            last = act.activation(o[g % 2][:, h * GDV:(h + 1) * GDV], ops[g % 2][h][:, 0:GDV], ACT.Copy)
                        last.then_inc(m["o_ok"], 1)


def out_phase(nc, l, io, keep):
    with phase(nc, "out") as P:
        raw = [P.sb(f"raw{j}", [128, D]) for j in range(3)]
        w = Split(P.sb, "w", [128, KC, D])
        gate = P.sb("gate", [128, 2, D])
        gw = P.sb("gw", [128, GH, GDV])
        mx = [P.sb(f"mx{j}", [128, D]) for j in range(2)]
        gt = [P.sb(f"gt{j}", [128, D]) for j in range(2)]
        x = [P.sb(f"x{j}", [128, D]) for j in range(3)]
        mT = [Split(P.sb, f"mT{j}", [128, KC, 128]) for j in range(2)]
        y = P.sb("y", [128, D])
        sq = P.sb("sq", [128, GH, GDV])
        ss = P.sb("ss", [128, 2, 2, GH])
        tp = [[P.ps(f"tp{j}{h}") for h in range(2)] for j in range(2)]
        acc = [[P.ps(f"acc{j}{h}") for h in range(2)] for j in range(2)]
        w_in, ss_ok, sr_ok, m_ok, t_mm, t_dve, t_act, y_mm, y_ok, x_ok = [P.sem(s) for s in (
            "w_in", "ss_ok", "sr_ok", "m_ok", "t_mm", "t_dve", "t_act", "y_mm", "y_ok", "x_ok")]
        raw_in = [P.sem(f"raw_in{j}") for j in range(3)]
        w_hi, w_ok = P.sem("w_hi"), P.sem("w_ok")
        ld = [P.sem(f"ld{j}") for j in range(2)]
        xl = [P.sem(f"xl{j}") for j in range(3)]
        xo = [P.sem(f"xo{j}") for j in range(3)]
        with nc.Block() as block:
            @block.sync
            def _(sp):
                for s in range(2):
                    sp.dma_start(gate[:, s, :], bcast_rows(io["gates"][s, :], D)).then_inc(w_in, 16)
                for h in range(GH):
                    sp.dma_start(gw[:, h, :], io["gla_norm_w"][bass.ds(l, 1), :].to_broadcast([128, GDV])).then_inc(w_in, 16)
                for t in range(NT):
                    rows = slice(t * 128, (t + 1) * 128)
                    if t >= 2:
                        sp.wait_ge(m_ok, t - 1)
                        sp.wait_ge(t_mm, t - 1)
                    sp.dma_start(mx[t % 2][:, :], io["mix"][rows, :]).then_inc(ld[t % 2], 16)
                    sp.dma_start(gt[t % 2][:, :], io["ztm"][rows, 0:D]).then_inc(ld[t % 2], 16)
                    if t >= 3:
                        sp.wait_ge(xo[t % 3], 16 * (t // 3))
                    sp.dma_start(x[t % 3][:, :], io["xres"][rows, :]).then_inc(xl[t % 3], 16)
                    if t == 0:
                        for k in range(KC):
                            if k >= 3:
                                sp.wait_ge(w_ok, k - 2)
                            sp.dma_start(raw[k % 3][:, :], io["w_out"][bass.ds(l, 1), k * 128:(k + 1) * 128, :].rearrange("a p n -> p (a n)")).then_inc(raw_in[k % 3], 16)

            @block.gpsimd
            def _(pool):
                for k in range(KC):
                    pool.wait_ge(w_hi, k + 1)
                    nc.gpsimd.tensor_tensor(w.lo[:, k, :], raw[k % 3][:, :], w.hi[:, k, :].bitcast(F32), ALU.subtract).then_inc(w_ok, 1)
                for t in range(NT):
                    pool.wait_ge(x_ok, t + 1)
                    pool.dma_start(io["xres"][t * 128:(t + 1) * 128, :], x[t % 3][:, :]).then_inc(xo[t % 3], 16)
                for j in range(3):
                    pool.wait_ge(xo[j], 16 * (NT // 3))

            @block.vector
            def _(dve):
                def mixed(t):
                    j = t % 2
                    g = mx[j][:, 640:1024].rearrange("p (h d) -> p h d", d=GDV)
                    dve.wait_ge(ld[j], 32 * (t // 2 + 1))
                    nc.vector.tensor_tensor(sq[:, :, :], g, g, ALU.mult)
                    dve.drain()
                    nc.vector.tensor_reduce(ss[:, j, 0, :], sq[:, :, :], AX.X, ALU.add).then_inc(ss_ok, 1)
                    nc.vector.tensor_tensor(mx[j][:, 0:640], mx[j][:, 0:640], gt[j][:, 0:640], ALU.mult)
                    dve.drain()
                    nc.vector.tensor_tensor(sq[:, :, :], gt[j][:, 640:1024].rearrange("p (h d) -> p h d", d=GDV), gw[:, :, :], ALU.mult)
                    dve.wait_ge(sr_ok, t + 1)
                    nc.vector.reciprocal(ss[:, j, 1, :], ss[:, j, 1, :])
                    dve.drain()
                    nc.vector.tensor_tensor(g, g, ss[:, j, 1, :, None].to_broadcast([128, GH, GDV]), ALU.mult)
                    dve.drain()
                    nc.vector.tensor_tensor(g, g, sq[:, :, :], ALU.mult).then_inc(m_ok, 1)

                def taken(t):
                    j = t % 2
                    dve.wait_ge(t_mm, t + 1)
                    if t >= 2:
                        dve.wait_ge(y_mm, t - 1)
                    for i in range(2):
                        if i:
                            dve.wait_ge(t_act, t + 1)
                        src = tp[j][i][:, :].rearrange("p (a b) -> p a b", b=128)
                        hi = mT[j].hi[:, 4 * i:4 * i + 4, :]
                        if i == 0:
                            nc.vector.tensor_copy(hi, src)
                            dve.drain()
                        last = nc.vector.tensor_tensor(mT[j].lo[:, 4 * i:4 * i + 4, :], src, hi.bitcast(F32), ALU.subtract)
                    last.then_inc(t_dve, 1)

                def residual(t):
                    j = t % 2
                    dve.wait_ge(y_mm, t + 1)
                    s = 0 if t < NX else 1
                    for h in range(2):
                        nc.vector.tensor_tensor(y[:, h * 512:(h + 1) * 512], acc[j][h][:, :], gate[:, s, h * 512:(h + 1) * 512], ALU.mult)
                    dve.drain().then_inc(y_ok, 1)
                    dve.wait_ge(xl[t % 3], 16 * (t // 3 + 1))
                    nc.vector.tensor_tensor(x[t % 3][:, :], x[t % 3][:, :], y[:, :], ALU.add).then_inc(x_ok, 1)
                    dve.drain()

                dve.wait_ge(w_in, 16 * (2 + GH))
                mixed(0)
                for t in range(NT):
                    taken(t)
                    if t + 1 < NT:
                        mixed(t + 1)
                    if t >= 1:
                        residual(t - 1)
                residual(NT - 1)

            @block.scalar
            def _(act):
                def root(t):
                    act.wait_ge(ss_ok, t + 1)
                    act.activation(ss[:, t % 2, 1, :], ss[:, t % 2, 0, :], ACT.Sqrt, scale=1.0 / GDV, bias=keep["eps"][:, 0:1]).then_inc(sr_ok, 1)
                root(0)
                for k in range(KC):
                    act.wait_ge(raw_in[k % 3], 16 * (k // 3 + 1))
                    act.activation(w.hi[:, k, :], raw[k % 3][:, :], ACT.Copy).then_inc(w_hi, 1)
                for t in range(NT):
                    act.wait_ge(t_mm, t + 1)
                    if t >= 2:
                        act.wait_ge(y_mm, t - 1)
                    act.activation(mT[t % 2].hi[:, 4:8, :], tp[t % 2][1][:, :].rearrange("p (a b) -> p a b", b=128), ACT.Copy).then_inc(t_act, 1)
                    if t + 1 < NT:
                        root(t + 1)

            @block.tensor
            def _(pe):
                def transposes(t):
                    pe.wait_ge(m_ok, t + 1)
                    if t >= 2:
                        pe.wait_ge(t_dve, t - 1)
                    for k in range(KC):
                        last = nc.tensor.transpose(tp[t % 2][k // 4][:, (k % 4) * 128:(k % 4 + 1) * 128],
                                                   mx[t % 2][:, k * 128:(k + 1) * 128], keep["ident"][:, :])
                    last.then_inc(t_mm, 1)
                transposes(0)
                for t in range(NT):
                    if t + 1 < NT:
                        transposes(t + 1)
                    pe.wait_ge(t_dve, t + 1)
                    if t >= 2:
                        pe.wait_ge(y_ok, t - 1)
                    for h in range(2):
                        for k in range(KC):
                            if t == 0 and h == 0:
                                pe.wait_ge(w_ok, k + 1)
                            last = matmul3(nc, acc[t % 2][h][:, :], mT[t % 2][:, k, :], w[:, k, h * 512:(h + 1) * 512], k == 0, k == KC - 1)
                    last.then_inc(y_mm, 1)

def qk_phase(nc, io, keep):
    with phase(nc, "qk") as P:
        TWO_PI = 2 * math.pi
        C1 = 6.28125
        C2 = float(np.float32(round((TWO_PI - C1) * 2 ** 20) / 2 ** 20))
        C3 = float(np.float32(TWO_PI - C1 - C2))
        MAGIC = 1.5 * 2 ** 23
        LIM = float(np.nextafter(np.float32(math.pi), np.float32(0)))
        pos = P.sb("pos", [128, NX], I32)
        posf = P.sb("posf", [128, NX])
        inv = P.sb("inv", [128, 32])
        ang = P.sb("ang", [128, NX, 32])
        trn = P.sb("trn", [128, NX, 32])
        sc = P.sb("sc", [128, 2, NX, 32])
        wqk = P.sb("wqk", [128, 2, HD])
        x = [P.sb(f"x{j}", [128, 16, HD]) for j in range(3)]
        y = [P.sb(f"y{j}", [128, 16, HD]) for j in range(2)]
        sq = [P.sb(f"sq{j}", [128, 16, HD]) for j in range(2)]
        pr = P.sb("pr", [128, 2, 16, 32])
        pp = P.sb("pp", [128, 2, 16, 32])
        ss = P.sb("ss", [128, 2, 2, 16])
        cst_in, red_ok, sc_ok, sq_ok, ss_ok, sr_ok, n_ok, y_dve, y_pool, w_ok = [P.sem(s) for s in (
            "cst_in", "red_ok", "sc_ok", "sq_ok", "ss_ok", "sr_ok", "n_ok", "y_dve", "y_pool", "w_ok")]
        ld = [P.sem(f"ld{j}") for j in range(3)]
        out = [P.sem(f"out{j}") for j in range(2)]
        def store(sp, t):
            sp.wait_ge(y_dve, t + 1)
            sp.wait_ge(y_pool, t + 1)
            sp.dma_start(io["z2"][t * 128:(t + 1) * 128, 0:1024], y[t % 2][:, :, :].rearrange("p h d -> p (h d)")).then_inc(out[t % 2], 16)

        with nc.Block() as block:
            @block.sync
            def _(sp):
                sp.dma_start(pos[:, :], io["positions"]).then_inc(cst_in, 16)
                sp.dma_start(inv[:, :], bcast_rows(io["inv_freq"], 32)).then_inc(cst_in, 16)
                sp.dma_start(wqk[:, 0, :], bcast_rows(io["q_norm"], HD)).then_inc(cst_in, 16)
                sp.dma_start(wqk[:, 1, :], bcast_rows(io["k_norm"], HD)).then_inc(cst_in, 16)
                for t in range(NX):
                    if t >= 3:
                        sp.wait_ge(y_dve, t - 2)
                        sp.wait_ge(y_pool, t - 2)
                    sp.dma_start(x[t % 3][:, :, :].rearrange("p h d -> p (h d)"), io["z2"][t * 128:(t + 1) * 128, 0:1024]).then_inc(ld[t % 3], 16)
                    if t >= 1:
                        store(sp, t - 1)
                store(sp, NX - 1)
                for j in range(2):
                    sp.wait_ge(out[j], 16 * (NX // 2))

            @block.scalar
            def _(act):
                for w in range(2):
                    act.wait_ge(red_ok, w + 1)
                    act.activation(sc[:, w, :, :], trn[:, :, :], ACT.Sin).then_inc(sc_ok, 1)
                for t in range(NX):
                    act.wait_ge(ld[t % 3], 16 * (t // 3 + 1))
                    if t >= 2:
                        act.wait_ge(ss_ok, t - 1)
                    act.activation(sq[t % 2][:, :, :], x[t % 3][:, :, :], ACT.Square).then_inc(sq_ok, 1)
                    act.wait_ge(ss_ok, t + 1)
                    act.activation(ss[:, t % 2, 1, :], ss[:, t % 2, 0, :], ACT.Sqrt, scale=1.0 / HD, bias=keep["eps"][:, 0:1]).then_inc(sr_ok, 1)

            @block.vector
            def _(dve):
                dve.wait_ge(cst_in, 64)
                nc.vector.tensor_scalar(wqk[:, 0, :], wqk[:, 0, :], HD ** -0.5, None, ALU.mult)
                nc.vector.tensor_copy(posf[:, :], pos[:, :])
                dve.drain()
                nc.vector.tensor_tensor(ang[:, :, :], posf[:, :, None].to_broadcast([128, NX, 32]),
                                        inv[:, None, :].to_broadcast([128, NX, 32]), ALU.mult)
                dve.drain()
                for w, (turn, add) in enumerate(((0.25, math.pi / 2), (0.0, 0.0))):
                    if w:
                        dve.wait_ge(sc_ok, 1)
                    nc.vector.tensor_scalar(trn[:, :, :], ang[:, :, :], 1 / TWO_PI, turn, ALU.mult, ALU.add)
                    dve.drain()
                    nc.vector.tensor_scalar(trn[:, :, :], trn[:, :, :], MAGIC, None, ALU.add)
                    dve.drain()
                    nc.vector.tensor_scalar(trn[:, :, :], trn[:, :, :], MAGIC, None, ALU.subtract)
                    dve.drain()
                    whole = sq[0][:, 0:8, :].rearrange("p a b -> p (a b)").rearrange("p (a b) -> p a b", b=32)
                    nc.vector.scalar_tensor_tensor(whole, trn[:, :, :], -C1, ang[:, :, :], ALU.mult, ALU.add)
                    dve.drain()
                    nc.vector.scalar_tensor_tensor(whole, trn[:, :, :], -C2, whole, ALU.mult, ALU.add)
                    dve.drain()
                    nc.vector.scalar_tensor_tensor(whole, trn[:, :, :], -C3, whole, ALU.mult, ALU.add)
                    dve.drain()
                    nc.vector.tensor_scalar(whole, whole, add, LIM, ALU.add, ALU.min)
                    dve.drain()
                    nc.vector.tensor_scalar(trn[:, :, :], whole, -LIM, None, ALU.max).then_inc(red_ok, 1)
                    dve.drain()
                dve.wait_ge(sc_ok, 2)
                for t in range(NX):
                    xs, ys = x[t % 3], y[t % 2]
                    dve.wait_ge(sq_ok, t + 1)
                    nc.vector.tensor_reduce(ss[:, t % 2, 0, :], sq[t % 2][:, :, :], AX.X, ALU.add).then_inc(ss_ok, 1)
                    dve.wait_ge(sr_ok, t + 1)
                    nc.vector.reciprocal(ss[:, t % 2, 1, :], ss[:, t % 2, 1, :])
                    dve.drain()
                    nc.vector.tensor_tensor(xs[:, :, :], xs[:, :, :], ss[:, t % 2, 1, :, None].to_broadcast([128, 16, HD]), ALU.mult)
                    dve.drain()
                    for w in range(2):
                        last = nc.vector.tensor_tensor(xs[:, 8 * w:8 * w + 8, :], xs[:, 8 * w:8 * w + 8, :],
                                                       wqk[:, w, None, :].to_broadcast([128, 8, HD]), ALU.mult)
                    dve.drain().then_inc(n_ok, 1)
                    c = sc[:, 0, t, None, :].to_broadcast([128, 16, 32])
                    s = sc[:, 1, t, None, :].to_broadcast([128, 16, 32])
                    nc.vector.tensor_tensor(pr[:, 0, :, :], xs[:, :, 0:32], c, ALU.mult)
                    nc.vector.tensor_tensor(pr[:, 1, :, :], xs[:, :, 32:64], s, ALU.mult)
                    dve.drain()
                    if t >= 2:
                        dve.wait_ge(out[t % 2], 16 * (t // 2))
                    nc.vector.tensor_tensor(ys[:, :, 0:32], pr[:, 0, :, :], pr[:, 1, :, :], ALU.subtract).then_inc(y_dve, 1)
                    dve.drain()

            @block.gpsimd
            def _(pool):
                pool.wait_ge(sc_ok, 2)
                for t in range(NX):
                    xs, ys = x[t % 3], y[t % 2]
                    pool.wait_ge(n_ok, t + 1)
                    c = sc[:, 0, t, None, :].to_broadcast([128, 16, 32])
                    s = sc[:, 1, t, None, :].to_broadcast([128, 16, 32])
                    nc.gpsimd.tensor_tensor(pp[:, 0, :, :], xs[:, :, 32:64], c, ALU.mult)
                    nc.gpsimd.tensor_tensor(pp[:, 1, :, :], xs[:, :, 0:32], s, ALU.mult).then_inc(w_ok, 1)
                    pool.wait_ge(w_ok, 2 * t + 1)
                    if t >= 2:
                        pool.wait_ge(out[t % 2], 16 * (t // 2))
                    nc.gpsimd.tensor_tensor(ys[:, :, 32:64], pp[:, 0, :, :], pp[:, 1, :, :], ALU.add).then_inc(y_pool, 1)
                    pool.wait_ge(y_pool, t + 1)
                    pool.drain().then_inc(w_ok, 1)


def branch_phase(nc, io, keep):
    blocks = []
    for br, r in enumerate((1, 4, 16)):
        for c in range(r):
            for b in range(LX // r // 128):
                blocks.append((br, r, c, b))
    NB = len(blocks)
    NG = 4 * NB
    steps = []
    use = {}
    def add(kind, i):
        use[(kind, i)] = len(steps)
        steps.append((kind, i))
    add("q", 0)
    add("k", 0)
    for g in range(NG):
        add("p", g)
        if g % 4 == 0 and g // 4 + 1 < NB:
            add("q", g // 4 + 1)
            add("k", g // 4 + 1)
    first = {}
    for u, (kind, i) in enumerate(steps):
        g = i if kind == "p" else 4 * (i - 1)
        first.setdefault(g, []).append(u)
    with phase(nc, "br") as P:
        band = P.sb("band", [128, 256])
        x = [P.sb(f"x{j}", [128, 1536]) for j in range(3)]
        vp = [P.sb(f"v{j}", [128, 4, 192]) for j in range(4)]
        qT = [P.sb(f"qT{j}", [128, 4, 128]) for j in range(2)]
        kT = [P.sb(f"kT{j}", [128, 4, 128]) for j in range(3)]
        s_sb = [P.sb(f"s{j}", [128, 2, 256]) for j in range(2)]
        pt = [P.sb(f"pt{j}", [128, 4, 128]) for j in range(2)]
        nm = P.sb("nm", [128, 2, 2])
        o = [P.sb(f"o{j}", [128, ORW]) for j in range(2)]
        S = [[P.ps(f"S{h}{j}") for j in range(2)] for h in range(2)]
        T = [P.ps(f"T{j}") for j in range(2)]
        O = [P.ps(f"O{j}") for j in range(2)]
        band_in, s_mm, m_ok, n_ok, e_ok, t_mm, pv_mm, o_ev = [P.sem(s) for s in (
            "band_in", "s_mm", "m_ok", "n_ok", "e_ok", "t_mm", "pv_mm", "o_ev")]
        ev = [P.sem("ev_dve"), P.sem("ev_act")]
        ld = [P.sem(f"ld{j}") for j in range(3)]
        v_ok, v_zero = P.sem("v_ok"), P.sem("v_zero")
        out = [P.sem(f"out{j}") for j in range(2)]

        def rows(name, n):
            br, r, c, b = blocks[n]
            base = io["z2"] if name == "z2" else io["branch"][br]
            return base.rearrange("(n r) c -> r n c", r=r)[c, b * 128:(b + 1) * 128, :]

        def halves(n):
            return (0, 1) if blocks[n][3] else (1,)

        def wait_evac(eng, u):
            eng.wait_ge(ev[u % 2], u // 2 + 1)

        with nc.Block() as block:
            @block.sync
            def _(sp):
                sp.dma_start(band[:, :], io["band"]).then_inc(band_in, 16)
                def load(n):
                    if n >= 3:
                        sp.wait_ge(t_mm, use[("k", n - 3)] + 1)
                        sp.wait_ge(v_ok, n - 2)
                    sp.dma_start(x[n % 3][:, :], rows("z2", n)[:, 0:1536]).then_inc(ld[n % 3], 16)
                load(0)
                load(1)
                for n in range(NB):
                    if n + 2 < NB:
                        load(n + 2)
                    sp.wait_ge(o_ev, n + 1)
                    sp.dma_start(rows("branch", n), o[n % 2][:, :]).then_inc(out[n % 2], 16)
                for j in range(2):
                    sp.wait_ge(out[j], 16 * (NB // 2))

            @block.tensor
            def _(pe):
                def transposes(u):
                    kind, i = steps[u]
                    if u >= 2:
                        pe.wait_ge(ev[u % 2], u // 2)
                    if kind == "p":
                        pe.wait_ge(e_ok, i + 1)
                        hs = halves(i // 4)
                        for h in range(2):
                            for w in hs:
                                last = nc.tensor.transpose(T[u % 2][:, (2 * h + w) * 128:(2 * h + w + 1) * 128],
                                                           s_sb[i % 2][:, h, w * 128:(w + 1) * 128], keep["ident"][:, :])
                    else:
                        pe.wait_ge(ld[i % 3], 16 * (i // 3 + 1))
                        o0 = 0 if kind == "q" else 512
                        for c in range(4):
                            last = nc.tensor.transpose(T[u % 2][:, c * 128:(c + 1) * 128],
                                                       x[i % 3][:, o0 + c * 128:o0 + (c + 1) * 128], keep["ident"][:, :])
                    last.then_inc(t_mm, 1)

                def scores(g):
                    n, p = g // 4, g % 4
                    if p == 0:
                        wait_evac(pe, use[("q", n)])
                        wait_evac(pe, use[("k", n)])
                    if g >= 2:
                        pe.wait_ge(m_ok, g - 1)
                    for h in range(2):
                        for w in halves(n):
                            last = nc.tensor.matmul(S[h][g % 2][:, w * 128:(w + 1) * 128], qT[n % 2][64 * h:64 * h + 64, p, :],
                                                    kT[(n - 1 + w) % 3][64 * h:64 * h + 64, p, :], start=True, stop=True)
                    last.then_inc(s_mm, 1)

                def values(g):
                    n, p = g // 4, g % 4
                    wait_evac(pe, use[("p", g)])
                    if p == 0:
                        pe.wait_ge(v_ok, n + 1)
                    if p == 0 and n >= 2:
                        pe.wait_ge(o_ev, n - 1)
                    hs = halves(n)
                    for h in range(2):
                        for w in hs:
                            last = nc.tensor.matmul(O[n % 2][:, p * 128:(p + 1) * 128], pt[g % 2][:, 2 * h + w, :],
                                                    vp[(n - 1 + w) % 4][:, p, 64 * h:64 * h + 128],
                                                    start=(w == hs[0] and h == 0), stop=(w == 1 and h == 1))
                    last.then_inc(pv_mm, 1)

                transposes(0)
                transposes(1)
                scores(0)
                for g in range(NG + 1):
                    if g + 1 < NG:
                        scores(g + 1)
                    if g < NG:
                        for u in first[g]:
                            transposes(u)
                    if g >= 1:
                        values(g - 1)

            @block.gpsimd
            def _(pool):
                for j in range(4):
                    last = nc.gpsimd.memset(vp[j][:, :, 64:128], 0.0)
                last.then_inc(v_zero, 1)
                pool.wait_ge(v_zero, 1)
                for n in range(NB):
                    pool.wait_ge(ld[n % 3], 16 * (n // 3 + 1))
                    if n >= 4:
                        pool.wait_ge(pv_mm, 4 * (n - 2))
                    nc.gpsimd.tensor_copy(vp[n % 4][:, :, :].rearrange("p a (b c) -> p a b c", c=64)[:, :, ::2, :],
                                          x[n % 3][:, 1024:1536].rearrange("p (a b c) -> p a b c", b=2, c=64)).then_inc(v_ok, 1)

            def take(eng, copy, u):
                kind, i = steps[u]
                eng.wait_ge(t_mm, u + 1)
                src = T[u % 2][:, :].rearrange("p (a b) -> p a b", b=128)
                if kind == "p":
                    if i >= 2:
                        eng.wait_ge(pv_mm, i - 1)
                    if len(halves(i // 4)) == 2:
                        copy(pt[i % 2][:, :, :], src).then_inc(ev[u % 2], 1)
                    else:
                        copy(pt[i % 2][:, 1::2, :], src[:, 1::2, :]).then_inc(ev[u % 2], 1)
                else:
                    if i >= 2:
                        eng.wait_ge(s_mm, 4 * (i - 1))
                    copy((qT[i % 2] if kind == "q" else kT[i % 3])[:, :, :], src).then_inc(ev[u % 2], 1)

            @block.vector
            def _(dve):
                def maxima(g):
                    n, p = g // 4, g % 4
                    dve.wait_ge(s_mm, g + 1)
                    if g >= 2:
                        dve.wait_ge(t_mm, use[("p", g - 2)] + 1)
                    if p == 0 and n >= 2:
                        dve.wait_ge(out[n % 2], 16 * (n // 2))
                    a = 128 * halves(n)[0]
                    for h in range(2):
                        last = nc.vector.tensor_tensor_reduce(out=s_sb[g % 2][:, h, a:256], in0=S[h][g % 2][:, a:256], in1=band[:, a:256],
                                                              scale=1.0, scalar=LOWEST, op0=ALU.add, op1=ALU.max,
                                                              accum_out=o[n % 2][:, 512 + 2 * p + h:513 + 2 * p + h])
                    dve.drain().then_inc(m_ok, 1)
                    if g >= 2:
                        dve.wait_ge(e_ok, g - 1)
                    nc.vector.tensor_scalar(nm[:, g % 2, :], o[n % 2][:, 512 + 2 * p:514 + 2 * p], -1.0, None, ALU.mult).then_inc(n_ok, 1)

                take_ = lambda u: take(dve, nc.vector.tensor_copy, u)
                take_(0)
                dve.wait_ge(band_in, 16)
                maxima(0)
                for g in range(NG):
                    if g + 1 < NG:
                        maxima(g + 1)
                    for u in first[g]:
                        if u % 2 == 0:
                            take_(u)

            @block.scalar
            def _(act):
                def exps(g):
                    n, p = g // 4, g % 4
                    act.wait_ge(n_ok, g + 1)
                    if p == 0 and n >= 2:
                        act.wait_ge(out[n % 2], 16 * (n // 2))
                    a = 128 * halves(n)[0]
                    for h in range(2):
                        last = act.activation(s_sb[g % 2][:, h, a:256], s_sb[g % 2][:, h, a:256], ACT.Exp, bias=nm[:, g % 2, h:h + 1],
                                              accum_out=o[n % 2][:, 520 + 2 * p + h:521 + 2 * p + h])
                    last.then_inc(e_ok, 1)
                take_ = lambda u: take(act, lambda d, s: act.activation(d, s, ACT.Copy), u)
                take_(1)
                exps(0)
                for g in range(NG + 1):
                    if g + 1 < NG:
                        exps(g + 1)
                    for u in (first[g] if g < NG else []):
                        if u % 2:
                            take_(u)
                    if g and g % 4 == 0:
                        n = g // 4 - 1
                        act.wait_ge(pv_mm, 4 * (n + 1))
                        act.activation(o[n % 2][:, 0:512], O[n % 2][:, :], ACT.Copy).then_inc(o_ev, 1)


def last_phase(nc, io, keep):
    with phase(nc, "fin") as P:
        wo = Split(P.sb, "wo", [128, KC, D])
        wg = P.sb("wg", [128, KC, D])
        wp = P.sb("wp", [128, 2, D])
        ws = P.sb("ws", [128, 4, 128])
        wsT = P.sb("wsT", [128, 4, 128])
        tril = P.sb("tril", [128, 128])
        bs = P.sb("bs", [128, 4])
        lg, lb = P.sb("lg", [128, 512]), P.sb("lb", [128, 512])
        bg = P.sb("bg", [128, D])
        gp = P.sb("gp", [128, KC])
        ob = [P.sb(f"ob{j}", [128, 3, ORW]) for j in range(2)]
        z = [P.sb(f"z{j}", [128, 4, 512]) for j in range(2)]
        h = [P.sb(f"h{j}", [128, D]) for j in range(4)]
        pl = [P.sb(f"pl{j}", [128, 256]) for j in range(2)]
        plT = [P.sb(f"plT{j}", [128, 2, 128]) for j in range(4)]
        mx = [P.sb(f"mx{j}", [128, D]) for j in range(2)]
        mT = Split(P.sb, "mT", [128, KC, 128])
        hn = P.sb("hn", [128, D])
        hT = P.sb("hT", [128, KC, 128])
        mTf = P.sb("mTf", [128, 4, 128])
        sg = P.sb("sg", [128, D])
        sg2 = P.sb("sg2", [128, D])
        tmp = P.sb("tmp", [128, 512])
        bn = P.sb("bn", [128, 6])
        mv = P.sb("mv", [128, 2, 4])
        sm = P.sb("sm", [128, 8, 3, HB])
        ss = P.sb("ss", [128, 2, 2])
        accO = [P.ps(f"accO{i}") for i in range(2)]
        accG = [P.ps(f"accG{i}") for i in range(2)]
        accP = [P.ps(f"accP{i}") for i in range(2)]
        TD, TE = P.ps("TD"), P.ps("TE")
        names = ("cst_in", "w_in", "wsT_mm", "wsT_ok", "sd_ok", "sr_ok", "vln_ok", "d_mm", "e_mm", "d_ev", "e_ev", "ed_ok", "ex_ok",
                 "mx_ok", "o_mm", "h2_ok", "h_ss", "hn_ok", "g_mm", "gb_ok", "sg_ok", "out_ok", "pl_mm", "lo_ok")
        m = {n: P.sem(n) for n in names}
        raw_in = [P.sem(f"raw_in{j}") for j in range(2)]
        w_hi, w_ok = P.sem("w_hi"), P.sem("w_ok")
        ldz = [P.sem(f"ldz{j}") for j in range(2)]
        ldh = [P.sem(f"ldh{j}") for j in range(4)]
        out = [P.sem(f"out{j}") for j in range(4)]
        NCST = 8
        order, idx = [], {}
        for t in range(-2, NX + 1):
            for kind, u in (("mix", t + 1), ("hn", t), ("pre", t + 2)):
                if 0 <= u < NX:
                    idx[(kind, u)] = len(order)
                    order.append((kind, u))
        ok = lambda t: 0 <= t < NX
        with nc.Block() as block:
            @block.sync
            def _(sp):
                for dst, src in ((ws[:, :, :], io["w_spatial"].rearrange("g t s -> t g s")), (tril[:, :], io["tril"]),
                                 (bs[:, :], io["b_spatial"]), (lg[:, :], bcast_rows(io["ln_v_g"], 512)),
                                 (lb[:, :], bcast_rows(io["ln_v_b"], 512)), (bg[:, :], bcast_rows(io["b_ple_gate"], D)),
                                 (gp[:, :], io["g_ple_T"]), (wp[:, :, :], io["w_ple_proj"].rearrange("(k p) n -> p k n", p=128))):
                    sp.dma_start(dst, src).then_inc(m["cst_in"], 16)

                def load(t):
                    rows = slice(t * 128, (t + 1) * 128)
                    if t >= 2:
                        sp.wait_ge(m["mx_ok"], t - 1)
                        sp.wait_ge(m["e_mm"], idx[("pre", t - 2)] + 1)
                    sp.dma_start(ob[t % 2][:, :, :], io["branch"][:, rows, :].rearrange("b p c -> p b c")).then_inc(ldz[t % 2], 16)
                    sp.dma_start(z[t % 2][:, :, :].rearrange("p a b -> p (a b)"), io["z2"][rows, 1536:WB]).then_inc(ldz[t % 2], 16)
                    sp.dma_start(pl[t % 2][:, :], io["p2"][rows, :]).then_inc(ldz[t % 2], 16)
                    if t >= 4:
                        sp.wait_ge(out[t % 4], 16 * (t // 4))
                    sp.dma_start(h[t % 4][:, :], io["xres"][rows, :]).then_inc(ldh[t % 4], 16)
                load(0)
                load(1)
                for k in range(KC):
                    if k >= 2:
                        sp.wait_ge(w_ok, k - 1)
                    sp.dma_start((sg, hn)[k % 2][:, :], io["w_out2"][k * 128:(k + 1) * 128, :]).then_inc(raw_in[k % 2], 16)
                sp.dma_start(wg[:, :, :], io["w_ple_gate"].rearrange("(k p) n -> p k n", p=128)).then_inc(m["w_in"], 16)
                for t in range(2, NX):
                    load(t)

            @block.gpsimd
            def _(pool):
                for k in range(KC):
                    pool.wait_ge(w_hi, k + 1)
                    nc.gpsimd.tensor_tensor(wo.lo[:, k, :], (sg, hn)[k % 2][:, :], wo.hi[:, k, :].bitcast(F32), ALU.subtract).then_inc(w_ok, 1)
                for t in range(-2, NX + 1):
                    if ok(t + 1):
                        pool.wait_ge(m["e_ev"], idx[("mix", t + 1)] + 1)
                        nc.gpsimd.tensor_tensor(mT.lo[:, 4:8, :], mTf[:, :, :], mT.hi[:, 4:8, :].bitcast(F32), ALU.subtract).then_inc(m["lo_ok"], 1)
                    if not ok(t - 1):
                        continue
                    t = t - 1
                    pool.wait_ge(m["out_ok"], t + 1)
                    pool.dma_start(io["out"][0, t * 128:(t + 1) * 128, :], h[t % 4][:, :]).then_inc(out[t % 4], 16)
                for j in range(4):
                    pool.wait_ge(out[j], 16 * (NX // 4))

            @block.tensor
            def _(pe):
                def banks_free(key):
                    n = idx[key] + 1
                    pe.wait_ge(m["d_ev"], n)
                    if n >= 2:
                        pe.wait_ge(m["e_ev"], n - 1)

                def spread(src, key):
                    banks_free(key)
                    for k in range(KC):
                        last = nc.tensor.transpose((TD if k < 4 else TE)[:, (k % 4) * 128:(k % 4 + 1) * 128],
                                                   src[:, k * 128:(k + 1) * 128], keep["ident"][:, :])
                        if k == 3:
                            last.then_inc(m["d_mm"], 1)
                    last.then_inc(m["e_mm"], 1)

                pe.wait_ge(m["cst_in"], 16 * NCST)
                for g in range(4):
                    last = nc.tensor.transpose(TD[:, g * 128:(g + 1) * 128], ws[:, g, :], keep["ident"][:, :])
                last.then_inc(m["wsT_mm"], 1)
                for t in range(-2, NX + 1):
                    if ok(t):
                        pe.wait_ge(m["w_in"], 16)
                        pe.wait_ge(w_ok, KC)
                        pe.wait_ge(m["d_ev"], idx[("mix", t)] + 2)
                        pe.wait_ge(m["lo_ok"], t + 1)
                        if t >= 1:
                            pe.wait_ge(m["h2_ok"], t)
                        for i in range(2):
                            for k in range(KC):
                                last = matmul3(nc, accO[i][:, :], mT[:, k, :], wo[:, k, i * 512:(i + 1) * 512], k == 0, k == KC - 1)
                        last.then_inc(m["o_mm"], 1)
                    if ok(t + 1):
                        pe.wait_ge(m["mx_ok"], t + 2)
                        spread(mx[(t + 1) % 2], ("mix", t + 1))
                    if ok(t - 1):
                        u = t - 1
                        pe.wait_ge(m["d_ev"], idx[("hn", u)] + 2)
                        pe.wait_ge(m["e_ev"], idx[("hn", u)] + 1)
                        if u >= 1:
                            pe.wait_ge(m["out_ok"], u)
                        for i in range(2):
                            for k in range(KC):
                                last = nc.tensor.matmul(accG[i][:, :], hT[:, k, :], wg[:, k, i * 512:(i + 1) * 512],
                                                        start=(k == 0), stop=(k == KC - 1))
                        last.then_inc(m["g_mm"], 1)
                        for i in range(2):
                            for k in range(2):
                                last = nc.tensor.matmul(accP[i][:, :], plT[u % 4][:, k, :], wp[:, k, i * 512:(i + 1) * 512],
                                                        start=(k == 0), stop=(k == 1))
                        last.then_inc(m["pl_mm"], 1)
                    if ok(t):
                        pe.wait_ge(m["hn_ok"], t + 1)
                        spread(hn, ("hn", t))
                    if ok(t + 2):
                        u = t + 2
                        banks_free(("pre", u))
                        pe.wait_ge(m["vln_ok"], u + 1)
                        for g in range(4):
                            last = nc.tensor.matmul(TD[:, g * 128:(g + 1) * 128], wsT[:, g, :], z[u % 2][:, 3, g * 128:(g + 1) * 128],
                                                    start=True, stop=True)
                        last.then_inc(m["d_mm"], 1)
                        for k in range(2):
                            last = nc.tensor.transpose(TE[:, k * 128:(k + 1) * 128], pl[u % 2][:, k * 128:(k + 1) * 128], keep["ident"][:, :])
                        last.then_inc(m["e_mm"], 1)

            @block.vector
            def _(dve):
                vec = nc.vector

                def layernorm(u):
                    v = z[u % 2][:, 3, :]
                    dve.wait_ge(ldz[u % 2], 48 * (u // 2 + 1))
                    vec.bn_stats(bn[:, :], v)
                    dve.drain()
                    vec.bn_aggr(mv[:, u % 2, 0:2], bn[:, :])
                    dve.drain().then_inc(m["sd_ok"], 1)
                    dve.wait_ge(m["sr_ok"], u + 1)
                    vec.reciprocal(mv[:, u % 2, 3:4], mv[:, u % 2, 2:3])
                    dve.drain()
                    vec.tensor_scalar(v, v, mv[:, u % 2, 0:1], mv[:, u % 2, 3:4], ALU.subtract, ALU.mult)
                    dve.drain()
                    vec.tensor_tensor(v, v, lg[:, :], ALU.mult)
                    dve.drain()
                    vec.tensor_tensor(v, v, lb[:, :], ALU.add).then_inc(m["vln_ok"], 1)

                def combine(u):
                    b, mo = ob[u % 2], mx[u % 2]
                    mb, den = b[:, :, 512:520], b[:, :, 520:528]
                    vec.tensor_tensor(sm[:, 0, 0, :], mb[:, 0, :], mb[:, 1, :], ALU.max)
                    dve.drain()
                    vec.tensor_tensor(sm[:, 0, 0, :], sm[:, 0, 0, :], mb[:, 2, :], ALU.max)
                    dve.drain()
                    vec.tensor_tensor(sm[:, 1, :, :], mb, sm[:, 0, 0, None, :].to_broadcast([128, 3, HB]), ALU.subtract).then_inc(m["ed_ok"], 1)
                    dve.wait_ge(m["ex_ok"], u + 1)
                    vec.tensor_tensor(sm[:, 3, :, :], sm[:, 2, :, :], den, ALU.mult)
                    dve.drain()
                    vec.tensor_tensor(sm[:, 4, 0, :], sm[:, 3, 0, :], sm[:, 3, 1, :], ALU.add)
                    dve.drain()
                    vec.tensor_tensor(sm[:, 4, 0, :], sm[:, 4, 0, :], sm[:, 3, 2, :], ALU.add)
                    dve.drain()
                    vec.reciprocal(sm[:, 4, 1, :], sm[:, 4, 0, :])
                    dve.drain()
                    vec.tensor_tensor(sm[:, 5, :, :], sm[:, 2, :, :], sm[:, 4, 1, None, :].to_broadcast([128, 3, HB]), ALU.mult)
                    dve.drain()
                    for br in range(3):
                        ov = b[:, br, 0:512].rearrange("p (h d) -> p h d", d=HD)
                        vec.tensor_tensor(ov, ov, sm[:, 5, br, :, None].to_broadcast([128, HB, HD]), ALU.mult)
                    dve.drain()
                    vec.tensor_tensor(b[:, 0, 0:512], b[:, 0, 0:512], b[:, 1, 0:512], ALU.add)
                    dve.drain()
                    vec.tensor_tensor(b[:, 0, 0:512], b[:, 0, 0:512], b[:, 2, 0:512], ALU.add)
                    dve.drain()
                    if u >= 2:
                        dve.wait_ge(m["e_mm"], idx[("mix", u - 2)] + 1)
                    vec.tensor_tensor(mo[:, 0:512], b[:, 0, 0:512], z[u % 2][:, 0, :], ALU.mult)
                    dve.wait_ge(m["d_mm"], idx[("pre", u)] + 1)
                    for g in range(4):
                        c = slice(g * 128, (g + 1) * 128)
                        last = vec.scalar_tensor_tensor(mo[:, 512 + g * 128:640 + g * 128], TD[:, c], bs[:, g:g + 1], z[u % 2][:, 2, c], ALU.add, ALU.mult)
                    last.then_inc(m["d_ev"], 1)
                    dve.drain()
                    vec.tensor_tensor(mo[:, 512:1024], mo[:, 512:1024], z[u % 2][:, 1, :], ALU.mult).then_inc(m["mx_ok"], 1)
                    dve.drain()

                dve.wait_ge(m["wsT_mm"], 1)
                vec.tensor_tensor(wsT[:, :, :], TD[:, :].rearrange("p (a b) -> p a b", b=128),
                                  tril[:, None, :].to_broadcast([128, 4, 128]), ALU.mult).then_inc(m["d_ev"], 1)
                for t in range(-2, NX + 1):
                    if ok(t):
                        dve.wait_ge(m["o_mm"], t + 1)
                        dve.wait_ge(ldh[t % 4], 16 * (t // 4 + 1))
                        for i in range(2):
                            c = slice(i * 512, (i + 1) * 512)
                            vec.tensor_tensor(h[t % 4][:, c], h[t % 4][:, c], accO[i][:, :], ALU.add)
                        dve.drain().then_inc(m["h2_ok"], 1)
                    if ok(t + 2):
                        layernorm(t + 2)
                    if ok(t):
                        dve.wait_ge(m["h_ss"], t + 1)
                        vec.reciprocal(ss[:, t % 2, 1:2], ss[:, t % 2, 1:2])
                        dve.drain()
                        if t >= 1:
                            dve.wait_ge(m["e_mm"], idx[("hn", t - 1)] + 1)
                        vec.tensor_scalar(hn[:, :], h[t % 4][:, :], ss[:, t % 2, 1:2], None, ALU.mult).then_inc(m["hn_ok"], 1)
                    if ok(t + 1):
                        dve.wait_ge(m["d_mm"], idx[("mix", t + 1)] + 1)
                        if t >= 0:
                            dve.wait_ge(m["o_mm"], t + 1)
                        src = TD[:, :].rearrange("p (a b) -> p a b", b=128)
                        vec.tensor_copy(mT.hi[:, 0:4, :], src)
                        dve.drain()
                        vec.tensor_tensor(mT.lo[:, 0:4, :], src, mT.hi[:, 0:4, :].bitcast(F32), ALU.subtract).then_inc(m["d_ev"], 1)
                    if ok(t - 1):
                        u = t - 1
                        dve.wait_ge(m["g_mm"], u + 1)
                        if u >= 1:
                            dve.drain()
                        for i in range(2):
                            c = slice(i * 512, (i + 1) * 512)
                            vec.tensor_tensor(sg[:, c], accG[i][:, :], bg[:, c], ALU.add)
                        dve.drain().then_inc(m["gb_ok"], 1)
                        dve.wait_ge(m["sg_ok"], u + 1)
                        dve.wait_ge(m["pl_mm"], u + 1)
                        for i in range(2):
                            c = slice(i * 512, (i + 1) * 512)
                            vec.tensor_tensor(sg[:, c], sg[:, c], accP[i][:, :], ALU.mult)
                        dve.drain()
                        vec.tensor_tensor(h[u % 4][:, :], h[u % 4][:, :], sg[:, :], ALU.add).then_inc(m["out_ok"], 1)
                    if ok(t):
                        dve.wait_ge(m["d_mm"], idx[("hn", t)] + 1)
                        for k in range(4):
                            last = vec.tensor_scalar(hT[:, k, :], TD[:, k * 128:(k + 1) * 128], gp[:, k:k + 1], None, ALU.mult)
                        last.then_inc(m["d_ev"], 1)
                    if ok(t + 2):
                        combine(t + 2)

            @block.scalar
            def _(act):
                for k in range(KC):
                    act.wait_ge(raw_in[k % 2], 16 * (k // 2 + 1))
                    act.activation(wo.hi[:, k, :], (sg, hn)[k % 2][:, :], ACT.Copy).then_inc(w_hi, 1)
                for t in range(-2, NX + 1):
                    if ok(t):
                        act.wait_ge(m["h2_ok"], t + 1)
                        act.activation(sg2[:, :], h[t % 4][:, :], ACT.Square, accum_out=ss[:, t % 2, 0:1])
                        act.drain()
                        act.activation(ss[:, t % 2, 1:2], ss[:, t % 2, 0:1], ACT.Sqrt, scale=1.0 / D, bias=keep["eps"][:, 0:1]).then_inc(m["h_ss"], 1)
                    if ok(t + 2):
                        u = t + 2
                        act.wait_ge(m["sd_ok"], u + 1)
                        act.activation(mv[:, u % 2, 2:3], mv[:, u % 2, 1:2], ACT.Sqrt, bias=keep["eps"][:, 0:1]).then_inc(m["sr_ok"], 1)
                    if ok(t + 1):
                        act.wait_ge(m["e_mm"], idx[("mix", t + 1)] + 1)
                        if t >= 0:
                            act.wait_ge(m["o_mm"], t + 1)
                            act.wait_ge(m["lo_ok"], t + 1)
                        act.activation(mT.hi[:, 4:8, :], TE[:, :].rearrange("p (a b) -> p a b", b=128), ACT.Copy)
                        act.activation(mTf[:, :, :], TE[:, :].rearrange("p (a b) -> p a b", b=128), ACT.Copy).then_inc(m["e_ev"], 1)
                    if ok(t - 1):
                        act.wait_ge(m["gb_ok"], t)
                        act.activation(sg[:, :], sg[:, :], ACT.Sigmoid).then_inc(m["sg_ok"], 1)
                    if ok(t):
                        act.wait_ge(m["e_mm"], idx[("hn", t)] + 1)
                        for k in range(4, KC):
                            last = act.activation(hT[:, k, :], TE[:, (k - 4) * 128:(k - 3) * 128], ACT.Copy, scale=gp[:, k:k + 1])
                        last.then_inc(m["e_ev"], 1)
                    if ok(t + 2):
                        u = t + 2
                        act.wait_ge(m["ed_ok"], u + 1)
                        act.activation(sm[:, 2, :, :], sm[:, 1, :, :], ACT.Exp).then_inc(m["ex_ok"], 1)
                        act.wait_ge(m["e_mm"], idx[("pre", u)] + 1)
                        if u >= 4:
                            act.wait_ge(m["pl_mm"], u - 3)
                        act.activation(plT[u % 4][:, :, :], TE[:, 0:256].rearrange("p (a b) -> p a b", b=128), ACT.Copy).then_inc(m["e_ev"], 1)


def second_block(nc, io, keep):
    with nc.cleanup_on_exit():
        hT = Split(nc.alloc_sbuf_tensor, "hT2", [128, KC, LX])
        gin = nc.alloc_sbuf_tensor("g_in", [128, KC], F32)
        with phase(nc, "gin") as P:
            got = P.sem("got")
            with nc.Block() as block:
                @block.sync
                def _(sp):
                    sp.dma_start(gin[:, :], io["g_in_T"]).then_inc(got, 16)
                    sp.wait_ge(got, 16)
        with phase(nc, "nt2") as P:
            norm_transpose(P, nc, io["xres"][0:LX, :], hT, keep["ident"], keep["eps"], [4] * 4,
                           lambda k, g: gin[:, k:k + 1], lambda k, g: 0.0, pre=(io["norm_f"], True))
        with phase(nc, "tz") as P:
            project_tm(P, nc, hT, lambda c: io["w_in2"][c, :, :, :],
                       lambda c, t: io["z2"][t * 128:(t + 1) * 128, c * 512:(c + 1) * 512],
                       512, [ACT.Copy] * 3 + [ACT.Silu] * 2 + [ACT.Gelu_apprx_tanh] * 2, NX)
    qk_phase(nc, io, keep)
    branch_phase(nc, io, keep)
    last_phase(nc, io, keep)

def first_layer(nc, l, io, keep):
    ada_phase(nc, l, io, keep)
    with nc.cleanup_on_exit():
        hT = Split(nc.alloc_sbuf_tensor, "hT", [128, KC, LT])
        with phase(nc, "nt") as P:
            norm_transpose(P, nc, io["xres"], hT, keep["ident"], keep["eps"], [4, 4, 4, 4, 2],
                           lambda k, g: keep["scale"][:, k, g // 4:g // 4 + 1],
                           lambda k, g: keep["shift"][:, k, g // 4:g // 4 + 1], copied=keep["copied"])
        with phase(nc, "cm") as P:
            project_cm(P, nc, hT, lambda c: io["w_cm"][bass.ds(l * CM + c, 1), :, :, :].rearrange("a p k m -> p (a k) m"),
                       lambda c: io["zcm"][bass.ds(c, 1), :, :].rearrange("a p t -> p (a t)"), CM)
        with phase(nc, "tg") as P:
            project_tm(P, nc, hT, lambda c: io["w_gate"][bass.ds(l * 2 + c, 1), :, :, :].rearrange("a p k m -> p (a k) m"),
                       lambda c, t: io["ztm"][t * 128:(t + 1) * 128, c * 512:(c + 1) * 512],
                       512, [ACT.Silu] * 2, NT)
        with phase(nc, "tv") as P:
            project_tm(P, nc, hT, lambda c: io["w_val"][bass.ds(l * 2 + c, 1), :, :, :].rearrange("a p k m -> p (a k) m"),
                       lambda c, t: io["ztm"][t * 128:(t + 1) * 128, 1024 + c * 384:1024 + (c + 1) * 384],
                       384, [ACT.Copy] * 2, NT)
    with phase(nc, "nain") as P:
        na = Neighbourhood(P)
        fourier_phase(nc, l, io, keep, na)
        neighbourhood_phase(nc, l, io, keep, na)
    gla_phase(nc, l, io, keep)
    out_phase(nc, l, io, keep)





def program(nc, io):
    keep = {
        "ident": nc.alloc_sbuf_tensor("ident", [128, 128], F32),
        "eps": nc.alloc_sbuf_tensor("eps", [128, 1], F32),
        "shift": nc.alloc_sbuf_tensor("shift", [128, KC, 2], F32),
        "scale": nc.alloc_sbuf_tensor("scale", [128, KC, 2], F32),
        "copied": nc.alloc_semaphore("copied"),
    }
    with phase(nc, "start") as P:
        ident_in, eps_ok = P.sem("ident_in"), P.sem("eps_ok")
        with nc.Block() as block:
            @block.sync
            def _(sp):
                sp.dma_start(keep["ident"][:, :], io["ident"]).then_inc(ident_in, 16)
                sp.dma_start(io["xres"][0:LX, :], io["x"]).then_inc(keep["copied"], 16)
                sp.dma_start(io["xres"][LX:LT, :], io["ctx"]).then_inc(keep["copied"], 16)
                sp.wait_ge(ident_in, 16)

            @block.vector
            def _(dve):
                nc.vector.memset(keep["eps"][:, :], EPS).then_inc(eps_ok, 1)
                dve.wait_ge(eps_ok, 1)
    with nc.Fori(0, DEPTH) as l:
        first_layer(nc, l, io, keep)
    second_block(nc, io, keep)





def laid_out(a):
    f = lambda n: np.ascontiguousarray(a[n])
    sizes = (256, 256, 384, 384, 384, 384, 192, 192, 384, 384, 16, 16)
    at = np.cumsum((0,) + sizes)
    w = f("w_in")
    fx, fg, nq, nk, nv, ng, gq, gk, gv, gg, zf, zb = (w[:, :, at[i]:at[i + 1]] for i in range(12))

    def heads_padded(t, n=GH):
        out = np.zeros(t.shape[:-1] + (n, 64), t.dtype)
        out[..., :GDK] = t.reshape(t.shape[:-1] + (n, GDK))
        return out.reshape(t.shape[:-1] + (n * 64,))

    gqz = heads_padded(gq)
    gqz[..., GDK:64], gqz[..., 64 + GDK:128] = zf, zb
    cm = np.concatenate([fx, nq, nk, gqz, heads_padded(gk)], -1)

    def chunks(t, m):
        L = t.shape[0]
        return np.ascontiguousarray(t.reshape(L, KC, 128, -1, m).transpose(0, 3, 2, 1, 4).reshape(-1, 128, KC, m))

    wa = np.zeros((DEPTH, 64, 256), np.float32)
    wa[:, 0:RANK] = heads_padded(f("w_alpha_fwd"))
    wa[:, 32:32 + RANK] = heads_padded(f("w_alpha_bwd"))
    ba = np.stack([heads_padded(f("b_alpha_fwd")), heads_padded(f("b_alpha_bwd"))], 1)
    ba = ba.reshape(DEPTH, 4, 128).transpose(0, 2, 1)
    w2 = f("w_in_2")[0]
    q2, k2, v2, gb2, u2, va2, ga2 = (w2[:, i * 512:(i + 1) * 512] for i in range(7))
    out = {
        "x": f("x")[0], "ctx": f("ctx")[0],
        "cT": np.stack([a["c"][0], a["c_ctx"]], -1).reshape(KC, 128, 2).transpose(1, 0, 2),
        "w_ada": f("w_ada"), "b_ada": f("b_ada"),
        "norm_wT": f("norm_w").reshape(DEPTH, KC, 128).transpose(0, 2, 1),
        "w_cm": chunks(cm, 128), "w_gate": chunks(np.concatenate([fg, ng, gg], -1), 512),
        "w_val": chunks(np.concatenate([nv, gv], -1), 384),
        "w_four": f("w_four").reshape(DEPTH, 2, 128, 256).transpose(0, 2, 1, 3),
        "rpb": f("rpb"), "w_alpha": wa, "b_alpha": ba, "gla_norm_w": f("gla_norm_w"),
        "w_out": f("w_out"), "norm_f": f("norm_f"),
        "p2": f("p_2")[0, 0], "positions": f("positions_2")[0].astype(np.int32).reshape(NX, 128).T,
        "g_in_T": f("g_in_2")[0].reshape(KC, 128).T,
        "w_in2": chunks(np.concatenate([q2, k2, v2, gb2, ga2, u2, va2], -1)[None], 512),
        "q_norm": f("q_norm_2")[0], "k_norm": f("k_norm_2")[0], "w_spatial": f("w_spatial_2")[0],
        "b_spatial": f("b_spatial_2")[0].T, "ln_v_g": f("ln_v_g_2")[0], "ln_v_b": f("ln_v_b_2")[0],
        "w_out2": f("w_out_2")[0], "g_ple_T": f("g_ple_2")[0].reshape(KC, 128).T,
        "w_ple_gate": f("w_ple_gate_2")[0], "b_ple_gate": f("b_ple_gate_2")[0], "w_ple_proj": f("w_ple_proj_2")[0],
    }
    out.update(shape_tables())
    return {n: np.ascontiguousarray(v) for n, v in out.items()}


def shape_tables():
    f8, f4 = np.float64, np.float32
    t = {"ident": np.eye(128, dtype=f4)}
    ang = 2 * np.pi * np.outer(np.arange(64), np.arange(64)) / 64
    bd = lambda m: np.kron(np.eye(4), m).astype(f4)
    ch = np.stack([bd(np.cos(ang) / 8), bd(np.sin(ang) / 8)])
    t["dft_ch"] = ch.reshape(2, 2, 128, 256).transpose(2, 0, 1, 3)
    tt = np.arange(LX).reshape(N1, N2)
    a1 = 2 * np.pi * tt[:, :, None] * np.arange(N1)[None, None, :] / LX
    s = LX ** -0.5
    t["dft_1"] = np.stack([np.cos(a1) * s, np.sin(a1) * s, -np.sin(a1) * s], 2).astype(f4)
    a2 = 2 * np.pi * np.outer(np.arange(N2), np.arange(N2)) / N2
    e = np.eye(8)
    k2 = lambda m: np.einsum("tk,ab->atkb", m, e).reshape(128, 128)
    t["dft_2"] = np.stack([k2(np.cos(a2)), k2(-np.sin(a2))], 1).astype(f4)
    a3 = 2 * np.pi * np.outer(np.arange(LC), np.arange(LC)) / LC
    d3 = np.stack([np.cos(a3), -np.sin(a3)]) * LC ** -0.5
    t["dft_ctx"] = d3.reshape(2, 2, 128, LC).transpose(2, 0, 1, 3).astype(f4)
    nf = GDK // 4
    inv = (np.float32(10000.0) ** (-np.arange(nf, dtype=f4) / nf)).astype(f4)
    pos = np.arange(LX)
    rows, cols = (pos // GRID).astype(f4), (pos % GRID).astype(f4)
    cs, sn, perm = np.zeros((128, LX)), np.zeros((128, LX)), np.zeros((128, 128))
    for h in range(2):
        for half, p in ((0, rows), (1, cols)):
            a = (p[None, :] * inv[:, None]).astype(f4).astype(f8)
            b = 64 * h + 24 * half
            for o in range(2):
                cs[b + nf * o:b + nf * o + nf], sn[b + nf * o:b + nf * o + nf] = np.cos(a), np.sin(a)
            for n in range(nf):
                perm[b + nf + n, b + n] = -1.0
                perm[b + n, b + nf + n] = 1.0
    t["rope_cs"] = np.stack([cs, sn], 1).astype(f4)
    t["rope_perm"] = perm.astype(f4)
    t["chunk_start"] = np.tile((np.arange(LT) % CH != 0).astype(f4), (128, 1))
    s_, t_ = np.arange(128)[:, None], np.arange(128)[None, :]
    same = (s_ // CH) == (t_ // CH)
    t["gla_mask"] = np.stack([same & (s_ <= t_), same & (s_ >= t_)], 1).astype(np.int32)
    cq = np.arange(GRID)
    st = np.clip(cq - KW // 2, 0, GRID - KW)
    inside = (cq[None, :] >= st[:, None]) & (cq[None, :] < st[:, None] + KW)
    t["col_mask"] = np.tile(np.where(inside, 0.0, NEGBIG).astype(f4), (2, 1))
    dist = (np.arange(128)[:, None] + 128) - np.arange(256)[None, :]
    t["band"] = np.where((dist >= 0) & (dist <= 128), 0.0, NEGBIG).astype(f4)
    t["inv_freq"] = np.exp(-math.log(10000.0) * np.arange(32, dtype=f4) / 32).astype(f4)
    t["tril"] = np.tril(np.ones((128, 128), f4)).T.copy()
    return t


def build(nc, arrays, debug=()):
    io = {n: nc.dram_tensor(f"in_{n}", v.shape, mybir.dt.from_np(v.dtype), kind="ExternalInput").ap()
          for n, v in arrays.items()}
    scratch = {"xres": [LT, D], "gates": [2, D], "zcm": [CM, 128, LT], "ztm": [LT, TM], "mix": [LT, D],
               "four_y": [N1 * N2, 512], "rpb_pad": [NA_H * 15, 64, 128], "z2": [LX, WB], "branch": [3, LX, ORW]}
    for n, s in scratch.items():
        io[n] = nc.dram_tensor(f"scr_{n}", s, F32, kind="ExternalOutput" if n in debug else "Internal").ap()
    io["out"] = nc.dram_tensor("out_0", [1, LX, D], F32, kind="ExternalOutput").ap()
    program(nc, io)


def kernel(**inputs):
    from concourse.bass_utils import run_bass_kernel_spmd
    import concourse.bacc as bacc
    arrays = laid_out(inputs)
    nc = bacc.Bacc("TRN2", target_bir_lowering=False, num_devices=1)
    build(nc, arrays)
    r = run_bass_kernel_spmd(nc, [{f"in_{n}": v for n, v in arrays.items()}], core_ids=[0])
    return r.results[0]["out_0"]
```

```python
import math
import numpy as np
import concourse.bass as bass
from concourse import mybir
from contextlib import contextmanager

F32 = mybir.dt.float32
F32R = mybir.dt.float32r
I32 = mybir.dt.int32
ALU = mybir.AluOpType
ACT = mybir.ActivationFunctionType
AX = mybir.AxisListType

D = 1024
KC = D // 128
LX, LC = 2048, 256
LT = LX + LC
NT = LT // 128
NX = LX // 128
DEPTH = 2
EPS = 1e-6
D_FOUR, D_NA, D_GK, D_GV = 256, 384, 192, 384
NA_H, NA_D = 6, 64
GRID = 64
ROWS = LX // GRID
KH, KW = 8, 16
GH, GDK, GDV, RANK, CH = 4, 48, 96, 16, 64
NCH = LT // CH
CM = 12
TM = 1024 + D_NA + D_GV
HB, HD = 8, 64
WB = 3584
N1, N2 = 128, 16
ORW = 512 + 2 * HB
NEGBIG = -1e30
LOWEST = -3e38


class Phase:

    def __init__(self, nc, name):
        self.nc, self.name = nc, name

    def sb(self, name, shape, dt=F32):
        return self.nc.alloc_sbuf_tensor(f"{self.name}_{name}", list(shape), dt)

    def ps(self, name, shape=(128, 512)):
        return self.nc.alloc_psum_tensor(f"{self.name}_{name}", list(shape), F32)

    def sem(self, name):
        return self.nc.alloc_semaphore(f"{self.name}_{name}")


class Split:

    def __init__(self, alloc, name, shape):
        self.hi, self.lo = alloc(f"{name}_hi", shape, F32R), alloc(f"{name}_lo", shape, F32R)

    def __getitem__(self, key):
        return self.hi[key], self.lo[key]


def matmul3(nc, out, lhsT, rhs, start, stop):
    (ah, al), (bh, bl) = lhsT, rhs
    nc.tensor.matmul(out, ah, bh, start=start, stop=False)
    nc.tensor.matmul(out, ah, bl, start=False, stop=False)
    return nc.tensor.matmul(out, al, bh, start=False, stop=stop)


@contextmanager
def phase(nc, name):
    with nc.cleanup_on_exit():
        yield Phase(nc, name)


def bcast_rows(row_ap, n, parts=128):
    return row_ap.rearrange("(a n) -> a n", a=1).to_broadcast([parts, n])


def ada_phase(nc, l, io, keep):
    with phase(nc, "ada") as P:
        cs = P.sb("cs", [128, KC, 2])
        wk = [P.sb(f"w{k}", [128, 3 * D]) for k in range(KC)]
        brow = P.sb("brow", [2, 3 * D])
        arow = P.sb("arow", [2, 3 * D])
        nw = P.sb("nw", [128, KC])
        acc = [P.ps(f"acc{n}") for n in range(6)]
        tp = P.ps("tp")
        w_in = [P.sem(f"w_in{k}") for k in range(KC)]
        c_in, b_in, c_ok, rows_ok, cols_ok, mm_ok, gate_out = [P.sem(s) for s in (
            "c_in", "b_in", "c_ok", "rows_ok", "cols_ok", "mm_ok", "gate_out")]
        wv = io["w_ada"].rearrange("l (k p) n -> l k p n", p=128)
        with nc.Block() as block:
            @block.sync
            def _(sp):
                sp.dma_start(cs[:, :, :], io["cT"]).then_inc(c_in, 16)
                for k in range(KC):
                    sp.dma_start(wk[k][:, :], wv[bass.ds(l, 1), k, :, :].rearrange("a p n -> p (a n)")).then_inc(w_in[k], 16)
                for r in range(2):
                    sp.dma_start(brow[r:r + 1, :], io["b_ada"][bass.ds(l, 1), :]).then_inc(b_in, 16)
                sp.dma_start(nw[:, :], io["norm_wT"][bass.ds(l, 1), :, :].rearrange("a p k -> p (a k)")).then_inc(b_in, 16)
                sp.wait_ge(rows_ok, 1)
                sp.dma_start(io["gates"], arow[:, 2 * D:3 * D]).then_inc(gate_out, 16)
                sp.wait_ge(gate_out, 16)

            @block.scalar
            def _(act):
                act.wait_ge(c_in, 16)
                act.activation(cs[:, :, :], cs[:, :, :], ACT.Silu).then_inc(c_ok, 1)

            @block.tensor
            def _(pe):
                pe.wait_ge(c_ok, 1)
                for k in range(KC):
                    pe.wait_ge(w_in[k], 16)
                    for n in range(6):
                        last = nc.tensor.matmul(acc[n][0:2, :], cs[:, k, :], wk[k][:, n * 512:(n + 1) * 512],
                                                start=(k == 0), stop=(k == KC - 1))
                last.then_inc(mm_ok, 1)
                pe.wait_ge(rows_ok, 1)
                for j in range(2 * KC):
                    last = nc.tensor.transpose(tp[:, 2 * j:2 * j + 2], arow[:, j * 128:(j + 1) * 128],
                                               keep["ident"][0:2, 0:2])
                last.then_inc(cols_ok, 1)

            @block.vector
            def _(dve):
                dve.wait_ge(mm_ok, 1)
                dve.wait_ge(b_in, 48)
                for n in range(6):
                    nc.vector.tensor_tensor(arow[:, n * 512:(n + 1) * 512], acc[n][0:2, :],
                                            brow[:, n * 512:(n + 1) * 512], ALU.add)
                dve.drain()
                nc.vector.tensor_scalar(arow[:, D:2 * D], arow[:, D:2 * D], 1.0, None, ALU.add).then_inc(rows_ok, 1)
                dve.wait_ge(cols_ok, 1)
                nc.vector.tensor_copy(keep["shift"][:, :, :], tp[:, 0:16].rearrange("p (k s) -> p k s", s=2))
                for s in range(2):
                    nc.vector.tensor_tensor(keep["scale"][:, :, s], tp[:, 16 + s:32:2], nw[:, :], ALU.mult)


def norm_transpose(P, nc, src, hT, ident, eps, groups, scale_of, shift_of, pre=None, copied=None):
    G = len(groups)
    xb = [P.sb(f"xb{j}", [128, 4, D]) for j in range(3)]
    sq = P.sb("sq", [128, D])
    ss = P.sb("ss", [128, 2, 8])
    if pre:
        wrow = P.sb("wrow", [128, D])
    tm = [P.sb(f"tm{b}", [128, 512]) for b in range(4)]
    tp = [P.ps(f"ntp{b}") for b in range(4)]
    x_in = [P.sem(f"x_in{j}") for j in range(3)]
    hi_ok = [P.sem("hi_dve"), P.sem("hi_act")]
    lo_ok = P.sem("lo_ok")
    x_free, ss_ok, xn_ok, tp_ok, ev_dve, ev_act, pre_ok, pre_out, w_in = [P.sem(s) for s in (
        "x_free", "ss_ok", "xn_ok", "tp_ok", "ev_dve", "ev_act", "pre_ok", "pre_out", "wrow_in")]
    stats = 2 if pre else 1

    def lo_taken(eng, g, k):
        g, k = (g, k - 4) if k >= 4 else (g - 1, k + 4)
        if g >= 0:
            eng.wait_ge(lo_ok, 6 * g + k - k // 4)
    rows = src.rearrange("(t p) d -> p t d", p=128)
    with nc.Block() as block:
        @block.sync
        def _(sp):
            if copied:
                sp.wait_ge(copied, 32)
            if pre:
                sp.dma_start(wrow[:, :], bcast_rows(pre[0], D)).then_inc(w_in, 16)
            for g, n in enumerate(groups):
                if g >= 3:
                    sp.wait_ge(x_free, g - 2)
                    if pre:
                        sp.wait_ge(pre_out, 16 * (g - 2))
                sp.dma_start(xb[g % 3][:, 0:n, :], rows[:, 4 * g:4 * g + n, :]).then_inc(x_in[g % 3], 16)

        @block.gpsimd
        def _(pool):
            for g in range(G + 1):
                if pre and g < G:
                    n = groups[g]
                    pool.wait_ge(pre_ok, g + 1)
                    pool.dma_start(rows[:, 4 * g:4 * g + n, :], xb[g % 3][:, 0:n, :]).then_inc(pre_out, 16)
                    pool.wait_ge(pre_out, 16 * (g + 1))
                if g >= 1:
                    n = groups[g - 1]
                    for k in (1, 2, 3, 5, 6, 7):
                        c = slice(512 * (g - 1), 512 * (g - 1) + 128 * n)
                        pool.wait_ge(hi_ok[k % 2], (KC * (g - 1) + k) // 2 + 1)
                        nc.gpsimd.tensor_tensor(hT.lo[:, k, c], tm[k % 4][:, 0:128 * n], hT.hi[:, k, c].bitcast(F32),
                                                ALU.subtract).then_inc(lo_ok, 1)

        def act_evac(act, g):
            n = groups[g]
            for k in range(1, KC, 2):
                act.wait_ge(tp_ok, KC * g + k + 1)
                lo_taken(act, g, k)
                act.activation(tm[k % 4][:, 0:128 * n], tp[k % 4][:, 0:128 * n], ACT.Identity,
                               scale=scale_of(k, g), bias=shift_of(k, g))
                act.drain().then_inc(ev_act, 1)
                act.activation(hT.hi[:, k, 512 * g:512 * g + 128 * n], tm[k % 4][:, 0:128 * n], ACT.Copy).then_inc(hi_ok[1], 1)

        @block.scalar
        def _(act):
            for g, n in enumerate(groups):
                for s in range(stats):
                    if s == 0:
                        act.wait_ge(x_in[g % 3], 16 * (g // 3 + 1))
                    else:
                        act.wait_ge(pre_ok, g + 1)
                    for t in range(n):
                        act.activation(sq[:, :], xb[g % 3][:, t, :], ACT.Square, accum_out=ss[:, g % 2, t:t + 1])
                        act.drain()
                    act.activation(ss[:, g % 2, 4:4 + n], ss[:, g % 2, 0:n], ACT.Sqrt,
                                   scale=1.0 / D, bias=eps[:, 0:1]).then_inc(ss_ok, 1)
                if g >= 1:
                    act_evac(act, g - 1)
            act_evac(act, G - 1)

        @block.vector
        def _(dve):
            def norm(g, s):
                n = groups[g]
                dve.wait_ge(ss_ok, stats * g + s + 1)
                nc.vector.reciprocal(ss[:, g % 2, 4:4 + n], ss[:, g % 2, 4:4 + n])
                dve.drain()
                for t in range(n):
                    if s < stats - 1:
                        if g == 0 and t == 0:
                            dve.wait_ge(w_in, 16)
                        last = nc.vector.scalar_tensor_tensor(xb[g % 3][:, t, :], xb[g % 3][:, t, :],
                                                              ss[:, g % 2, 4 + t:5 + t], wrow[:, :], ALU.mult, ALU.mult)
                    else:
                        if pre and t == 0:
                            dve.wait_ge(pre_out, 16 * (g + 1))
                        last = nc.vector.tensor_scalar(xb[g % 3][:, t, :], xb[g % 3][:, t, :],
                                                       ss[:, g % 2, 4 + t:5 + t], None, ALU.mult)
                last.then_inc(xn_ok if s == stats - 1 else pre_ok, 1)

            def evac(g):
                n = groups[g]
                for k in range(0, KC, 2):
                    dve.wait_ge(tp_ok, KC * g + k + 1)
                    if k % 4:
                        lo_taken(dve, g, k)
                    nc.vector.tensor_scalar(tm[k % 4][:, 0:128 * n], tp[k % 4][:, 0:128 * n],
                                            scale_of(k, g), shift_of(k, g), ALU.mult, ALU.add)
                    dve.drain().then_inc(ev_dve, 1)
                    c = slice(512 * g, 512 * g + 128 * n)
                    nc.vector.tensor_copy(hT.hi[:, k, c], tm[k % 4][:, 0:128 * n]).then_inc(hi_ok[0], 1)
                    if k % 4 == 0:
                        dve.drain()
                        nc.vector.tensor_tensor(hT.lo[:, k, c], tm[0][:, 0:128 * n], hT.hi[:, k, c].bitcast(F32), ALU.subtract)
                        dve.drain()

            for g in range(G):
                for s in range(stats):
                    norm(g, s)
                if g >= 1:
                    evac(g - 1)
            evac(G - 1)

        @block.tensor
        def _(pe):
            for g, n in enumerate(groups):
                pe.wait_ge(xn_ok, g + 1)
                for k in range(KC):
                    e = (KC * g + k) // 2
                    if e >= 2:
                        pe.wait_ge(ev_act if k % 2 else ev_dve, e - 1)
                    for t in range(n):
                        last = nc.tensor.transpose(tp[k % 4][:, t * 128:(t + 1) * 128],
                                                   xb[g % 3][:, t, k * 128:(k + 1) * 128], ident[:, :])
                    last.then_inc(tp_ok, 1)
                nc.tensor.drain().then_inc(x_free, 1)


def project_cm(P, nc, hT, w, dst, n_chunks):
    TT = [(i * 512, min(512, LT - i * 512)) for i in range((LT + 511) // 512)]
    raw = [P.sb(f"raw{j}", [128, KC, 128]) for j in range(2)]
    wb = [Split(P.sb, f"wb{j}", [128, KC, 128]) for j in range(2)]
    zo = [P.sb(f"zo{j}", [128, LT]) for j in range(2)]
    acc = [P.ps(f"acc{b}") for b in range(len(TT))]
    w_in = [P.sem(f"w_in{j}") for j in range(2)]
    z_out = [P.sem(f"z_out{j}") for j in range(2)]
    mm_ok, ev_dve, ev_act, w_ok = [P.sem(s) for s in ("mm_ok", "ev_dve", "ev_act", "w_ok")]
    nD, nA = (len(TT) + 1) // 2, len(TT) // 2
    pairs = (n_chunks - 1) // 2

    def both(eng, body):
        with eng.Fori(0, pairs) as i:
            for j in range(2):
                body(i, j)
        for j in range(n_chunks - 2 * pairs):
            body(pairs, j)

    with nc.Block() as block:
        @block.sync
        def _(sp):
            for j in range(2):
                sp.sem_inc(z_out[j], 1)

            def load(c, j):
                src = w(c)
                sp.wait_ge(w_ok, c)
                sp.dma_start(raw[j][:, :, :], src).then_inc(w_in[j], 16)

            def body(i, j):
                c = 2 * i + j
                if not isinstance(c, int) or c + 1 < n_chunks:
                    load(c + 1, 1 - j)
                out = dst(c)
                sp.wait_ge(ev_dve, nD * (c + 1) + nD)
                sp.wait_ge(ev_act, nA * (c + 1) + nA)
                sp.dma_start(out, zo[j][:, :]).then_inc(z_out[j], 16)

            sp.dma_start(raw[0][:, :, :], w(0)).then_inc(w_in[0], 16)
            both(sp, body)
            for j in range(2):
                sp.wait_ge(z_out[j], 16 * ((n_chunks + 1 - j) // 2) + 1)

        @block.tensor
        def _(pe):
            pe.drain().then_inc(mm_ok, 2 * len(TT))
            def body(i, j):
                c = 2 * i + j
                pe.wait_ge(w_ok, c + 2)
                for n, (t0, tn) in enumerate(TT):
                    own, e = (ev_act, nA * c + n // 2) if n % 2 else (ev_dve, nD * c + n // 2)
                    pe.wait_ge(own, e + 1)
                    for k in range(KC):
                        last = matmul3(nc, acc[n][:, 0:tn], wb[j][:, k, :], hT[:, k, t0:t0 + tn], k == 0, k == KC - 1)
                    last.then_inc(mm_ok, 1)
            both(pe, body)

        @block.vector
        def _(dve):
            dve.drain().then_inc(ev_dve, nD)
            dve.drain().then_inc(w_ok, 1)

            def split(c, i, j):
                dve.wait_ge(w_in[j], 16 * i + 16)
                dve.wait_ge(mm_ok, len(TT) * (c + 1))
                nc.vector.tensor_copy(wb[j].hi[:, :, :], raw[j][:, :, :])
                dve.drain()
                nc.vector.tensor_tensor(wb[j].lo[:, :, :], raw[j][:, :, :], wb[j].hi[:, :, :].bitcast(F32), ALU.subtract).then_inc(w_ok, 1)

            split(0, 0, 0)

            def body(i, j):
                c = 2 * i + j
                if not isinstance(c, int) or c + 1 < n_chunks:
                    split(c + 1, i + j, 1 - j)
                dve.wait_ge(z_out[j], 16 * i + 1)
                for n, (t0, tn) in enumerate(TT):
                    if n % 2 == 0:
                        dve.wait_ge(mm_ok, len(TT) * (c + 2) + n + 1)
                        nc.vector.tensor_copy(zo[j][:, t0:t0 + tn], acc[n][:, 0:tn]).then_inc(ev_dve, 1)
            both(dve, body)

        @block.scalar
        def _(act):
            act.drain().then_inc(ev_act, nA)
            def body(i, j):
                c = 2 * i + j
                act.wait_ge(z_out[j], 16 * i + 1)
                for n, (t0, tn) in enumerate(TT):
                    if n % 2:
                        act.wait_ge(mm_ok, len(TT) * (c + 2) + n + 1)
                        act.activation(zo[j][:, t0:t0 + tn], acc[n][:, 0:tn], ACT.Copy).then_inc(ev_act, 1)
            both(act, body)


def project_tm(P, nc, hT, w, dst, widths, funcs, tiles, heads=None):
    n_chunks, width = len(funcs), max(widths)
    raw = P.sb("traw", [128, KC, width])
    wb = Split(P.sb, "tw", [128, KC, width])
    zo = [P.sb(f"tz{j}", [128, width]) for j in range(3)]
    acc = [P.ps(f"tacc{b}") for b in range(3)]
    w_in, k_used = P.sem("tw_in"), P.sem("k_used")
    hi_ok, lo_dve, lo_pool = P.sem("hi_ok"), P.sem("lo_dve"), P.sem("lo_pool")
    z_out = [P.sem(f"tz_out{j}") for j in range(3)]
    units = {n: u for u, n in enumerate(c * tiles + t for c in range(n_chunks) if funcs[c] is None for t in range(tiles))}
    mm_ok, ev = [P.sem(s) for s in ("tmm_ok", "tev")]
    with nc.Block() as block:
        @block.sync
        def _(sp):
            if heads:
                heads.load(sp)

            def load(c):
                if c >= 1:
                    sp.wait_ge(lo_dve, KC // 2 * c)
                    sp.wait_ge(lo_pool, KC // 2 * c)
                sp.dma_start(raw[:, :, 0:widths[c]], w(c)).then_inc(w_in, 16)
            load(0)
            for c in range(n_chunks):
                if c + 1 < n_chunks:
                    load(c + 1)
                for t in range(tiles):
                    n = c * tiles + t
                    if n in units:
                        heads.finished(sp, units[n])
                    else:
                        sp.wait_ge(ev, n + 1)
                    sp.dma_start(dst(c, t), zo[n % 3][:, 0:widths[c]]).then_inc(z_out[n % 3], 16)
            total = n_chunks * tiles
            for j in range(3):
                sp.wait_ge(z_out[j], 16 * ((total + 2 - j) // 3))

        @block.tensor
        def _(pe):
            for c in range(n_chunks):
                for t in range(tiles):
                    n = c * tiles + t
                    if n >= 3:
                        pe.wait_ge(ev, n - 2)
                    for k in range(KC):
                        if t == 0:
                            pe.wait_ge(lo_pool if k % 2 else lo_dve, KC // 2 * c + k // 2 + 1)
                        last = matmul3(nc, acc[n % 3][:, 0:widths[c]], hT[:, k, t * 128:(t + 1) * 128], wb[:, k, 0:widths[c]], k == 0, k == KC - 1)
                        if t == tiles - 1:
                            last.then_inc(k_used, 1)
                    pe.drain().then_inc(mm_ok, 1) if t == tiles - 1 else last.then_inc(mm_ok, 1)

        @block.vector
        def _(dve):
            def split(c):
                dve.wait_ge(w_in, 16 * (c + 1))
                for k in range(KC):
                    if c >= 1:
                        dve.wait_ge(k_used, KC * (c - 1) + k + 1)
                    s = slice(0, widths[c])
                    nc.vector.tensor_copy(wb.hi[:, k, s], raw[:, k, s])
                    dve.drain().then_inc(hi_ok, 1)
                    if k % 2 == 0:
                        nc.vector.tensor_tensor(wb.lo[:, k, s], raw[:, k, s], wb.hi[:, k, s].bitcast(F32), ALU.subtract).then_inc(lo_dve, 1)

            split(0)
            if heads:
                heads.tables_dve(dve)
            for c in range(n_chunks):
                for t in range(tiles):
                    if t == tiles - 1 and c + 1 < n_chunks:
                        split(c + 1)
                    n = c * tiles + t
                    if n in units:
                        heads.dve(dve, units[n], acc[n % 3], zo[n % 3], ev, z_out[n % 3], 16 * (n // 3))

        @block.gpsimd
        def _(pool):
            def split(c):
                for k in range(1, KC, 2):
                    pool.wait_ge(hi_ok, KC * c + k + 1)
                    s = slice(0, widths[c])
                    nc.gpsimd.tensor_tensor(wb.lo[:, k, s], raw[:, k, s], wb.hi[:, k, s].bitcast(F32), ALU.subtract).then_inc(lo_pool, 1)

            split(0)
            for c in range(n_chunks):
                for t in range(tiles):
                    if t == tiles - 1 and c + 1 < n_chunks:
                        split(c + 1)
                    n = c * tiles + t
                    if n in units:
                        heads.pool(pool, units[n], zo[n % 3], z_out[n % 3], 16 * (n // 3))

        @block.scalar
        def _(act):
            if heads:
                heads.tables_act(act)
            for c in range(n_chunks):
                for t in range(tiles):
                    n = c * tiles + t
                    act.wait_ge(mm_ok, n + 1)
                    if n in units:
                        heads.act(act, units[n], acc[n % 3])
                        continue
                    if n >= 3:
                        act.wait_ge(z_out[n % 3], 16 * (n // 3))
                    act.activation(zo[n % 3][:, 0:widths[c]], acc[n % 3][:, 0:widths[c]], funcs[c]).then_inc(ev, 1)

class Neighbourhood:

    def __init__(self, P):
        self.q = P.sb("q", [128, 3, LT])
        self.kk = P.sb("k", [128, 3, LT])
        self.t2 = P.sb("t2", [128, NA_H, 15, GRID])
        self.ti = P.sb("ti", [128, NA_H, 9, GRID])
        self.cmask = P.sb("cmask", [128, GRID])
        self.pad = P.sb("pad", [90, 128])
        self.q_in, self.k_in, self.pad_ok, self.pad_in, self.pad_out, self.t_in, self.z_ok = [P.sem(s) for s in (
            "q_in", "k_in", "pad_ok", "pad_in", "pad_out", "t_in", "tz_ok")]

    def load(self, eng, l, io):
        eng.dma_start(self.cmask[:, :], io["col_mask"]).then_inc(self.pad_in, 16)
        eng.wait_ge(self.pad_ok, 1)
        eng.dma_start(self.pad[:, 48:79], io["rpb"][bass.ds(l, 1), :, :, :].rearrange("a h r c -> (a h r) c")).then_inc(self.pad_in, 16)
        eng.wait_ge(self.pad_in, 32)
        eng.dma_start(io["rpb_pad"], self.pad[:, None, :].to_broadcast([90, 64, 128])).then_inc(self.pad_out, 16)
        eng.wait_ge(self.pad_out, 16)
        for s in range(2):
            for h in range(NA_H):
                base = io["rpb_pad"][h * 15:h * 15 + 15 - s, 0, 0:GRID]
                diag = bass.AP(base.tensor, base.offset + 63, [[127, 64], [64 * 128, 15 - s], [1, GRID]])
                eng.dma_start(self.t2[64 * s:64 * s + 64, h, s:15, :], diag).then_inc(self.t_in, 16)
        eng.dma_start(self.q[:, :, :], io["zcm"][2:5, :, :].rearrange("c p t -> p c t")).then_inc(self.q_in, 16)
        eng.dma_start(self.kk[:, :, :], io["zcm"][5:8, :, :].rearrange("c p t -> p c t")).then_inc(self.k_in, 16)

    def clear(self, nc, pool):
        nc.gpsimd.memset(self.pad[:, :], 0.0).then_inc(self.pad_ok, 1)
        pool.wait_ge(self.pad_ok, 1)
        nc.gpsimd.memset(self.t2[64:128, :, 0, :], 0.0).then_inc(self.z_ok, 1)

    def scale(self, nc, pool):
        pool.wait_ge(self.z_ok, 1)
        pool.wait_ge(self.q_in, 16)
        for c in range(3):
            nc.gpsimd.tensor_scalar(self.q[:, c, :], self.q[:, c, :], NA_D ** -0.5, None, ALU.mult)

    def bias(self, nc, dve):
        t2, ti = self.t2, self.ti
        dve.wait_ge(self.t_in, 16 * 12)
        dve.wait_ge(self.z_ok, 1)
        dve.wait_ge(self.pad_in, 32)
        nc.vector.tensor_tensor(t2[:, :, :, :].rearrange("p h r c -> p (h r) c"), t2[:, :, :, :].rearrange("p h r c -> p (h r) c"),
                                self.cmask[:, None, :].to_broadcast([128, NA_H * 15, GRID]), ALU.add)
        dve.drain()
        nc.vector.tensor_copy(ti[:, :, :, :], t2[:, :, 3:12, :])
        dve.drain()
        nc.vector.memset(ti[0:64, :, 8, :], NEGBIG)
        nc.vector.memset(ti[64:128, :, 0, :], NEGBIG)


def fourier_phase(nc, l, io, keep, na):
    with phase(nc, "four") as P:
        dch = P.sb("dch", [128, 2, 2, 256])
        wf = P.sb("wf", [128, 2, 256])
        w2 = P.sb("w2", [128, 2, 512])
        fx = P.sb("fx", [128, 2, LT])
        d1 = P.sb("d1", [128, N2, 3, 128])
        d2 = P.sb("d2", [128, 2, 128])
        dc = P.sb("dc", [128, 2, 2, 256])
        ab = P.sb("ab", [128, N2 + 2, 512])
        yo = [P.sb(f"yo{j}", [128, 512]) for j in range(4)]
        fo = [P.sb(f"fo{j}", [128, 256]) for j in range(3)]
        acc = [P.ps(f"acc{b}") for b in range(6)]
        fx_in, w_in, d1_in, d2_in, w2_mm, w2_ok, ab_mm, ab_dve, ab_act, y_mm, y_ev, o_mm, o_ev = [P.sem(s) for s in (
            "fx_in", "w_in", "d1_in", "d2_in", "w2_mm", "w2_ok", "ab_mm", "ab_dve", "ab_act", "y_mm", "y_ev",
            "o_mm", "o_ev")]
        y_out = [P.sem(f"y_out{j}") for j in range(4)]
        yi_in = [P.sem(f"yi_in{j}") for j in range(4)]
        o_out = [P.sem(f"o_out{j}") for j in range(3)]
        NAB = N2 + 2
        yrows = io["four_y"].rearrange("(p t) c -> p t c", t=N2)
        NO = 16 + 2
        with nc.Block() as block:
            @block.sync
            def _(sp):
                sp.dma_start(dch[:, :, :, :], io["dft_ch"]).then_inc(w_in, 16)
                sp.dma_start(wf[:, :, :], io["w_four"][bass.ds(l, 1), :, :, :].rearrange("a p k n -> p (a k) n")).then_inc(w_in, 16)
                sp.dma_start(fx[:, :, :], io["zcm"][0:2, :, :].rearrange("c p t -> p c t")).then_inc(fx_in, 16)
                sp.dma_start(d1[:, :, :, :], io["dft_1"]).then_inc(d1_in, 16)
                sp.dma_start(d2[:, :, :], io["dft_2"]).then_inc(d2_in, 16)
                sp.dma_start(dc[:, :, :, :], io["dft_ctx"]).then_inc(d2_in, 16)
                na.load(sp, l, io)
                for t in range(N2):
                    sp.wait_ge(y_ev, t + 1)
                    sp.dma_start(yrows[:, t, :], yo[t % 4][:, :]).then_inc(y_out[t % 4], 16)
                for j in range(4):
                    sp.wait_ge(y_out[j], 16 * (N2 // 4))
                sp.wait_ge(y_mm, N2)
                for j in range(4):
                    sp.dma_start(ab[:, 4 * j:4 * j + 4, :],
                                 io["four_y"][j * 512:(j + 1) * 512, :].rearrange("(a p) c -> p a c", p=128)).then_inc(yi_in[j], 16)

            @block.gpsimd
            def _(pool):
                na.clear(nc, pool)
                na.scale(nc, pool)
                for n in range(NO):
                    pool.wait_ge(o_ev, n + 1)
                    if n < 16:
                        dst = io["mix"][0:LX, 0:256].rearrange("(a b c) d -> b a c d", a=16, b=16)[n, :, :, :]
                        pool.dma_start(dst, fo[n % 3][:, :]).then_inc(o_out[n % 3], 16)
                    else:
                        pool.dma_start(io["mix"][LX + (n - 16) * 128:LX + (n - 15) * 128, 0:256],
                                       fo[n % 3][:, :]).then_inc(o_out[n % 3], 16)
                for j in range(3):
                    pool.wait_ge(o_out[j], 16 * (NO // 3))

            @block.tensor
            def _(pe):
                pe.wait_ge(w_in, 32)
                for m in range(2):
                    for cs in range(2):
                        for k in range(2):
                            last = nc.tensor.matmul(acc[m][:, cs * 256:(cs + 1) * 256], dch[:, cs, k, m * 128:(m + 1) * 128],
                                                    wf[:, k, :], start=(k == 0), stop=(k == 1))
                last.then_inc(w2_mm, 1)
                pe.wait_ge(w2_ok, 1)
                pe.wait_ge(fx_in, 16)
                for t in range(NAB):
                    if t >= 2:
                        pe.wait_ge(ab_act if t % 2 else ab_dve, t // 2)
                    for k in range(2):
                        lhs = fx[:, k, t:LX:N2] if t < N2 else fx[:, k, LX + (t - N2) * 128:LX + (t - N2 + 1) * 128]
                        last = nc.tensor.matmul(acc[2 + t % 2][:, :], lhs, w2[:, k, :], start=(k == 0), stop=(k == 1))
                    last.then_inc(ab_mm, 1)
                pe.wait_ge(d1_in, 16)
                pe.wait_ge(ab_dve, NAB // 2)
                pe.wait_ge(ab_act, NAB // 2)
                for t in range(N2):
                    if t >= 2:
                        pe.wait_ge(y_ev, t - 1)
                    b = acc[4 + t % 2]
                    nc.tensor.matmul(b[:, 0:256], d1[:, t, 0, :], ab[:, t, 0:256], start=True, stop=False)
                    nc.tensor.matmul(b[:, 0:256], d1[:, t, 2, :], ab[:, t, 256:512], start=False, stop=True)
                    nc.tensor.matmul(b[:, 256:512], d1[:, t, 1, :], ab[:, t, 0:256], start=True, stop=False)
                    nc.tensor.matmul(b[:, 256:512], d1[:, t, 0, :], ab[:, t, 256:512], start=False, stop=True).then_inc(y_mm, 1)
                pe.wait_ge(d2_in, 32)
                for n in range(NO):
                    if n >= 2:
                        pe.wait_ge(o_ev, n - 1)
                    b = acc[n % 2]
                    if n < 16:
                        pe.wait_ge(yi_in[n // 4], 16)
                        nc.tensor.matmul(b[:, 0:256], d2[:, 0, :], ab[:, n, 0:256], start=True, stop=False)
                        last = nc.tensor.matmul(b[:, 0:256], d2[:, 1, :], ab[:, n, 256:512], start=False, stop=True)
                    else:
                        for k in range(2):
                            for cs in range(2):
                                last = nc.tensor.matmul(b[:, 0:256], dc[:, cs, k, (n - 16) * 128:(n - 15) * 128],
                                                        ab[:, N2 + k, cs * 256:(cs + 1) * 256],
                                                        start=(k + cs == 0), stop=(k + cs == 2))
                    last.then_inc(o_mm, 1)

            @block.vector
            def _(dve):
                dve.wait_ge(w2_mm, 1)
                nc.vector.tensor_copy(w2[:, 0, :], acc[0][:, :])
                nc.vector.tensor_copy(w2[:, 1, :], acc[1][:, :]).then_inc(w2_ok, 1)
                for t in range(0, NAB, 2):
                    dve.wait_ge(ab_mm, t + 1)
                    nc.vector.tensor_copy(ab[:, t, :], acc[2][:, :]).then_inc(ab_dve, 1)
                na.bias(nc, dve)
                for n in range(NO):
                    dve.wait_ge(o_mm, n + 1)
                    if n >= 3:
                        dve.wait_ge(o_out[n % 3], 16 * (n // 3))
                    nc.vector.tensor_copy(fo[n % 3][:, :], acc[n % 2][:, 0:256]).then_inc(o_ev, 1)

            @block.scalar
            def _(act):
                for t in range(1, NAB, 2):
                    act.wait_ge(ab_mm, t + 1)
                    act.activation(ab[:, t, :], acc[3][:, :], ACT.Copy).then_inc(ab_act, 1)
                for t in range(N2):
                    act.wait_ge(y_mm, t + 1)
                    if t >= 4:
                        act.wait_ge(y_out[t % 4], 16 * (t // 4))
                    act.activation(yo[t % 4][:, :], acc[4 + t % 2][:, :], ACT.Copy).then_inc(y_ev, 1)


def neighbourhood_phase(nc, l, io, keep, na):
    with phase(nc, "na") as P:
        q, kk, t2, ti = na.q, na.kk, na.t2, na.ti
        v = P.sb("v", [128, NT, 3, 192])
        s_sb = [P.sb(f"s{j}", [128, 832]) for j in range(2)]
        pt = [P.sb(f"pt{j}", [128, 7, 128]) for j in range(2)]
        st = P.sb("st", [128, 2, NA_H, 4])
        rd = P.sb("rd", [128, 2, NA_H])
        o = [P.sb(f"o{j}", [128, D_NA]) for j in range(2)]
        sp_ps = [P.ps(f"sp{j}", (128, 1024)) for j in range(2)]
        tpa, tpb = P.ps("tpa"), P.ps("tpb")
        ops = [P.ps(f"ops{j}") for j in range(2)]
        (v_in, s_mm, s_used, m_ok, e_ok, ta_mm, tb_mm, ta_ev,
         tb_ev, pv_mm, o_ev, z_ok) = [P.sem(s) for s in (
            "v_in", "s_mm", "s_used", "m_ok", "e_ok",
            "ta_mm", "tb_mm", "ta_ev", "tb_ev", "pv_mm", "o_ev", "z_ok")]
        o_out = [P.sem(f"o_out{j}") for j in range(2)]

        tiles = []
        for i in range(ROWS // 2):
            w0 = min(max(2 * i - 4, 0), ROWS - KH)
            inner = 2 <= i < ROWS // 2 - 2
            tiles.append((128 * i, w0, 9 if inner else 8, w0 - 2 * i + 7, inner))
        for i in range(LC // 128):
            tiles.append((LX + 128 * i, 0, 0, 0, False))
        units = [(i, h) for i in range(len(tiles)) for h in range(NA_H)]
        NU = len(units)

        def key_tiles(i):
            _, w0, nr, _, _ = tiles[i]
            wl = nr * GRID
            out = [(0, j, 128, j * 128, w0 // 2 + j) for j in range(wl // 128)]
            out += [(1, j, 128, wl + j * 128, NX + j) for j in range(2)]
            if wl % 128:
                out.append((1, 2, 64, wl - 64, w0 // 2 + wl // 128))
            return out

        with nc.Block() as block:
            @block.sync
            def _(sp):
                for h in range(NA_H):
                    sp.dma_start(v[:, :, h // 2, 128 * (h % 2):128 * (h % 2) + 64],
                                 io["ztm"][:, 1024 + 64 * h:1088 + 64 * h].rearrange("(t p) c -> p t c", p=128)).then_inc(v_in, 16)
                for i, t in enumerate(tiles):
                    sp.wait_ge(o_ev, i + 1)
                    sp.dma_start(io["mix"][t[0]:t[0] + 128, 256:640], o[i % 2][:, :]).then_inc(o_out[i % 2], 16)
                for j in range(2):
                    sp.wait_ge(o_out[j], 16 * (len(tiles) // 2))

            @block.gpsimd
            def _(pool):
                nc.gpsimd.memset(v[:, :, :, 64:128], 0.0).then_inc(z_ok, 1)

            @block.tensor
            def _(pe):
                def scores(n):
                    i, h = units[n]
                    tok, w0, nr, _, _ = tiles[i]
                    if n >= 2:
                        pe.wait_ge(s_used, n - 1)
                    lo, c = 64 * (h % 2), h // 2
                    ps = sp_ps[n % 2]
                    qt = q[lo:lo + 64, c, tok:tok + 128]
                    wl = nr * GRID
                    for a in range(0, wl, 512):
                        b = min(a + 512, wl)
                        nc.tensor.matmul(ps[:, a:b], qt, kk[lo:lo + 64, c, w0 * GRID + a:w0 * GRID + b], start=True, stop=True)
                    nc.tensor.matmul(ps[:, wl:wl + 256], qt, kk[lo:lo + 64, c, LX:LT], start=True, stop=True).then_inc(s_mm, 1)

                def transposes(n):
                    i, h = units[n]
                    pe.wait_ge(e_ok, n + 1)
                    ks = key_tiles(i)
                    if n >= 1:
                        pe.wait_ge(ta_ev, n)
                    local = [x for x in ks if x[0] == 0]
                    for _, j, nk, c0, _ in local:
                        last = nc.tensor.transpose(tpa[0:nk, j * 128:(j + 1) * 128], s_sb[n % 2][:, c0:c0 + nk], keep["ident"][:, :])
                    (last if local else pe.drain()).then_inc(ta_mm, 1)
                    if n >= 1:
                        pe.wait_ge(tb_ev, n)
                    for bk, j, nk, c0, _ in ks:
                        if bk == 1:
                            last = nc.tensor.transpose(tpb[0:nk, j * 128:(j + 1) * 128], s_sb[n % 2][:, c0:c0 + nk], keep["ident"][:, :])
                    last.then_inc(tb_mm, 1)

                def values(n):
                    i, h = units[n]
                    pe.wait_ge(ta_ev, n + 1)
                    pe.wait_ge(tb_ev, n + 1)
                    if h == 0 and i >= 2:
                        pe.wait_ge(o_ev, i - 1)
                    ks = key_tiles(i)
                    for m, (bk, j, nk, _, vt) in enumerate(ks):
                        last = nc.tensor.matmul(ops[i % 2][:, (h // 2) * 128:(h // 2 + 1) * 128], pt[n % 2][0:nk, 4 * bk + j, :],
                                                v[0:nk, vt, h // 2, 64 * (h % 2):64 * (h % 2) + 128],
                                                start=(m == 0 and h % 2 == 0), stop=(m == len(ks) - 1 and h % 2 == 1))
                    last.then_inc(pv_mm, 1)

                pe.wait_ge(na.k_in, 16)
                scores(0)
                for n in range(NU + 1):
                    if n + 1 < NU:
                        scores(n + 1)
                    if n < NU:
                        transposes(n)
                    if n == 1:
                        pe.wait_ge(v_in, 16 * NA_H)
                        pe.wait_ge(z_ok, 1)
                    if n >= 1:
                        values(n - 1)

            @block.vector
            def _(dve):
                def softmax_max(n):
                    i, h = units[n]
                    _, _, nr, b0, inner = tiles[i]
                    wl = nr * GRID
                    dve.wait_ge(s_mm, n + 1)
                    if n >= 2:
                        dve.wait_ge(tb_mm, n - 1)
                    ps, ss, m = sp_ps[n % 2], s_sb[n % 2], st[:, i % 2, h, :]
                    if nr:
                        bias = (ti[:, h, :, :] if inner else t2[:, h, b0:b0 + nr, :]).rearrange("p r c -> p (r c)")
                        nc.vector.tensor_tensor_reduce(out=ss[:, 0:wl], in0=ps[:, 0:wl], in1=bias, scale=1.0, scalar=LOWEST,
                                                       op0=ALU.add, op1=ALU.max, accum_out=m[:, 0:1])
                        dve.drain()
                    nc.vector.tensor_scalar(ss[:, wl:wl + 256], ps[:, wl:wl + 256], 1.0, m[:, 0:1] if nr else LOWEST,
                                            ALU.mult, ALU.max, accum_out=m[:, 1:2]).then_inc(s_used, 1)
                    dve.drain()
                    nc.vector.tensor_scalar(m[:, 2:3], m[:, 1:2], -1.0, None, ALU.mult).then_inc(m_ok, 1)

                def probs_out(n):
                    i, h = units[n]
                    dve.wait_ge(ta_mm, n + 1)
                    if n >= 2:
                        dve.wait_ge(pv_mm, n - 1)
                    if tiles[i][2]:
                        nc.vector.tensor_copy(pt[n % 2][:, 0:4, :], tpa[:, :].rearrange("p (a b) -> p a b", b=128)).then_inc(ta_ev, 1)
                    else:
                        dve.drain().then_inc(ta_ev, 1)

                def out(i):
                    dve.wait_ge(pv_mm, NA_H * (i + 1))
                    dve.wait_ge(e_ok, NA_H * (i + 1))
                    if i >= 2:
                        dve.wait_ge(o_out[i % 2], 16 * (i // 2))
                    nc.vector.reciprocal(rd[:, i % 2, :], st[:, i % 2, :, 3])
                    dve.drain()
                    nc.vector.tensor_tensor(o[i % 2][:, :].rearrange("p (h d) -> p h d", d=64),
                                            ops[i % 2][:, 0:D_NA].rearrange("p (h d) -> p h d", d=64),
                                            rd[:, i % 2, :, None].to_broadcast([128, NA_H, 64]), ALU.mult).then_inc(o_ev, 1)

                softmax_max(0)
                for n in range(NU + 1):
                    if n + 1 < NU:
                        softmax_max(n + 1)
                    if n < NU:
                        probs_out(n)
                    if n >= 2 and (n - 1) % NA_H == NA_H - 1:
                        out((n - 1) // NA_H)

            @block.scalar
            def _(act):
                def exps(n):
                    i, h = units[n]
                    w = tiles[i][2] * GRID + 256
                    act.wait_ge(m_ok, n + 1)
                    if h == 0 and i >= 2:
                        act.wait_ge(o_ev, i - 1)
                    m = st[:, i % 2, h, :]
                    act.activation(s_sb[n % 2][:, 0:w], s_sb[n % 2][:, 0:w], ACT.Exp, bias=m[:, 2:3],
                                   accum_out=m[:, 3:4]).then_inc(e_ok, 1)
                exps(0)
                for n in range(NU):
                    if n + 1 < NU:
                        exps(n + 1)
                    act.wait_ge(tb_mm, n + 1)
                    if n >= 2:
                        act.wait_ge(pv_mm, n - 1)
                    ks = key_tiles(units[n][0])
                    last = act.activation(pt[n % 2][:, 4:6, :], tpb[:, 0:256].rearrange("p (a b) -> p a b", b=128), ACT.Copy)
                    if ks[-1][2] == 64:
                        last = act.activation(pt[n % 2][0:64, 6, :], tpb[0:64, 256:384], ACT.Copy)
                    last.then_inc(tb_ev, 1)

def gla_phase(nc, l, io, keep):
    NCC = LC // CH
    fwd = list(range(LX // CH, NCH)) + list(range(LX // CH))
    order = [fwd, list(range(NCH - 1, LX // CH - 1, -1)) + list(range(LX // CH - 1, -1, -1))]
    TT = [(i * 512, min(512, LT - i * 512)) for i in range((LT + 511) // 512)]
    with phase(nc, "gla") as P:
        perm = P.sb("perm", [128, 128])
        mask = P.sb("mask", [128, 2, 128], I32)
        start = P.sb("start", [128, LT])
        wa = P.sb("wa", [64, 256])
        ba = P.sb("ba", [128, 4])
        z = P.sb("z", [64, LT])
        q = P.sb("q", [128, LT])
        k = P.sb("k", [128, LT])
        v = P.sb("v", [128, NT, 2 * GDV])
        b = [P.sb(f"b{d}", [128, LT]) for d in range(2)]
        t1 = [P.sb(f"t{d}", [128, LT]) for d in range(2)]
        cs, sn = t1[0][:, 0:LX], t1[1][:, 0:LX]
        qd = [P.sb(f"qd{d}", [128, LT]) for d in range(2)]
        kd = [P.sb(f"kd{d}", [128, LT]) for d in range(2)]
        kt = [P.sb(f"kt{d}", [128, NT, 128]) for d in range(2)]
        eb = P.sb("eb", [128, 2, NCH])
        S = P.sb("S", [128, 2, NCH, GDV])
        at = P.sb("at", [128, 2, 2, 128])
        asum = [P.sb(f"asum{j}", [128, 2, 128]) for j in range(2)]
        o = [P.sb(f"o{j}", [128, 2 * GDV]) for j in range(2)]
        bank = [P.ps(f"bank{n}") for n in range(8)]
        turn = lambda d, n: bank[(5 * d + n) % 8]
        ups = [[bank[2 * p + j] for j in range(2)] for p in range(2)]
        aps = [[bank[2 * j + h] for h in range(2)] for j in range(2)]
        ops = [[bank[4 + 2 * j + h] for h in range(2)] for j in range(2)]
        UB = 5
        batches = [range(s0, min(s0 + UB, NCH - 1)) for s0 in range(0, NCH - 1, UB)]
        NB = len(batches)
        names = ("perm_in", "cst_in", "q_in", "k_in", "v_in", "rot_mm", "rot_ev", "qk_ok", "g_mm", "abs_ok", "min_ok", "ln_ok", "b_ok",
                 "exp_q", "exp_k", "end_ok", "exp_e", "qd_ok", "kd_ok", "kte_ok", "kt_mm", "kt_dve", "kt_act", "u_mm", "s_ok",
                 "a_mm", "a_ok", "o_mm", "o_ok")
        m = {n: P.sem(n) for n in names}
        o_out = [P.sem(f"o_out{j}") for j in range(2)]
        KG = (NT + 3) // 4
        KD, KA = (KG + 1) // 2, KG // 2

        def group(g):
            return range(4 * g, min(4 * g + 4, NT))

        def store(sp, g):
            hh, n = g // NT, g % NT
            sp.wait_ge(m["o_ok"], g + 1)
            sp.dma_start(io["mix"][n * 128:(n + 1) * 128, 640 + hh * 192:640 + (hh + 1) * 192],
                         o[g % 2][:, :]).then_inc(o_out[g % 2], 16)

        with nc.Block() as block:
            @block.sync
            def _(sp):
                def load_qk(hh):
                    sp.dma_start(q[:, :], io["zcm"][8 + hh, :, :]).then_inc(m["q_in"], 16)
                    sp.dma_start(cs, io["rope_cs"][:, 0, :]).then_inc(m["k_in"], 16)
                    sp.dma_start(sn, io["rope_cs"][:, 1, :]).then_inc(m["k_in"], 16)
                    sp.dma_start(k[:, :], io["zcm"][10 + hh, :, :]).then_inc(m["k_in"], 16)

                sp.dma_start(perm[:, :], io["rope_perm"]).then_inc(m["perm_in"], 16)
                load_qk(0)
                for dst, src in ((mask[:, :, :], io["gla_mask"]), (start[:, :], io["chunk_start"]),
                                 (wa[:, :], io["w_alpha"][bass.ds(l, 1), :, :].rearrange("a p n -> p (a n)")),
                                 (ba[:, :], io["b_alpha"][bass.ds(l, 1), :, :].rearrange("a p n -> p (a n)")),
                                 (z[0:RANK, :], io["zcm"][8, GDK:64, :]), (z[32:32 + RANK, :], io["zcm"][8, 64 + GDK:128, :])):
                    sp.dma_start(dst, src).then_inc(m["cst_in"], 16)
                for hh in range(2):
                    if hh:
                        sp.wait_ge(m["kt_mm"], 2 * KG)
                        sp.wait_ge(m["kd_ok"], 2)
                        sp.wait_ge(m["qd_ok"], 2)
                        load_qk(1)
                        for n in range(NT):
                            store(sp, n)
                    c0 = 1024 + D_NA + hh * 2 * GDV
                    sp.dma_start(v[:, :, :], io["ztm"][:, c0:c0 + 2 * GDV].rearrange("(t p) c -> p t c", p=128)).then_inc(m["v_in"], 16)
                for n in range(NT, 2 * NT):
                    store(sp, n)
                for j in range(2):
                    sp.wait_ge(o_out[j], 16 * NT)

            @block.tensor
            def _(pe):
                def products(g):
                    n = g % NT
                    if g >= 2:
                        pe.wait_ge(m["a_ok"], g - 1)
                    for h in range(2):
                        for d in range(2):
                            last = nc.tensor.matmul(aps[g % 2][h][:, d * 128:(d + 1) * 128],
                                                    kd[d][64 * h:64 * h + 64, n * 128:(n + 1) * 128],
                                                    qd[d][64 * h:64 * h + 64, n * 128:(n + 1) * 128], start=True, stop=True)
                    last.then_inc(m["a_mm"], 1)

                pe.wait_ge(m["perm_in"], 16)
                for hh in range(2):
                    pe.wait_ge(m["q_in"], 16 * (hh + 1))
                    if hh:
                        pe.wait_ge(m["a_ok"], NT)
                        pe.wait_ge(m["o_ok"], NT)
                    for w, src in enumerate((q, k)):
                        if w:
                            pe.wait_ge(m["k_in"], 48 * (hh + 1))
                        for n in range(4):
                            last = nc.tensor.matmul(bank[4 * w + n][:, :], perm[:, :], src[:, n * 512:(n + 1) * 512], start=True, stop=True)
                        last.then_inc(m["rot_mm"], 1)
                    pe.wait_ge(m["rot_ev"], 2 * hh + 1)
                    if hh == 0:
                        pe.wait_ge(m["cst_in"], 16 * 6)
                    for d in range(2):
                        for n, (a, w) in enumerate(TT):
                            if d == 0 and n == 4:
                                pe.wait_ge(m["rot_ev"], 2 * hh + 2)
                            if d == 1 and n == 3:
                                pe.wait_ge(m["abs_ok"], 2 * hh + 1)
                                pe.wait_ge(m["min_ok"], 2 * hh + 1)
                            last = nc.tensor.matmul(turn(d, n)[:, 0:w], wa[32 * d:32 * d + RANK, hh * 128:(hh + 1) * 128],
                                                    z[32 * d:32 * d + RANK, a:a + w], start=True, stop=True)
                        last.then_inc(m["g_mm"], 1)
                    pe.wait_ge(m["abs_ok"], 2 * hh + 2)
                    pe.wait_ge(m["min_ok"], 2 * hh + 2)
                    for d in range(2):
                        r = 2 * hh + d
                        pe.wait_ge(m["kte_ok"], r + 1)
                        for g in range(KG):
                            if d == 1 and g == 3:
                                pe.wait_ge(m["kt_dve"], KD * r)
                                pe.wait_ge(m["kt_act"], KA * r)
                            for t in group(g):
                                last = nc.tensor.transpose(turn(d, g)[:, (t - 4 * g) * 128:(t - 4 * g + 1) * 128],
                                                           t1[d][:, t * 128:(t + 1) * 128], keep["ident"][:, :])
                            last.then_inc(m["kt_mm"], 1)
                    pe.wait_ge(m["kt_dve"], KD * 2 * (hh + 1))
                    pe.wait_ge(m["kt_act"], KA * 2 * (hh + 1))
                    pe.wait_ge(m["v_in"], 16 * (hh + 1))
                    for i, steps in enumerate(batches):
                        if i >= 2:
                            pe.wait_ge(m["s_ok"], hh * NB + i - 1)
                        for d in range(2):
                            for s in steps:
                                c = order[d][s]
                                p0 = 64 * (c % 2)
                                for h in range(2):
                                    last = nc.tensor.matmul(ups[c % 2][i % 2][64 * h:64 * h + 64, (s - steps[0]) * GDV:(s - steps[0] + 1) * GDV],
                                                            kt[d][p0:p0 + 64, c // 2, 64 * h:64 * h + 64],
                                                            v[p0:p0 + 64, c // 2, h * GDV:(h + 1) * GDV], start=True, stop=True)
                        last.then_inc(m["u_mm"], 1)
                    pe.wait_ge(m["s_ok"], (hh + 1) * NB)
                    pe.wait_ge(m["qd_ok"], 2 * (hh + 1))
                    pe.wait_ge(m["kd_ok"], 2 * (hh + 1))
                    products(hh * NT)
                    for n in range(NT):
                        g = hh * NT + n
                        if n + 1 < NT:
                            products(g + 1)
                        pe.wait_ge(m["a_ok"], g + 1)
                        if g >= 2:
                            pe.wait_ge(m["o_ok"], g - 1)
                        for h in range(2):
                            oc = ops[g % 2][h][:, 0:GDV]
                            nc.tensor.matmul(oc, asum[g % 2][:, h, :], v[:, n, h * GDV:(h + 1) * GDV],
                                             start=True, stop=False, skip_group_check=True)
                            for cc in range(2):
                                for d in range(2):
                                    c = 2 * n + cc
                                    last = nc.tensor.matmul(ops[g % 2][h][64 * cc:64 * cc + 64, 0:GDV],
                                                            qd[d][64 * h:64 * h + 64, c * 64:(c + 1) * 64],
                                                            S[64 * h:64 * h + 64, d, c, :], start=False, stop=(d == 1),
                                                            skip_group_check=True)
                        last.then_inc(m["o_mm"], 1)

            @block.vector
            def _(dve):
                nc.vector.memset(at[:, :, :, :], 0.0)
                for d in range(2):
                    nc.vector.memset(S[:, d, order[d][0], :], 0.0)
                for hh in range(2):
                    dve.wait_ge(m["q_in"], 16 * (hh + 1))
                    dve.wait_ge(m["k_in"], 48 * (hh + 1))
                    for w, x in enumerate((q, k)):
                        dve.wait_ge(m["rot_mm"], 2 * hh + w + 1)
                        nc.vector.tensor_tensor(x[:, 0:LX], x[:, 0:LX], cs, ALU.mult)
                        for n in range(4):
                            nc.vector.tensor_tensor(b[w][:, n * 512:(n + 1) * 512], bank[4 * w + n][:, :], sn[:, n * 512:(n + 1) * 512], ALU.mult)
                        dve.drain().then_inc(m["rot_ev"], 1)
                        nc.vector.tensor_tensor(x[:, 0:LX], x[:, 0:LX], b[w][:, 0:LX], ALU.add)
                        dve.drain()
                    nc.vector.tensor_scalar(q[:, :], q[:, :], GDK ** -0.5, None, ALU.mult).then_inc(m["qk_ok"], 1)
                    if hh == 0:
                        dve.wait_ge(m["cst_in"], 16 * 6)
                    for d in range(2):
                        r = 2 * hh + d
                        dve.wait_ge(m["abs_ok"], r + 1)
                        for n, (a, w) in enumerate(TT):
                            nc.vector.tensor_scalar(b[d][:, a:a + w], turn(d, n)[:, 0:w], ba[:, 2 * d + hh:2 * d + hh + 1], 0.0, ALU.add, ALU.min)
                        dve.drain().then_inc(m["min_ok"], 1)
                    for d in range(2):
                        r = 2 * hh + d
                        dve.wait_ge(m["ln_ok"], r + 1)
                        nc.vector.tensor_tensor(t1[d][:, :], b[d][:, :], t1[d][:, :], ALU.subtract)
                        dve.drain()
                        if d == 0:
                            nc.vector.tensor_tensor_scan(b[d][:, :], start[:, :], t1[d][:, :], 0.0, ALU.mult, ALU.add)
                        else:
                            nc.vector.tensor_tensor_scan(b[d][:, ::-1], start[:, :], t1[d][:, ::-1], 0.0, ALU.mult, ALU.add)
                        dve.drain().then_inc(m["b_ok"], 1)
                        bc = b[d][:, :].rearrange("p (c t) -> p c t", t=CH)
                        end = bc[:, :, CH - 1] if d == 0 else bc[:, :, 0]
                        nc.vector.tensor_tensor(t1[d][:, :].rearrange("p (c t) -> p c t", t=CH),
                                                end[:, :, None].to_broadcast([128, NCH, CH]), bc, ALU.subtract).then_inc(m["end_ok"], 1)
                    for d in range(2):
                        r = 2 * hh + d
                        dve.wait_ge(m["exp_e"], r + 1)
                        nc.vector.tensor_tensor(t1[d][:, :], k[:, :], t1[d][:, :], ALU.mult).then_inc(m["kte_ok"], 1)
                    for d in range(2):
                        r = 2 * hh + d
                        for g in range(0, KG, 2):
                            dve.wait_ge(m["kt_mm"], KG * r + g + 1)
                            n = len(group(g))
                            nc.vector.tensor_copy(kt[d][:, 4 * g:4 * g + n, :],
                                                  turn(d, g)[:, 0:128 * n].rearrange("p (a b) -> p a b", b=128)).then_inc(m["kt_dve"], 1)
                    for i, steps in enumerate(batches):
                        dve.wait_ge(m["u_mm"], hh * NB + i + 1)
                        for s in steps:
                            for d in range(2):
                                c, nx = order[d][s], order[d][s + 1]
                                nc.vector.scalar_tensor_tensor(S[:, d, nx, :], S[:, d, c, :], eb[:, d, c:c + 1],
                                                               ups[c % 2][i % 2][:, (s - steps[0]) * GDV:(s - steps[0] + 1) * GDV],
                                                               ALU.mult, ALU.add)
                            last = dve.drain()
                        last.then_inc(m["s_ok"], 1)
                    for n in range(NT):
                        g = hh * NT + n
                        dve.wait_ge(m["a_mm"], g + 1)
                        if g >= 2:
                            dve.wait_ge(m["o_mm"], g - 1)
                        for h in range(2):
                            nc.vector.copy_predicated(at[:, h, :, :].rearrange("p a b -> p (a b)"),
                                                      mask[:, :, :].rearrange("p b c -> p (b c)"), aps[g % 2][h][:, 0:256])
                        dve.drain()
                        nc.vector.tensor_tensor(asum[g % 2][:, :, :], at[:, :, 0, :], at[:, :, 1, :], ALU.add).then_inc(m["a_ok"], 1)
                        dve.drain()

            @block.gpsimd
            def _(pool):
                for hh in range(2):
                    for d in range(2):
                        r = 2 * hh + d
                        pool.wait_ge(m["exp_q"], r + 1)
                        nc.gpsimd.tensor_tensor(qd[d][:, :], q[:, :], qd[d][:, :], ALU.mult).then_inc(m["qd_ok"], 1)
                        pool.wait_ge(m["exp_k"], r + 1)
                        nc.gpsimd.tensor_tensor(kd[d][:, :], k[:, :], kd[d][:, :], ALU.mult).then_inc(m["kd_ok"], 1)

            @block.scalar
            def _(act):
                for hh in range(2):
                    for d in range(2):
                        r = 2 * hh + d
                        act.wait_ge(m["g_mm"], r + 1)
                        if d == 0:
                            act.wait_ge(m["qk_ok"], hh + 1)
                        for n, (a, w) in enumerate(TT):
                            act.activation(t1[d][:, a:a + w], turn(d, n)[:, 0:w], ACT.Abs, bias=ba[:, 2 * d + hh:2 * d + hh + 1])
                        act.drain().then_inc(m["abs_ok"], 1)
                        act.activation(t1[d][:, :], t1[d][:, :], ACT.Exp, scale=-1.0)
                        act.drain()
                        act.activation(t1[d][:, :], t1[d][:, :], ACT.Ln, bias=1.0).then_inc(m["ln_ok"], 1)
                    if hh:
                        act.wait_ge(m["o_mm"], NT)
                    for d in range(2):
                        r = 2 * hh + d
                        act.wait_ge(m["b_ok"], r + 1)
                        bc = b[d][:, :].rearrange("p (c t) -> p c t", t=CH)
                        act.activation(eb[:, d, :], bc[:, :, CH - 1] if d == 0 else bc[:, :, 0], ACT.Exp, scale=1.0 / 16)
                        act.activation(qd[d][:, :], b[d][:, :], ACT.Exp, scale=1.0 / 16).then_inc(m["exp_q"], 1)
                        act.wait_ge(m["end_ok"], r + 1)
                        act.activation(t1[d][:, :], t1[d][:, :], ACT.Exp, scale=1.0 / 16).then_inc(m["exp_e"], 1)
                        act.activation(kd[d][:, :], b[d][:, :], ACT.Exp, scale=-1.0 / 16).then_inc(m["exp_k"], 1)
                    for d in range(2):
                        r = 2 * hh + d
                        for g in range(1, KG, 2):
                            act.wait_ge(m["kt_mm"], KG * r + g + 1)
                            n = len(group(g))
                            act.activation(kt[d][:, 4 * g:4 * g + n, :],
                                           turn(d, g)[:, 0:128 * n].rearrange("p (a b) -> p a b", b=128), ACT.Copy).then_inc(m["kt_act"], 1)
                    for n in range(NT):
                        g = hh * NT + n
                        act.wait_ge(m["o_mm"], g + 1)
                        if g >= 2:
                            act.wait_ge(o_out[g % 2], 16 * (g // 2))
                        for h in range(2):
                            last = act.activation(o[g % 2][:, h * GDV:(h + 1) * GDV], ops[g % 2][h][:, 0:GDV], ACT.Copy)
                        last.then_inc(m["o_ok"], 1)


def out_phase(nc, l, io, keep):
    with phase(nc, "out") as P:
        raw = [P.sb(f"raw{k}", [128, D]) for k in range(KC)]
        w = Split(P.sb, "w", [128, KC, D])
        gate = P.sb("gate", [128, 2, D])
        gw = P.sb("gw", [128, GH, GDV])
        mx = [P.sb(f"mx{j}", [128, D]) for j in range(2)]
        gt = [P.sb(f"gt{j}", [128, D]) for j in range(2)]
        x = [P.sb(f"x{j}", [128, D]) for j in range(3)]
        mT = [Split(P.sb, f"mT{j}", [128, KC, 128]) for j in range(2)]
        y = P.sb("y", [128, D])
        sq = P.sb("sq", [128, GH, GDV])
        ss = P.sb("ss", [128, 2, 2, GH])
        tp = [[P.ps(f"tp{j}{h}") for h in range(2)] for j in range(2)]
        acc = [[P.ps(f"acc{j}{h}") for h in range(2)] for j in range(2)]
        w_in, ss_ok, sr_ok, m_ok, t_mm, t_dve, t_act, y_mm, y_ok, x_ok = [P.sem(s) for s in (
            "w_in", "ss_ok", "sr_ok", "m_ok", "t_mm", "t_dve", "t_act", "y_mm", "y_ok", "x_ok")]
        raw_in = [P.sem(f"raw_in{k}") for k in range(KC)]
        w_hi, w_dve, w_pool = P.sem("w_hi"), P.sem("w_dve"), P.sem("w_pool")
        ld = [P.sem(f"ld{j}") for j in range(2)]
        xl = [P.sem(f"xl{j}") for j in range(3)]
        xo = [P.sem(f"xo{j}") for j in range(3)]
        with nc.Block() as block:
            @block.sync
            def _(sp):
                for s in range(2):
                    sp.dma_start(gate[:, s, :], bcast_rows(io["gates"][s, :], D)).then_inc(w_in, 16)
                for h in range(GH):
                    sp.dma_start(gw[:, h, :], io["gla_norm_w"][bass.ds(l, 1), :].to_broadcast([128, GDV])).then_inc(w_in, 16)
                for t in range(NT):
                    rows = slice(t * 128, (t + 1) * 128)
                    if t >= 2:
                        sp.wait_ge(m_ok, t - 1)
                        sp.wait_ge(t_mm, t - 1)
                    sp.dma_start(mx[t % 2][:, :], io["mix"][rows, :]).then_inc(ld[t % 2], 16)
                    sp.dma_start(gt[t % 2][:, :], io["ztm"][rows, 0:D]).then_inc(ld[t % 2], 16)
                    if t >= 3:
                        sp.wait_ge(xo[t % 3], 16 * (t // 3))
                    sp.dma_start(x[t % 3][:, :], io["xres"][rows, :]).then_inc(xl[t % 3], 16)
                    if t == 0:
                        for k in range(KC):
                            sp.dma_start(raw[k][:, :], io["w_out"][bass.ds(l, 1), k * 128:(k + 1) * 128, :].rearrange("a p n -> p (a n)")).then_inc(raw_in[k], 16)

            @block.gpsimd
            def _(pool):
                for k in range(1, KC, 2):
                    pool.wait_ge(w_hi, k + 1)
                    nc.gpsimd.tensor_tensor(w.lo[:, k, :], raw[k][:, :], w.hi[:, k, :].bitcast(F32), ALU.subtract).then_inc(w_pool, 1)
                for t in range(NT):
                    pool.wait_ge(x_ok, t + 1)
                    pool.dma_start(io["xres"][t * 128:(t + 1) * 128, :], x[t % 3][:, :]).then_inc(xo[t % 3], 16)
                for j in range(3):
                    pool.wait_ge(xo[j], 16 * (NT // 3))

            @block.vector
            def _(dve):
                def mixed(t):
                    j = t % 2
                    g = mx[j][:, 640:1024].rearrange("p (h d) -> p h d", d=GDV)
                    dve.wait_ge(ld[j], 32 * (t // 2 + 1))
                    nc.vector.tensor_tensor(sq[:, :, :], g, g, ALU.mult)
                    dve.drain()
                    nc.vector.tensor_reduce(ss[:, j, 0, :], sq[:, :, :], AX.X, ALU.add).then_inc(ss_ok, 1)
                    nc.vector.tensor_tensor(mx[j][:, 0:640], mx[j][:, 0:640], gt[j][:, 0:640], ALU.mult)
                    dve.drain()
                    nc.vector.tensor_tensor(sq[:, :, :], gt[j][:, 640:1024].rearrange("p (h d) -> p h d", d=GDV), gw[:, :, :], ALU.mult)
                    dve.wait_ge(sr_ok, t + 1)
                    nc.vector.reciprocal(ss[:, j, 1, :], ss[:, j, 1, :])
                    dve.drain()
                    nc.vector.tensor_tensor(g, g, ss[:, j, 1, :, None].to_broadcast([128, GH, GDV]), ALU.mult)
                    dve.drain()
                    nc.vector.tensor_tensor(g, g, sq[:, :, :], ALU.mult).then_inc(m_ok, 1)

                def taken(t):
                    j = t % 2
                    dve.wait_ge(t_mm, t + 1)
                    if t >= 2:
                        dve.wait_ge(y_mm, t - 1)
                    for i in range(2):
                        if i:
                            dve.wait_ge(t_act, t + 1)
                        src = tp[j][i][:, :].rearrange("p (a b) -> p a b", b=128)
                        hi = mT[j].hi[:, 4 * i:4 * i + 4, :]
                        if i == 0:
                            nc.vector.tensor_copy(hi, src)
                            dve.drain()
                        last = nc.vector.tensor_tensor(mT[j].lo[:, 4 * i:4 * i + 4, :], src, hi.bitcast(F32), ALU.subtract)
                    last.then_inc(t_dve, 1)

                def residual(t):
                    j = t % 2
                    dve.wait_ge(y_mm, t + 1)
                    s = 0 if t < NX else 1
                    for h in range(2):
                        nc.vector.tensor_tensor(y[:, h * 512:(h + 1) * 512], acc[j][h][:, :], gate[:, s, h * 512:(h + 1) * 512], ALU.mult)
                    dve.drain().then_inc(y_ok, 1)
                    dve.wait_ge(xl[t % 3], 16 * (t // 3 + 1))
                    nc.vector.tensor_tensor(x[t % 3][:, :], x[t % 3][:, :], y[:, :], ALU.add).then_inc(x_ok, 1)
                    dve.drain()

                dve.wait_ge(w_in, 16 * (2 + GH))
                mixed(0)
                for k in range(0, KC, 2):
                    dve.wait_ge(w_hi, k + 1)
                    nc.vector.tensor_tensor(w.lo[:, k, :], raw[k][:, :], w.hi[:, k, :].bitcast(F32), ALU.subtract).then_inc(w_dve, 1)
                for t in range(NT):
                    taken(t)
                    if t + 1 < NT:
                        mixed(t + 1)
                    if t >= 1:
                        residual(t - 1)
                residual(NT - 1)

            @block.scalar
            def _(act):
                def root(t):
                    act.wait_ge(ss_ok, t + 1)
                    act.activation(ss[:, t % 2, 1, :], ss[:, t % 2, 0, :], ACT.Sqrt, scale=1.0 / GDV, bias=keep["eps"][:, 0:1]).then_inc(sr_ok, 1)
                root(0)
                for k in range(KC):
                    act.wait_ge(raw_in[k], 16)
                    act.activation(w.hi[:, k, :], raw[k][:, :], ACT.Copy).then_inc(w_hi, 1)
                for t in range(NT):
                    act.wait_ge(t_mm, t + 1)
                    if t >= 2:
                        act.wait_ge(y_mm, t - 1)
                    act.activation(mT[t % 2].hi[:, 4:8, :], tp[t % 2][1][:, :].rearrange("p (a b) -> p a b", b=128), ACT.Copy).then_inc(t_act, 1)
                    if t + 1 < NT:
                        root(t + 1)

            @block.tensor
            def _(pe):
                def transposes(t):
                    pe.wait_ge(m_ok, t + 1)
                    if t >= 2:
                        pe.wait_ge(t_dve, t - 1)
                    for k in range(KC):
                        last = nc.tensor.transpose(tp[t % 2][k // 4][:, (k % 4) * 128:(k % 4 + 1) * 128],
                                                   mx[t % 2][:, k * 128:(k + 1) * 128], keep["ident"][:, :])
                    last.then_inc(t_mm, 1)
                transposes(0)
                for t in range(NT):
                    if t + 1 < NT:
                        transposes(t + 1)
                    pe.wait_ge(t_dve, t + 1)
                    if t >= 2:
                        pe.wait_ge(y_ok, t - 1)
                    for h in range(2):
                        for k in range(KC):
                            if t == 0 and h == 0:
                                pe.wait_ge(w_pool if k % 2 else w_dve, k // 2 + 1)
                            last = matmul3(nc, acc[t % 2][h][:, :], mT[t % 2][:, k, :], w[:, k, h * 512:(h + 1) * 512], k == 0, k == KC - 1)
                    last.then_inc(y_mm, 1)

class HeadNormRope:

    def __init__(self, P, nc, io, keep):
        self.nc, self.io, self.keep = nc, io, keep
        self.pos_i = P.sb("pos", [128, NX], I32)
        self.pos_f = P.sb("posf", [128, NX])
        self.inv = P.sb("inv", [128, 32])
        self.ang = P.sb("ang", [128, NX, 32])
        self.trn = P.sb("trn", [128, NX, 32])
        self.sc = P.sb("sc", [128, 2, NX, 32])
        self.wqk = P.sb("wqk", [128, 2, HD])
        self.x = [P.sb(f"x{j}", [128, HB, HD]) for j in range(2)]
        self.sq = [P.sb(f"sq{j}", [128, HB, HD]) for j in range(2)]
        self.pr = P.sb("pr", [128, 2, HB, 32])
        self.pp = P.sb("pp", [128, 2, HB, 32])
        self.ss = P.sb("ss", [128, 2, 2, HB])
        (self.cst_in, self.red_ok, self.sc_ok, self.sq_ok, self.ss_ok, self.sr_ok, self.n_ok, self.y_dve, self.y_pool,
         self.pp_ok) = [P.sem(s) for s in ("cst_in", "red_ok", "sc_ok", "sq_ok", "ss_ok", "sr_ok", "n_ok", "y_dve",
                                           "y_pool", "pp_ok")]

    def load(self, sp):
        io = self.io
        for dst, src in ((self.pos_i[:, :], io["positions"]), (self.inv[:, :], bcast_rows(io["inv_freq"], 32)),
                         (self.wqk[:, 0, :], bcast_rows(io["q_norm"], HD)), (self.wqk[:, 1, :], bcast_rows(io["k_norm"], HD))):
            sp.dma_start(dst, src).then_inc(self.cst_in, 16)

    def tables_act(self, act):
        for w in range(2):
            act.wait_ge(self.red_ok, w + 1)
            act.activation(self.sc[:, w, :, :], self.trn[:, :, :], ACT.Sin).then_inc(self.sc_ok, 1)

    def tables_dve(self, dve):
        nc = self.nc
        TWO_PI = 2 * math.pi
        C1 = 6.28125
        C2 = float(np.float32(round((TWO_PI - C1) * 2 ** 20) / 2 ** 20))
        C3 = float(np.float32(TWO_PI - C1 - C2))
        MAGIC = 1.5 * 2 ** 23
        LIM = float(np.nextafter(np.float32(math.pi), np.float32(0)))
        ang, trn = self.ang, self.trn
        dve.wait_ge(self.cst_in, 64)
        nc.vector.tensor_scalar(self.wqk[:, 0, :], self.wqk[:, 0, :], HD ** -0.5, None, ALU.mult)
        nc.vector.tensor_copy(self.pos_f[:, :], self.pos_i[:, :])
        dve.drain()
        nc.vector.tensor_tensor(ang[:, :, :], self.pos_f[:, :, None].to_broadcast([128, NX, 32]),
                                self.inv[:, None, :].to_broadcast([128, NX, 32]), ALU.mult)
        dve.drain()
        for w, (turn, add) in enumerate(((0.25, math.pi / 2), (0.0, 0.0))):
            if w:
                dve.wait_ge(self.sc_ok, 1)
            nc.vector.tensor_scalar(trn[:, :, :], ang[:, :, :], 1 / TWO_PI, turn, ALU.mult, ALU.add)
            dve.drain()
            nc.vector.tensor_scalar(trn[:, :, :], trn[:, :, :], MAGIC, None, ALU.add)
            dve.drain()
            nc.vector.tensor_scalar(trn[:, :, :], trn[:, :, :], MAGIC, None, ALU.subtract)
            dve.drain()
            whole = self.x[0][:, :, :].rearrange("p a b -> p (a b)").rearrange("p (a b) -> p a b", b=32)
            nc.vector.scalar_tensor_tensor(whole, trn[:, :, :], -C1, ang[:, :, :], ALU.mult, ALU.add)
            dve.drain()
            nc.vector.scalar_tensor_tensor(whole, trn[:, :, :], -C2, whole, ALU.mult, ALU.add)
            dve.drain()
            nc.vector.scalar_tensor_tensor(whole, trn[:, :, :], -C3, whole, ALU.mult, ALU.add)
            dve.drain()
            nc.vector.tensor_scalar(whole, whole, add, LIM, ALU.add, ALU.min)
            dve.drain()
            nc.vector.tensor_scalar(trn[:, :, :], whole, -LIM, None, ALU.max).then_inc(self.red_ok, 1)
            dve.drain()
        dve.wait_ge(self.sc_ok, 2)

    def act(self, act, u, bank):
        j = u % 2
        if u >= 2:
            act.wait_ge(self.ss_ok, u - 1)
        act.activation(self.sq[j][:, :, :].rearrange("p h d -> p (h d)"), bank[:, :], ACT.Square).then_inc(self.sq_ok, 1)
        act.wait_ge(self.ss_ok, u + 1)
        act.activation(self.ss[:, j, 1, :], self.ss[:, j, 0, :], ACT.Sqrt, scale=1.0 / HD,
                       bias=self.keep["eps"][:, 0:1]).then_inc(self.sr_ok, 1)

    def dve(self, dve, u, bank, out, bank_read, stored, stores):
        nc, j = self.nc, u % 2
        x, t, w = self.x[j], u % NX, u // NX
        y = out[:, :].rearrange("p (h d) -> p h d", d=HD)
        dve.wait_ge(self.sq_ok, u + 1)
        if u >= 2:
            dve.wait_ge(self.y_pool, u - 1)
        nc.vector.tensor_tensor(x[:, :, :], bank[:, :].rearrange("p (h d) -> p h d", d=HD),
                                self.wqk[:, w, None, :].to_broadcast([128, HB, HD]), ALU.mult).then_inc(bank_read, 1)
        nc.vector.tensor_reduce(self.ss[:, j, 0, :], self.sq[j][:, :, :], AX.X, ALU.add).then_inc(self.ss_ok, 1)
        dve.wait_ge(self.sr_ok, u + 1)
        nc.vector.reciprocal(self.ss[:, j, 1, :], self.ss[:, j, 1, :])
        dve.drain()
        nc.vector.tensor_tensor(x[:, :, :], x[:, :, :], self.ss[:, j, 1, :, None].to_broadcast([128, HB, HD]), ALU.mult)
        dve.drain().then_inc(self.n_ok, 1)
        c = self.sc[:, 0, t, None, :].to_broadcast([128, HB, 32])
        s = self.sc[:, 1, t, None, :].to_broadcast([128, HB, 32])
        nc.vector.tensor_tensor(self.pr[:, 0, :, :], x[:, :, 0:32], c, ALU.mult)
        nc.vector.tensor_tensor(self.pr[:, 1, :, :], x[:, :, 32:64], s, ALU.mult)
        dve.drain()
        dve.wait_ge(stored, stores)
        nc.vector.tensor_tensor(y[:, :, 0:32], self.pr[:, 0, :, :], self.pr[:, 1, :, :], ALU.subtract).then_inc(self.y_dve, 1)
        dve.drain()

    def pool(self, pool, u, out, stored, stores):
        nc, x, t = self.nc, self.x[u % 2], u % NX
        y = out[:, :].rearrange("p (h d) -> p h d", d=HD)
        pool.wait_ge(self.n_ok, u + 1)
        c = self.sc[:, 0, t, None, :].to_broadcast([128, HB, 32])
        s = self.sc[:, 1, t, None, :].to_broadcast([128, HB, 32])
        nc.gpsimd.tensor_tensor(self.pp[:, 0, :, :], x[:, :, 32:64], c, ALU.mult)
        nc.gpsimd.tensor_tensor(self.pp[:, 1, :, :], x[:, :, 0:32], s, ALU.mult).then_inc(self.pp_ok, 1)
        pool.wait_ge(self.pp_ok, u + 1)
        pool.wait_ge(stored, stores)
        nc.gpsimd.tensor_tensor(y[:, :, 32:64], self.pp[:, 0, :, :], self.pp[:, 1, :, :], ALU.add).then_inc(self.y_pool, 1)
        pool.wait_ge(self.y_pool, u + 1)

    def finished(self, sp, u):
        sp.wait_ge(self.y_dve, u + 1)
        sp.wait_ge(self.y_pool, u + 1)


class FinalWeights:

    def __init__(self, P):
        self.wo = Split(P.sb, "wo", [128, KC, D])
        self.wg = P.sb("wg", [128, KC, D])
        self.wp = P.sb("wp", [128, 2, D])
        self.raw_in = [P.sem(f"raw_in{j}") for j in range(2)]
        self.hi_ok, self.lo_ok, self.plain_in = P.sem("hi_ok"), P.sem("lo_ok"), P.sem("plain_in")

    def load(self, sp, io, raw, k):
        if k >= 2:
            sp.wait_ge(self.lo_ok, k - 1)
        sp.dma_start(raw[k % 2][:, :], io["w_out2"][k * 128:(k + 1) * 128, :]).then_inc(self.raw_in[k % 2], 16)
        if k == KC - 1:
            sp.dma_start(self.wg[:, :, :], io["w_ple_gate"].rearrange("(k p) n -> p k n", p=128)).then_inc(self.plain_in, 16)
            sp.dma_start(self.wp[:, :, :], io["w_ple_proj"].rearrange("(k p) n -> p k n", p=128)).then_inc(self.plain_in, 16)

    def split(self, nc, pool, raw, k):
        pool.wait_ge(self.raw_in[k % 2], 16 * (k // 2 + 1))
        nc.gpsimd.tensor_copy(self.wo.hi[:, k, :], raw[k % 2][:, :]).then_inc(self.hi_ok, 1)
        pool.wait_ge(self.hi_ok, k + 1)
        nc.gpsimd.tensor_tensor(self.wo.lo[:, k, :], raw[k % 2][:, :], self.wo.hi[:, k, :].bitcast(F32), ALU.subtract).then_inc(self.lo_ok, 1)


def branch_phase(nc, io, keep, fw):
    blocks = []
    for br, r in enumerate((1, 4, 16)):
        for c in range(r):
            for b in range(LX // r // 128):
                blocks.append((br, r, c, b))
    NB = len(blocks)
    NG = 4 * NB
    steps = []
    use = {}
    def add(kind, i):
        use[(kind, i)] = len(steps)
        steps.append((kind, i))
    add("q", 0)
    add("k", 0)
    for g in range(NG):
        add("p", g)
        if g % 4 == 0 and g // 4 + 1 < NB:
            add("q", g // 4 + 1)
            add("k", g // 4 + 1)
    first = {}
    for u, (kind, i) in enumerate(steps):
        g = i if kind == "p" else 4 * (i - 1)
        first.setdefault(g, []).append(u)
    with phase(nc, "br") as P:
        band = P.sb("band", [128, 256])
        raw = [P.sb(f"raw{j}", [128, D]) for j in range(2)]
        x = [P.sb(f"x{j}", [128, 1536]) for j in range(3)]
        vp = [P.sb(f"v{j}", [128, 4, 192]) for j in range(4)]
        qT = [P.sb(f"qT{j}", [128, 4, 128]) for j in range(2)]
        kT = [P.sb(f"kT{j}", [128, 4, 128]) for j in range(3)]
        s_sb = [P.sb(f"s{j}", [128, 2, 256]) for j in range(2)]
        pt = [P.sb(f"pt{j}", [128, 4, 128]) for j in range(2)]
        nm = P.sb("nm", [128, 2, 2])
        o = [P.sb(f"o{j}", [128, ORW]) for j in range(2)]
        S = [[P.ps(f"S{h}{j}") for j in range(2)] for h in range(2)]
        T = [P.ps(f"T{j}") for j in range(2)]
        O = [P.ps(f"O{j}") for j in range(2)]
        band_in, s_mm, m_ok, n_ok, e_ok, t_mm, pv_mm, o_ev = [P.sem(s) for s in (
            "band_in", "s_mm", "m_ok", "n_ok", "e_ok", "t_mm", "pv_mm", "o_ev")]
        ev = [P.sem("ev_dve"), P.sem("ev_act")]
        ld = [P.sem(f"ld{j}") for j in range(3)]
        v_ok, v_zero = P.sem("v_ok"), P.sem("v_zero")
        out = [P.sem(f"out{j}") for j in range(2)]

        def rows(name, n):
            br, r, c, b = blocks[n]
            base = io["z2"] if name == "z2" else io["branch"][br]
            return base.rearrange("(n r) c -> r n c", r=r)[c, b * 128:(b + 1) * 128, :]

        def halves(n):
            return (0, 1) if blocks[n][3] else (1,)

        def wait_evac(eng, u):
            eng.wait_ge(ev[u % 2], u // 2 + 1)

        with nc.Block() as block:
            @block.sync
            def _(sp):
                sp.dma_start(band[:, :], io["band"]).then_inc(band_in, 16)
                def load(n):
                    if n >= 3:
                        sp.wait_ge(t_mm, use[("k", n - 3)] + 1)
                        sp.wait_ge(v_ok, n - 2)
                    sp.dma_start(x[n % 3][:, :], rows("z2", n)[:, 0:1536]).then_inc(ld[n % 3], 16)
                load(0)
                load(1)
                for n in range(NB):
                    if n + 2 < NB:
                        load(n + 2)
                    if n % 4 == 2 and n // 4 < KC:
                        fw.load(sp, io, raw, n // 4)
                    sp.wait_ge(o_ev, n + 1)
                    sp.dma_start(rows("branch", n), o[n % 2][:, :]).then_inc(out[n % 2], 16)
                for j in range(2):
                    sp.wait_ge(out[j], 16 * (NB // 2))

            @block.tensor
            def _(pe):
                def transposes(u):
                    kind, i = steps[u]
                    if u >= 2:
                        pe.wait_ge(ev[u % 2], u // 2)
                    if kind == "p":
                        pe.wait_ge(e_ok, i + 1)
                        hs = halves(i // 4)
                        for h in range(2):
                            for w in hs:
                                last = nc.tensor.transpose(T[u % 2][:, (2 * h + w) * 128:(2 * h + w + 1) * 128],
                                                           s_sb[i % 2][:, h, w * 128:(w + 1) * 128], keep["ident"][:, :])
                    else:
                        pe.wait_ge(ld[i % 3], 16 * (i // 3 + 1))
                        o0 = 0 if kind == "q" else 512
                        for c in range(4):
                            last = nc.tensor.transpose(T[u % 2][:, c * 128:(c + 1) * 128],
                                                       x[i % 3][:, o0 + c * 128:o0 + (c + 1) * 128], keep["ident"][:, :])
                    last.then_inc(t_mm, 1)

                def scores(g):
                    n, p = g // 4, g % 4
                    if p == 0:
                        wait_evac(pe, use[("q", n)])
                        wait_evac(pe, use[("k", n)])
                    if g >= 2:
                        pe.wait_ge(m_ok, g - 1)
                    for h in range(2):
                        for w in halves(n):
                            last = nc.tensor.matmul(S[h][g % 2][:, w * 128:(w + 1) * 128], qT[n % 2][64 * h:64 * h + 64, p, :],
                                                    kT[(n - 1 + w) % 3][64 * h:64 * h + 64, p, :], start=True, stop=True)
                    last.then_inc(s_mm, 1)

                def values(g):
                    n, p = g // 4, g % 4
                    wait_evac(pe, use[("p", g)])
                    if p == 0:
                        pe.wait_ge(v_ok, n + 1)
                    if p == 0 and n >= 2:
                        pe.wait_ge(o_ev, n - 1)
                    hs = halves(n)
                    for h in range(2):
                        for w in hs:
                            last = nc.tensor.matmul(O[n % 2][:, p * 128:(p + 1) * 128], pt[g % 2][:, 2 * h + w, :],
                                                    vp[(n - 1 + w) % 4][:, p, 64 * h:64 * h + 128],
                                                    start=(w == hs[0] and h == 0), stop=(w == 1 and h == 1))
                    last.then_inc(pv_mm, 1)

                transposes(0)
                transposes(1)
                scores(0)
                for g in range(NG + 1):
                    if g + 1 < NG:
                        scores(g + 1)
                    if g < NG:
                        for u in first[g]:
                            transposes(u)
                    if g >= 1:
                        values(g - 1)

            @block.gpsimd
            def _(pool):
                for j in range(4):
                    last = nc.gpsimd.memset(vp[j][:, :, 64:128], 0.0)
                last.then_inc(v_zero, 1)
                pool.wait_ge(v_zero, 1)
                for n in range(NB):
                    pool.wait_ge(ld[n % 3], 16 * (n // 3 + 1))
                    if n >= 4:
                        pool.wait_ge(pv_mm, 4 * (n - 2))
                    nc.gpsimd.tensor_copy(vp[n % 4][:, :, :].rearrange("p a (b c) -> p a b c", c=64)[:, :, ::2, :],
                                          x[n % 3][:, 1024:1536].rearrange("p (a b c) -> p a b c", b=2, c=64)).then_inc(v_ok, 1)
                    if n % 4 == 3 and n // 4 < KC:
                        fw.split(nc, pool, raw, n // 4)

            def take(eng, copy, u):
                kind, i = steps[u]
                eng.wait_ge(t_mm, u + 1)
                src = T[u % 2][:, :].rearrange("p (a b) -> p a b", b=128)
                if kind == "p":
                    if i >= 2:
                        eng.wait_ge(pv_mm, i - 1)
                    if len(halves(i // 4)) == 2:
                        copy(pt[i % 2][:, :, :], src).then_inc(ev[u % 2], 1)
                    else:
                        copy(pt[i % 2][:, 1::2, :], src[:, 1::2, :]).then_inc(ev[u % 2], 1)
                else:
                    if i >= 2:
                        eng.wait_ge(s_mm, 4 * (i - 1))
                    copy((qT[i % 2] if kind == "q" else kT[i % 3])[:, :, :], src).then_inc(ev[u % 2], 1)

            @block.vector
            def _(dve):
                def maxima(g):
                    n, p = g // 4, g % 4
                    dve.wait_ge(s_mm, g + 1)
                    if g >= 2:
                        dve.wait_ge(t_mm, use[("p", g - 2)] + 1)
                    if p == 0 and n >= 2:
                        dve.wait_ge(out[n % 2], 16 * (n // 2))
                    a = 128 * halves(n)[0]
                    for h in range(2):
                        last = nc.vector.tensor_tensor_reduce(out=s_sb[g % 2][:, h, a:256], in0=S[h][g % 2][:, a:256], in1=band[:, a:256],
                                                              scale=1.0, scalar=LOWEST, op0=ALU.add, op1=ALU.max,
                                                              accum_out=o[n % 2][:, 512 + 2 * p + h:513 + 2 * p + h])
                    dve.drain().then_inc(m_ok, 1)
                    if g >= 2:
                        dve.wait_ge(e_ok, g - 1)
                    nc.vector.tensor_scalar(nm[:, g % 2, :], o[n % 2][:, 512 + 2 * p:514 + 2 * p], -1.0, None, ALU.mult).then_inc(n_ok, 1)

                take_ = lambda u: take(dve, nc.vector.tensor_copy, u)
                take_(0)
                dve.wait_ge(band_in, 16)
                maxima(0)
                for g in range(NG):
                    if g + 1 < NG:
                        maxima(g + 1)
                    for u in first[g]:
                        if u % 2 == 0:
                            take_(u)

            @block.scalar
            def _(act):
                def exps(g):
                    n, p = g // 4, g % 4
                    act.wait_ge(n_ok, g + 1)
                    if p == 0 and n >= 2:
                        act.wait_ge(out[n % 2], 16 * (n // 2))
                    a = 128 * halves(n)[0]
                    for h in range(2):
                        last = act.activation(s_sb[g % 2][:, h, a:256], s_sb[g % 2][:, h, a:256], ACT.Exp, bias=nm[:, g % 2, h:h + 1],
                                              accum_out=o[n % 2][:, 520 + 2 * p + h:521 + 2 * p + h])
                    last.then_inc(e_ok, 1)
                take_ = lambda u: take(act, lambda d, s: act.activation(d, s, ACT.Copy), u)
                take_(1)
                exps(0)
                for g in range(NG + 1):
                    if g + 1 < NG:
                        exps(g + 1)
                    for u in (first[g] if g < NG else []):
                        if u % 2:
                            take_(u)
                    if g and g % 4 == 0:
                        n = g // 4 - 1
                        act.wait_ge(pv_mm, 4 * (n + 1))
                        act.activation(o[n % 2][:, 0:512], O[n % 2][:, :], ACT.Copy).then_inc(o_ev, 1)


def last_phase(nc, io, keep, fw):
    with phase(nc, "fin") as P:
        wo, wg, wp = fw.wo, fw.wg, fw.wp
        ws = P.sb("ws", [128, 4, 128])
        wsT = P.sb("wsT", [128, 4, 128])
        tril = P.sb("tril", [128, 128])
        bs = P.sb("bs", [128, 4])
        lg, lb = P.sb("lg", [128, 512]), P.sb("lb", [128, 512])
        bg = P.sb("bg", [128, D])
        gp = P.sb("gp", [128, KC])
        ob = [P.sb(f"ob{j}", [128, 3, ORW]) for j in range(2)]
        z = [P.sb(f"z{j}", [128, 4, 512]) for j in range(2)]
        h = [P.sb(f"h{j}", [128, D]) for j in range(4)]
        pl = [P.sb(f"pl{j}", [128, 256]) for j in range(2)]
        plT = [P.sb(f"plT{j}", [128, 2, 128]) for j in range(4)]
        mx = [P.sb(f"mx{j}", [128, D]) for j in range(2)]
        mT = Split(P.sb, "mT", [128, KC, 128])
        hn = P.sb("hn", [128, D])
        hT = P.sb("hT", [128, KC, 128])
        mTf = P.sb("mTf", [128, 4, 128])
        sg = P.sb("sg", [128, D])
        sg2 = P.sb("sg2", [128, D])
        bn = P.sb("bn", [128, 6])
        mv = P.sb("mv", [128, 2, 4])
        sm = P.sb("sm", [128, 8, 3, HB])
        ss = P.sb("ss", [128, 2, 2])
        accO = [P.ps(f"accO{i}") for i in range(2)]
        accG = [P.ps(f"accG{i}") for i in range(2)]
        accP = [P.ps(f"accP{i}") for i in range(2)]
        TD, TE = P.ps("TD"), P.ps("TE")
        names = ("cst_in", "wsT_mm", "wsT_ok", "sd_ok", "sr_ok", "vln_ok", "d_mm", "e_mm", "d_ev", "e_ev", "ed_ok", "ex_ok",
                 "mx_ok", "o_mm", "h2_ok", "h_ss", "hn_ok", "g_mm", "gb_ok", "sg_ok", "out_ok", "pl_mm", "lo_ok")
        m = {n: P.sem(n) for n in names}
        ldz = [P.sem(f"ldz{j}") for j in range(2)]
        ldh = [P.sem(f"ldh{j}") for j in range(4)]
        out = [P.sem(f"out{j}") for j in range(4)]
        NCST = 7
        order, idx = [], {}
        for t in range(-2, NX + 1):
            for kind, u in (("mix", t + 1), ("hn", t), ("pre", t + 2)):
                if 0 <= u < NX:
                    idx[(kind, u)] = len(order)
                    order.append((kind, u))
        ok = lambda t: 0 <= t < NX
        with nc.Block() as block:
            @block.sync
            def _(sp):
                for dst, src in ((ws[:, :, :], io["w_spatial"].rearrange("g t s -> t g s")), (tril[:, :], io["tril"]),
                                 (bs[:, :], io["b_spatial"]), (lg[:, :], bcast_rows(io["ln_v_g"], 512)),
                                 (lb[:, :], bcast_rows(io["ln_v_b"], 512)), (bg[:, :], bcast_rows(io["b_ple_gate"], D)),
                                 (gp[:, :], io["g_ple_T"])):
                    sp.dma_start(dst, src).then_inc(m["cst_in"], 16)

                def load(t):
                    rows = slice(t * 128, (t + 1) * 128)
                    if t >= 2:
                        sp.wait_ge(m["mx_ok"], t - 1)
                        sp.wait_ge(m["e_mm"], idx[("pre", t - 2)] + 1)
                    sp.dma_start(ob[t % 2][:, :, :], io["branch"][:, rows, :].rearrange("b p c -> p b c")).then_inc(ldz[t % 2], 16)
                    sp.dma_start(z[t % 2][:, :, :].rearrange("p a b -> p (a b)"), io["z2"][rows, 1536:WB]).then_inc(ldz[t % 2], 16)
                    sp.dma_start(pl[t % 2][:, :], io["p2"][rows, :]).then_inc(ldz[t % 2], 16)
                    if t >= 4:
                        sp.wait_ge(out[t % 4], 16 * (t // 4))
                    sp.dma_start(h[t % 4][:, :], io["xres"][rows, :]).then_inc(ldh[t % 4], 16)
                for t in range(NX):
                    load(t)

            @block.gpsimd
            def _(pool):
                for t in range(-2, NX + 1):
                    if ok(t + 1):
                        pool.wait_ge(m["e_ev"], idx[("mix", t + 1)] + 1)
                        nc.gpsimd.tensor_tensor(mT.lo[:, 4:8, :], mTf[:, :, :], mT.hi[:, 4:8, :].bitcast(F32), ALU.subtract).then_inc(m["lo_ok"], 1)
                    if not ok(t - 1):
                        continue
                    t = t - 1
                    pool.wait_ge(m["out_ok"], t + 1)
                    pool.dma_start(io["out"][0, t * 128:(t + 1) * 128, :], h[t % 4][:, :]).then_inc(out[t % 4], 16)
                for j in range(4):
                    pool.wait_ge(out[j], 16 * (NX // 4))

            @block.tensor
            def _(pe):
                def banks_free(key):
                    n = idx[key] + 1
                    pe.wait_ge(m["d_ev"], n)
                    if n >= 2:
                        pe.wait_ge(m["e_ev"], n - 1)

                def spread(src, key):
                    banks_free(key)
                    for k in range(KC):
                        last = nc.tensor.transpose((TD if k < 4 else TE)[:, (k % 4) * 128:(k % 4 + 1) * 128],
                                                   src[:, k * 128:(k + 1) * 128], keep["ident"][:, :])
                        if k == 3:
                            last.then_inc(m["d_mm"], 1)
                    last.then_inc(m["e_mm"], 1)

                pe.wait_ge(m["cst_in"], 16 * NCST)
                for g in range(4):
                    last = nc.tensor.transpose(TD[:, g * 128:(g + 1) * 128], ws[:, g, :], keep["ident"][:, :])
                last.then_inc(m["wsT_mm"], 1)
                for t in range(-2, NX + 1):
                    if ok(t):
                        pe.wait_ge(fw.plain_in, 32)
                        pe.wait_ge(m["d_ev"], idx[("mix", t)] + 2)
                        pe.wait_ge(m["lo_ok"], t + 1)
                        if t >= 1:
                            pe.wait_ge(m["h2_ok"], t)
                        for i in range(2):
                            for k in range(KC):
                                last = matmul3(nc, accO[i][:, :], mT[:, k, :], wo[:, k, i * 512:(i + 1) * 512], k == 0, k == KC - 1)
                        last.then_inc(m["o_mm"], 1)
                    if ok(t + 1):
                        pe.wait_ge(m["mx_ok"], t + 2)
                        spread(mx[(t + 1) % 2], ("mix", t + 1))
                    if ok(t - 1):
                        u = t - 1
                        pe.wait_ge(m["d_ev"], idx[("hn", u)] + 2)
                        pe.wait_ge(m["e_ev"], idx[("hn", u)] + 1)
                        if u >= 1:
                            pe.wait_ge(m["out_ok"], u)
                        for i in range(2):
                            for k in range(KC):
                                last = nc.tensor.matmul(accG[i][:, :], hT[:, k, :], wg[:, k, i * 512:(i + 1) * 512],
                                                        start=(k == 0), stop=(k == KC - 1))
                        last.then_inc(m["g_mm"], 1)
                        for i in range(2):
                            for k in range(2):
                                last = nc.tensor.matmul(accP[i][:, :], plT[u % 4][:, k, :], wp[:, k, i * 512:(i + 1) * 512],
                                                        start=(k == 0), stop=(k == 1))
                        last.then_inc(m["pl_mm"], 1)
                    if ok(t):
                        pe.wait_ge(m["hn_ok"], t + 1)
                        spread(hn, ("hn", t))
                    if ok(t + 2):
                        u = t + 2
                        banks_free(("pre", u))
                        pe.wait_ge(m["vln_ok"], u + 1)
                        for g in range(4):
                            last = nc.tensor.matmul(TD[:, g * 128:(g + 1) * 128], wsT[:, g, :], z[u % 2][:, 3, g * 128:(g + 1) * 128],
                                                    start=True, stop=True)
                        last.then_inc(m["d_mm"], 1)
                        for k in range(2):
                            last = nc.tensor.transpose(TE[:, k * 128:(k + 1) * 128], pl[u % 2][:, k * 128:(k + 1) * 128], keep["ident"][:, :])
                        last.then_inc(m["e_mm"], 1)

            @block.vector
            def _(dve):
                vec = nc.vector

                def layernorm(u):
                    v = z[u % 2][:, 3, :]
                    dve.wait_ge(ldz[u % 2], 48 * (u // 2 + 1))
                    vec.bn_stats(bn[:, :], v)
                    dve.drain()
                    vec.bn_aggr(mv[:, u % 2, 0:2], bn[:, :])
                    dve.drain().then_inc(m["sd_ok"], 1)
                    dve.wait_ge(m["sr_ok"], u + 1)
                    vec.reciprocal(mv[:, u % 2, 3:4], mv[:, u % 2, 2:3])
                    dve.drain()
                    vec.tensor_scalar(v, v, mv[:, u % 2, 0:1], mv[:, u % 2, 3:4], ALU.subtract, ALU.mult)
                    dve.drain()
                    vec.tensor_tensor(v, v, lg[:, :], ALU.mult)
                    dve.drain()
                    vec.tensor_tensor(v, v, lb[:, :], ALU.add).then_inc(m["vln_ok"], 1)

                def combine(u):
                    b, mo = ob[u % 2], mx[u % 2]
                    mb, den = b[:, :, 512:520], b[:, :, 520:528]
                    vec.tensor_tensor(sm[:, 0, 0, :], mb[:, 0, :], mb[:, 1, :], ALU.max)
                    dve.drain()
                    vec.tensor_tensor(sm[:, 0, 0, :], sm[:, 0, 0, :], mb[:, 2, :], ALU.max)
                    dve.drain()
                    vec.tensor_tensor(sm[:, 1, :, :], mb, sm[:, 0, 0, None, :].to_broadcast([128, 3, HB]), ALU.subtract).then_inc(m["ed_ok"], 1)
                    dve.wait_ge(m["ex_ok"], u + 1)
                    vec.tensor_tensor(sm[:, 3, :, :], sm[:, 2, :, :], den, ALU.mult)
                    dve.drain()
                    vec.tensor_tensor(sm[:, 4, 0, :], sm[:, 3, 0, :], sm[:, 3, 1, :], ALU.add)
                    dve.drain()
                    vec.tensor_tensor(sm[:, 4, 0, :], sm[:, 4, 0, :], sm[:, 3, 2, :], ALU.add)
                    dve.drain()
                    vec.reciprocal(sm[:, 4, 1, :], sm[:, 4, 0, :])
                    dve.drain()
                    vec.tensor_tensor(sm[:, 5, :, :], sm[:, 2, :, :], sm[:, 4, 1, None, :].to_broadcast([128, 3, HB]), ALU.mult)
                    dve.drain()
                    for br in range(3):
                        ov = b[:, br, 0:512].rearrange("p (h d) -> p h d", d=HD)
                        vec.tensor_tensor(ov, ov, sm[:, 5, br, :, None].to_broadcast([128, HB, HD]), ALU.mult)
                    dve.drain()
                    vec.tensor_tensor(b[:, 0, 0:512], b[:, 0, 0:512], b[:, 1, 0:512], ALU.add)
                    dve.drain()
                    vec.tensor_tensor(b[:, 0, 0:512], b[:, 0, 0:512], b[:, 2, 0:512], ALU.add)
                    dve.drain()
                    if u >= 2:
                        dve.wait_ge(m["e_mm"], idx[("mix", u - 2)] + 1)
                    vec.tensor_tensor(mo[:, 0:512], b[:, 0, 0:512], z[u % 2][:, 0, :], ALU.mult)
                    dve.wait_ge(m["d_mm"], idx[("pre", u)] + 1)
                    for g in range(4):
                        c = slice(g * 128, (g + 1) * 128)
                        last = vec.scalar_tensor_tensor(mo[:, 512 + g * 128:640 + g * 128], TD[:, c], bs[:, g:g + 1], z[u % 2][:, 2, c], ALU.add, ALU.mult)
                    last.then_inc(m["d_ev"], 1)
                    dve.drain()
                    vec.tensor_tensor(mo[:, 512:1024], mo[:, 512:1024], z[u % 2][:, 1, :], ALU.mult).then_inc(m["mx_ok"], 1)
                    dve.drain()

                dve.wait_ge(m["wsT_mm"], 1)
                vec.tensor_tensor(wsT[:, :, :], TD[:, :].rearrange("p (a b) -> p a b", b=128),
                                  tril[:, None, :].to_broadcast([128, 4, 128]), ALU.mult).then_inc(m["d_ev"], 1)
                for t in range(-2, NX + 1):
                    if ok(t):
                        dve.wait_ge(m["o_mm"], t + 1)
                        dve.wait_ge(ldh[t % 4], 16 * (t // 4 + 1))
                        for i in range(2):
                            c = slice(i * 512, (i + 1) * 512)
                            vec.tensor_tensor(h[t % 4][:, c], h[t % 4][:, c], accO[i][:, :], ALU.add)
                        dve.drain().then_inc(m["h2_ok"], 1)
                    if ok(t + 2):
                        layernorm(t + 2)
                    if ok(t):
                        dve.wait_ge(m["h_ss"], t + 1)
                        vec.reciprocal(ss[:, t % 2, 1:2], ss[:, t % 2, 1:2])
                        dve.drain()
                        if t >= 1:
                            dve.wait_ge(m["e_mm"], idx[("hn", t - 1)] + 1)
                        vec.tensor_scalar(hn[:, :], h[t % 4][:, :], ss[:, t % 2, 1:2], None, ALU.mult).then_inc(m["hn_ok"], 1)
                    if ok(t + 1):
                        dve.wait_ge(m["d_mm"], idx[("mix", t + 1)] + 1)
                        if t >= 0:
                            dve.wait_ge(m["o_mm"], t + 1)
                        src = TD[:, :].rearrange("p (a b) -> p a b", b=128)
                        vec.tensor_copy(mT.hi[:, 0:4, :], src)
                        dve.drain()
                        vec.tensor_tensor(mT.lo[:, 0:4, :], src, mT.hi[:, 0:4, :].bitcast(F32), ALU.subtract).then_inc(m["d_ev"], 1)
                    if ok(t - 1):
                        u = t - 1
                        dve.wait_ge(m["g_mm"], u + 1)
                        if u >= 1:
                            dve.drain()
                        for i in range(2):
                            c = slice(i * 512, (i + 1) * 512)
                            vec.tensor_tensor(sg[:, c], accG[i][:, :], bg[:, c], ALU.add)
                        dve.drain().then_inc(m["gb_ok"], 1)
                        dve.wait_ge(m["sg_ok"], u + 1)
                        dve.wait_ge(m["pl_mm"], u + 1)
                        for i in range(2):
                            c = slice(i * 512, (i + 1) * 512)
                            vec.tensor_tensor(sg[:, c], sg[:, c], accP[i][:, :], ALU.mult)
                        dve.drain()
                        vec.tensor_tensor(h[u % 4][:, :], h[u % 4][:, :], sg[:, :], ALU.add).then_inc(m["out_ok"], 1)
                    if ok(t):
                        dve.wait_ge(m["d_mm"], idx[("hn", t)] + 1)
                        for k in range(4):
                            last = vec.tensor_scalar(hT[:, k, :], TD[:, k * 128:(k + 1) * 128], gp[:, k:k + 1], None, ALU.mult)
                        last.then_inc(m["d_ev"], 1)
                    if ok(t + 2):
                        combine(t + 2)

            @block.scalar
            def _(act):
                for t in range(-2, NX + 1):
                    if ok(t):
                        act.wait_ge(m["h2_ok"], t + 1)
                        act.activation(sg2[:, :], h[t % 4][:, :], ACT.Square, accum_out=ss[:, t % 2, 0:1])
                        act.drain()
                        act.activation(ss[:, t % 2, 1:2], ss[:, t % 2, 0:1], ACT.Sqrt, scale=1.0 / D, bias=keep["eps"][:, 0:1]).then_inc(m["h_ss"], 1)
                    if ok(t + 2):
                        u = t + 2
                        act.wait_ge(m["sd_ok"], u + 1)
                        act.activation(mv[:, u % 2, 2:3], mv[:, u % 2, 1:2], ACT.Sqrt, bias=keep["eps"][:, 0:1]).then_inc(m["sr_ok"], 1)
                    if ok(t + 1):
                        act.wait_ge(m["e_mm"], idx[("mix", t + 1)] + 1)
                        if t >= 0:
                            act.wait_ge(m["o_mm"], t + 1)
                            act.wait_ge(m["lo_ok"], t + 1)
                        act.activation(mT.hi[:, 4:8, :], TE[:, :].rearrange("p (a b) -> p a b", b=128), ACT.Copy)
                        act.activation(mTf[:, :, :], TE[:, :].rearrange("p (a b) -> p a b", b=128), ACT.Copy).then_inc(m["e_ev"], 1)
                    if ok(t - 1):
                        act.wait_ge(m["gb_ok"], t)
                        act.activation(sg[:, :], sg[:, :], ACT.Sigmoid).then_inc(m["sg_ok"], 1)
                    if ok(t):
                        act.wait_ge(m["e_mm"], idx[("hn", t)] + 1)
                        for k in range(4, KC):
                            last = act.activation(hT[:, k, :], TE[:, (k - 4) * 128:(k - 3) * 128], ACT.Copy, scale=gp[:, k:k + 1])
                        last.then_inc(m["e_ev"], 1)
                    if ok(t + 2):
                        u = t + 2
                        act.wait_ge(m["ed_ok"], u + 1)
                        act.activation(sm[:, 2, :, :], sm[:, 1, :, :], ACT.Exp).then_inc(m["ex_ok"], 1)
                        act.wait_ge(m["e_mm"], idx[("pre", u)] + 1)
                        if u >= 4:
                            act.wait_ge(m["pl_mm"], u - 3)
                        act.activation(plT[u % 4][:, :, :], TE[:, 0:256].rearrange("p (a b) -> p a b", b=128), ACT.Copy).then_inc(m["e_ev"], 1)


def second_block(nc, io, keep):
    with nc.cleanup_on_exit():
        hT = Split(nc.alloc_sbuf_tensor, "hT2", [128, KC, LX])
        gin = nc.alloc_sbuf_tensor("g_in", [128, KC], F32)
        with phase(nc, "gin") as P:
            got = P.sem("got")
            with nc.Block() as block:
                @block.sync
                def _(sp):
                    sp.dma_start(gin[:, :], io["g_in_T"]).then_inc(got, 16)
                    sp.wait_ge(got, 16)
        with phase(nc, "nt2") as P:
            norm_transpose(P, nc, io["xres"][0:LX, :], hT, keep["ident"], keep["eps"], [4] * 4,
                           lambda k, g: gin[:, k:k + 1], lambda k, g: 0.0, pre=(io["norm_f"], True))
        with phase(nc, "tz") as P:
            order = [2, 0, 1, 3, 4, 5, 6]
            project_tm(P, nc, hT, lambda c: io["w_in2"][order[c], :, :, :],
                       lambda c, t: io["z2"][t * 128:(t + 1) * 128, order[c] * 512:(order[c] + 1) * 512],
                       [512] * 7, [ACT.Copy] + [None] * 2 + [ACT.Silu] * 2 + [ACT.Gelu_apprx_tanh] * 2, NX,
                       HeadNormRope(P, nc, io, keep))
    with phase(nc, "fw") as P:
        fw = FinalWeights(P)
        branch_phase(nc, io, keep, fw)
        last_phase(nc, io, keep, fw)

def first_layer(nc, l, io, keep):
    ada_phase(nc, l, io, keep)
    with nc.cleanup_on_exit():
        hT = Split(nc.alloc_sbuf_tensor, "hT", [128, KC, LT])
        with phase(nc, "nt") as P:
            norm_transpose(P, nc, io["xres"], hT, keep["ident"], keep["eps"], [4, 4, 4, 4, 2],
                           lambda k, g: keep["scale"][:, k, g // 4:g // 4 + 1],
                           lambda k, g: keep["shift"][:, k, g // 4:g // 4 + 1], copied=keep["copied"])
        with phase(nc, "cm") as P:
            project_cm(P, nc, hT, lambda c: io["w_cm"][bass.ds(l * CM + c, 1), :, :, :].rearrange("a p k m -> p (a k) m"),
                       lambda c: io["zcm"][bass.ds(c, 1), :, :].rearrange("a p t -> p (a t)"), CM)
        with phase(nc, "tm") as P:
            project_tm(P, nc, hT,
                       lambda c: io["w_gate" if c < 2 else "w_val"][bass.ds(l * 2 + c % 2, 1), :, :, :].rearrange("a p k m -> p (a k) m"),
                       lambda c, t: io["ztm"][t * 128:(t + 1) * 128, (c * 512 if c < 2 else 256 + c * 384):(c * 512 + 512 if c < 2 else 640 + c * 384)],
                       [512, 512, 384, 384], [ACT.Silu] * 2 + [ACT.Copy] * 2, NT)
    with phase(nc, "nain") as P:
        na = Neighbourhood(P)
        fourier_phase(nc, l, io, keep, na)
        neighbourhood_phase(nc, l, io, keep, na)
    gla_phase(nc, l, io, keep)
    out_phase(nc, l, io, keep)





def program(nc, io):
    keep = {
        "ident": nc.alloc_sbuf_tensor("ident", [128, 128], F32),
        "eps": nc.alloc_sbuf_tensor("eps", [128, 1], F32),
        "shift": nc.alloc_sbuf_tensor("shift", [128, KC, 2], F32),
        "scale": nc.alloc_sbuf_tensor("scale", [128, KC, 2], F32),
        "copied": nc.alloc_semaphore("copied"),
    }
    with phase(nc, "start") as P:
        ident_in, eps_ok = P.sem("ident_in"), P.sem("eps_ok")
        with nc.Block() as block:
            @block.sync
            def _(sp):
                sp.dma_start(keep["ident"][:, :], io["ident"]).then_inc(ident_in, 16)
                sp.dma_start(io["xres"][0:LX, :], io["x"]).then_inc(keep["copied"], 16)
                sp.dma_start(io["xres"][LX:LT, :], io["ctx"]).then_inc(keep["copied"], 16)
                sp.wait_ge(ident_in, 16)

            @block.vector
            def _(dve):
                nc.vector.memset(keep["eps"][:, :], EPS).then_inc(eps_ok, 1)
                dve.wait_ge(eps_ok, 1)
    with nc.Fori(0, DEPTH) as l:
        first_layer(nc, l, io, keep)
    second_block(nc, io, keep)





def laid_out(a):
    f = lambda n: np.ascontiguousarray(a[n])
    sizes = (256, 256, 384, 384, 384, 384, 192, 192, 384, 384, 16, 16)
    at = np.cumsum((0,) + sizes)
    w = f("w_in")
    fx, fg, nq, nk, nv, ng, gq, gk, gv, gg, zf, zb = (w[:, :, at[i]:at[i + 1]] for i in range(12))

    def heads_padded(t, n=GH):
        out = np.zeros(t.shape[:-1] + (n, 64), t.dtype)
        out[..., :GDK] = t.reshape(t.shape[:-1] + (n, GDK))
        return out.reshape(t.shape[:-1] + (n * 64,))

    gqz = heads_padded(gq)
    gqz[..., GDK:64], gqz[..., 64 + GDK:128] = zf, zb
    cm = np.concatenate([fx, nq, nk, gqz, heads_padded(gk)], -1)

    def chunks(t, m):
        L = t.shape[0]
        return np.ascontiguousarray(t.reshape(L, KC, 128, -1, m).transpose(0, 3, 2, 1, 4).reshape(-1, 128, KC, m))

    wa = np.zeros((DEPTH, 64, 256), np.float32)
    wa[:, 0:RANK] = heads_padded(f("w_alpha_fwd"))
    wa[:, 32:32 + RANK] = heads_padded(f("w_alpha_bwd"))
    ba = np.stack([heads_padded(f("b_alpha_fwd")), heads_padded(f("b_alpha_bwd"))], 1)
    ba = ba.reshape(DEPTH, 4, 128).transpose(0, 2, 1)
    w2 = f("w_in_2")[0]
    q2, k2, v2, gb2, u2, va2, ga2 = (w2[:, i * 512:(i + 1) * 512] for i in range(7))
    out = {
        "x": f("x")[0], "ctx": f("ctx")[0],
        "cT": np.stack([a["c"][0], a["c_ctx"]], -1).reshape(KC, 128, 2).transpose(1, 0, 2),
        "w_ada": f("w_ada"), "b_ada": f("b_ada"),
        "norm_wT": f("norm_w").reshape(DEPTH, KC, 128).transpose(0, 2, 1),
        "w_cm": chunks(cm, 128), "w_gate": chunks(np.concatenate([fg, ng, gg], -1), 512),
        "w_val": chunks(np.concatenate([nv, gv], -1), 384),
        "w_four": f("w_four").reshape(DEPTH, 2, 128, 256).transpose(0, 2, 1, 3),
        "rpb": f("rpb"), "w_alpha": wa, "b_alpha": ba, "gla_norm_w": f("gla_norm_w"),
        "w_out": f("w_out"), "norm_f": f("norm_f"),
        "p2": f("p_2")[0, 0], "positions": f("positions_2")[0].astype(np.int32).reshape(NX, 128).T,
        "g_in_T": f("g_in_2")[0].reshape(KC, 128).T,
        "w_in2": chunks(np.concatenate([q2, k2, v2, gb2, ga2, u2, va2], -1)[None], 512),
        "q_norm": f("q_norm_2")[0], "k_norm": f("k_norm_2")[0], "w_spatial": f("w_spatial_2")[0],
        "b_spatial": f("b_spatial_2")[0].T, "ln_v_g": f("ln_v_g_2")[0], "ln_v_b": f("ln_v_b_2")[0],
        "w_out2": f("w_out_2")[0], "g_ple_T": f("g_ple_2")[0].reshape(KC, 128).T,
        "w_ple_gate": f("w_ple_gate_2")[0], "b_ple_gate": f("b_ple_gate_2")[0], "w_ple_proj": f("w_ple_proj_2")[0],
    }
    out.update(shape_tables())
    return {n: np.ascontiguousarray(v) for n, v in out.items()}


def shape_tables():
    f8, f4 = np.float64, np.float32
    t = {"ident": np.eye(128, dtype=f4)}
    ang = 2 * np.pi * np.outer(np.arange(64), np.arange(64)) / 64
    bd = lambda m: np.kron(np.eye(4), m).astype(f4)
    ch = np.stack([bd(np.cos(ang) / 8), bd(np.sin(ang) / 8)])
    t["dft_ch"] = ch.reshape(2, 2, 128, 256).transpose(2, 0, 1, 3)
    tt = np.arange(LX).reshape(N1, N2)
    a1 = 2 * np.pi * tt[:, :, None] * np.arange(N1)[None, None, :] / LX
    s = LX ** -0.5
    t["dft_1"] = np.stack([np.cos(a1) * s, np.sin(a1) * s, -np.sin(a1) * s], 2).astype(f4)
    a2 = 2 * np.pi * np.outer(np.arange(N2), np.arange(N2)) / N2
    e = np.eye(8)
    k2 = lambda m: np.einsum("tk,ab->atkb", m, e).reshape(128, 128)
    t["dft_2"] = np.stack([k2(np.cos(a2)), k2(-np.sin(a2))], 1).astype(f4)
    a3 = 2 * np.pi * np.outer(np.arange(LC), np.arange(LC)) / LC
    d3 = np.stack([np.cos(a3), -np.sin(a3)]) * LC ** -0.5
    t["dft_ctx"] = d3.reshape(2, 2, 128, LC).transpose(2, 0, 1, 3).astype(f4)
    nf = GDK // 4
    inv = (np.float32(10000.0) ** (-np.arange(nf, dtype=f4) / nf)).astype(f4)
    pos = np.arange(LX)
    rows, cols = (pos // GRID).astype(f4), (pos % GRID).astype(f4)
    cs, sn, perm = np.zeros((128, LX)), np.zeros((128, LX)), np.zeros((128, 128))
    for h in range(2):
        for half, p in ((0, rows), (1, cols)):
            a = (p[None, :] * inv[:, None]).astype(f4).astype(f8)
            b = 64 * h + 24 * half
            for o in range(2):
                cs[b + nf * o:b + nf * o + nf], sn[b + nf * o:b + nf * o + nf] = np.cos(a), np.sin(a)
            for n in range(nf):
                perm[b + nf + n, b + n] = -1.0
                perm[b + n, b + nf + n] = 1.0
    t["rope_cs"] = np.stack([cs, sn], 1).astype(f4)
    t["rope_perm"] = perm.astype(f4)
    t["chunk_start"] = np.tile((np.arange(LT) % CH != 0).astype(f4), (128, 1))
    s_, t_ = np.arange(128)[:, None], np.arange(128)[None, :]
    same = (s_ // CH) == (t_ // CH)
    t["gla_mask"] = np.stack([same & (s_ <= t_), same & (s_ >= t_)], 1).astype(np.int32)
    cq = np.arange(GRID)
    st = np.clip(cq - KW // 2, 0, GRID - KW)
    inside = (cq[None, :] >= st[:, None]) & (cq[None, :] < st[:, None] + KW)
    t["col_mask"] = np.tile(np.where(inside, 0.0, NEGBIG).astype(f4), (2, 1))
    dist = (np.arange(128)[:, None] + 128) - np.arange(256)[None, :]
    t["band"] = np.where((dist >= 0) & (dist <= 128), 0.0, NEGBIG).astype(f4)
    t["inv_freq"] = np.exp(-math.log(10000.0) * np.arange(32, dtype=f4) / 32).astype(f4)
    t["tril"] = np.tril(np.ones((128, 128), f4)).T.copy()
    return t


def build(nc, arrays, debug=()):
    io = {n: nc.dram_tensor(f"in_{n}", v.shape, mybir.dt.from_np(v.dtype), kind="ExternalInput").ap()
          for n, v in arrays.items()}
    scratch = {"xres": [LT, D], "gates": [2, D], "zcm": [CM, 128, LT], "ztm": [LT, TM], "mix": [LT, D],
               "four_y": [N1 * N2, 512], "rpb_pad": [NA_H * 15, 64, 128], "z2": [LX, WB], "branch": [3, LX, ORW]}
    for n, s in scratch.items():
        io[n] = nc.dram_tensor(f"scr_{n}", s, F32, kind="ExternalOutput" if n in debug else "Internal").ap()
    io["out"] = nc.dram_tensor("out_0", [1, LX, D], F32, kind="ExternalOutput").ap()
    program(nc, io)


def kernel(**inputs):
    from concourse.bass_utils import run_bass_kernel_spmd
    import concourse.bacc as bacc
    arrays = laid_out(inputs)
    nc = bacc.Bacc("TRN2", target_bir_lowering=False, num_devices=1)
    build(nc, arrays)
    r = run_bass_kernel_spmd(nc, [{f"in_{n}": v for n, v in arrays.items()}], core_ids=[0])
    return r.results[0]["out_0"]
```
